# Optimizing a Trainium2 kernel written in Bass

```python
import math
import jax, jax.numpy as jnp
from jax import lax
import numpy as np

D_MODEL = 1024
BATCH = 1
SEQ = 1024
DEPTH = 2

GRID_W = 64
CTX_LEN = 256
ROPE_THETA = 10000.0
Q_BLOCK = 128
EPS = 1e-6
HALF_WIDTH = D_MODEL // 2

A_HEAD_DIM = 64
A_HEADS = HALF_WIDTH // A_HEAD_DIM
A_KV_HEADS = 2
A_WIDTH = A_HEADS * A_HEAD_DIM
A_KV_WIDTH = A_KV_HEADS * A_HEAD_DIM
B_HEAD_DIM = 128
B_HEADS = HALF_WIDTH // B_HEAD_DIM
B_WIDTH = B_HEADS * B_HEAD_DIM
B_CONV = 3
B_CHUNK = 128
IN_EVEN = A_WIDTH + 2 * A_KV_WIDTH + 4 * B_WIDTH + 4 * B_HEADS
MIX_EVEN = A_WIDTH + B_WIDTH
C_HEAD_DIM = 64
C_V_DIM = 2 * C_HEAD_DIM
C_HEADS = HALF_WIDTH // C_V_DIM
C_WIDTH = C_HEADS * C_V_DIM
D_HEADS = 4
D_Q_LORA = 256
D_KV_LORA = 128
D_NOPE = 64
D_ROPE = 32
D_V_DIM = HALF_WIDTH // D_HEADS
D_WIDTH = D_HEADS * D_V_DIM
IN_ODD = 3 * C_WIDTH + D_Q_LORA + D_KV_LORA + D_ROPE
MIX_ODD = C_WIDTH + D_WIDTH
N_EXPERTS = 32
N_GROUPS = 4
TOP_K = 2
D_EXPERT = 512
MOE_BLOCK = 128

kernel_name = "hybrid_gqa_mlstm_diffattn_mla_moe_prefix_dit"

def rms_norm(x, g):
    xf = x.astype(jnp.float32)
    y = xf * lax.rsqrt(jnp.mean(xf * xf, axis=-1, keepdims=True) + EPS)
    return (y * g.astype(jnp.float32)).astype(x.dtype)

def modulate(x, g, shift, scale):
    return rms_norm(x, g) * (1.0 + scale) + shift

def split_cols(z, sizes):
    bounds = [int(b) for b in np.cumsum(sizes)[:-1]]
    return jnp.split(z, bounds, axis=-1)

def axial_rope_tables(n_tokens, rot_dim):
    rows = n_tokens // GRID_W
    row = jnp.repeat(jnp.arange(rows), GRID_W)
    col = jnp.tile(jnp.arange(GRID_W), rows)
    n_freq = rot_dim // 4
    inv = ROPE_THETA ** (-jnp.arange(n_freq, dtype=jnp.float32) / n_freq)
    ang = jnp.concatenate([row[:, None] * inv, col[:, None] * inv], axis=-1)
    return jnp.cos(ang), jnp.sin(ang)

def apply_rope(x, cos, sin):
    xp = x.reshape(*x.shape[:-1], -1, 2)
    x0, x1 = xp[..., 0], xp[..., 1]
    c = cos[:, None, :].astype(x.dtype)
    s = sin[:, None, :].astype(x.dtype)
    return jnp.stack([x0 * c - x1 * s, x0 * s + x1 * c], axis=-1).reshape(x.shape)

def q_layout(q, n_kv):
    b, n, h, d = q.shape
    return q.reshape(b, n, n_kv, h // n_kv, d).transpose(0, 2, 3, 1, 4)

def kv_layout(t):
    return t.transpose(0, 2, 1, 3)

def merge_heads(o):
    b, hk, g, n, d = o.shape
    return o.transpose(0, 3, 1, 2, 4).reshape(b, n, hk * g * d)

def blocked_attention(q, k, v, scale):
    b, hk, g, sq, d = q.shape
    nb = sq // Q_BLOCK
    qb = jnp.moveaxis(q.reshape(b, hk, g, nb, Q_BLOCK, d), 3, 0)

    def one(qi):
        s = jnp.einsum('bhgqd,bhkd->bhgqk', qi, k).astype(jnp.float32) * scale
        p = jax.nn.softmax(s, axis=-1)
        return jnp.einsum('bhgqk,bhkd->bhgqd', p.astype(v.dtype), v)

    out = lax.map(one, qb)
    return jnp.moveaxis(out, 0, 3).reshape(b, hk, g, sq, v.shape[-1])

def blocked_diff_attention(q1, q2, k1, k2, v, lam, scale):
    b, h, sq, d = q1.shape
    nb = sq // Q_BLOCK
    q1b = jnp.moveaxis(q1.reshape(b, h, nb, Q_BLOCK, d), 2, 0)
    q2b = jnp.moveaxis(q2.reshape(b, h, nb, Q_BLOCK, d), 2, 0)

    def one(qs):
        qa, qb = qs
        p1 = jax.nn.softmax(jnp.einsum('bhqd,bhkd->bhqk', qa, k1).astype(jnp.float32) * scale, axis=-1)
        p2 = jax.nn.softmax(jnp.einsum('bhqd,bhkd->bhqk', qb, k2).astype(jnp.float32) * scale, axis=-1)
        return jnp.einsum('bhqk,bhkd->bhqd', (p1 - lam * p2).astype(v.dtype), v)

    out = lax.map(one, (q1b, q2b))
    return jnp.moveaxis(out, 0, 2).reshape(b, h, sq, v.shape[-1])

def centred_conv(x, w, bias):
    n = x.shape[1]
    pad = B_CONV // 2
    xp = jnp.pad(x, ((0, 0), (pad, pad), (0, 0)))
    return sum(xp[:, j:j + n] * w[j] for j in range(B_CONV)) + bias

def mlstm_chunkwise(q, k, v, i_pre, log_f, state):
    b, h, L, d = q.shape
    nc = L // B_CHUNK

    def chunks(t):
        return jnp.moveaxis(t.reshape(b, h, nc, B_CHUNK, *t.shape[3:]), 2, 0)

    tril = jnp.tril(jnp.ones((B_CHUNK, B_CHUNK), dtype=bool))

    def step(carry, inp):
        C, n, m = carry
        qc, kc, vc, ic, fc = inp
        bcum = jnp.cumsum(fc, axis=-1)
        log_w = jnp.where(tril, bcum[..., :, None] - bcum[..., None, :] + ic[..., None, :], -jnp.inf)
        log_inter = bcum + m[..., None]
        m_row = jnp.maximum(log_inter, jnp.max(log_w, axis=-1))
        w_intra = jnp.exp(log_w - m_row[..., None])
        a_inter = jnp.exp(log_inter - m_row)
        s = jnp.einsum('bhjd,bhsd->bhjs', qc, kc) * w_intra
        num = a_inter[..., None] * jnp.einsum('bhjd,bhde->bhje', qc, C) + jnp.einsum('bhjs,bhse->bhje', s, vc)
        den = a_inter * jnp.einsum('bhjd,bhd->bhj', qc, n) + jnp.sum(s, axis=-1)
        hc = num / jnp.maximum(jnp.abs(den), jnp.exp(-m_row))[..., None]
        b_last = bcum[..., -1]
        log_g = b_last[..., None] - bcum + ic
        m_new = jnp.maximum(b_last + m, jnp.max(log_g, axis=-1))
        g = jnp.exp(log_g - m_new[..., None])
        decay = jnp.exp(b_last + m - m_new)
        C_new = decay[..., None, None] * C + jnp.einsum('bhsd,bhse->bhde', kc * g[..., None], vc)
        n_new = decay[..., None] * n + jnp.einsum('bhs,bhsd->bhd', g, kc)
        return (C_new, n_new, m_new), hc

    state, hs = lax.scan(step, state, (chunks(q), chunks(k), chunks(v), chunks(i_pre), chunks(log_f)))
    return jnp.moveaxis(hs, 0, 2).reshape(b, h, L, d), state

def mlstm_bidirectional(ctx_in, lat_in):
    q_c, k_c, v_c, if_c, ff_c, ib_c, fb_c = ctx_in
    q_l, k_l, v_l, if_l, ff_l, ib_l, fb_l = lat_in
    bsz, nh, _, dh = q_c.shape
    zero = (jnp.zeros((bsz, nh, dh, dh), jnp.float32), jnp.zeros((bsz, nh, dh), jnp.float32),
            jnp.zeros((bsz, nh), jnp.float32))
    flip = lambda t: jnp.flip(t, axis=2)
    hf_c, st_f = mlstm_chunkwise(q_c, k_c, v_c, if_c, ff_c, zero)
    hf_l, _ = mlstm_chunkwise(q_l, k_l, v_l, if_l, ff_l, st_f)
    hb_c, st_b = mlstm_chunkwise(flip(q_c), flip(k_c), flip(v_c), flip(ib_c), flip(fb_c), zero)
    hb_l, _ = mlstm_chunkwise(flip(q_l), flip(k_l), flip(v_l), flip(ib_l), flip(fb_l), st_b)
    return hf_c + flip(hb_c), hf_l + flip(hb_l)

def even_mixer(h_lat, h_ctx, need_ctx, w_in, w_out, g_q, g_k, conv_w, conv_b, b_gates, g_h, rope):
    sizes = (A_WIDTH, A_KV_WIDTH, A_KV_WIDTH, 2 * B_WIDTH, B_WIDTH, B_WIDTH, 4 * B_HEADS)

    def project(h):
        bsz, n = h.shape[:2]
        qa, ka, va, qk_b, vb, ob, gates = split_cols(h @ w_in, sizes)
        qk_b = jax.nn.silu(centred_conv(qk_b, conv_w, conv_b))
        qb, kb = jnp.split(qk_b, 2, axis=-1)
        heads = lambda t: t.reshape(bsz, n, B_HEADS, B_HEAD_DIM).transpose(0, 2, 1, 3).astype(jnp.float32)
        gates = (gates + b_gates).astype(jnp.float32).reshape(bsz, n, 4, B_HEADS).transpose(2, 0, 3, 1)
        i_f, f_f, i_b, f_b = gates
        m_in = (heads(qb), heads(kb) * (B_HEAD_DIM ** -0.5), heads(vb),
                i_f, jax.nn.log_sigmoid(f_f), i_b, jax.nn.log_sigmoid(f_b))
        ka = rms_norm(ka.reshape(bsz, n, A_KV_HEADS, A_HEAD_DIM), g_k)
        va = va.reshape(bsz, n, A_KV_HEADS, A_HEAD_DIM)
        return qa, ka, va, m_in, ob

    def gqa_q(qa):
        bsz, n = qa.shape[:2]
        return rms_norm(qa.reshape(bsz, n, A_HEADS, A_HEAD_DIM), g_q)

    def finish_b(hb, ob):
        bsz, _, n, _ = hb.shape
        hn = rms_norm(hb.transpose(0, 2, 1, 3), g_h.reshape(B_HEADS, B_HEAD_DIM))
        return hn.reshape(bsz, n, B_WIDTH).astype(ob.dtype) * jax.nn.sigmoid(ob)

    scale = A_HEAD_DIM ** -0.5
    cos, sin = rope
    qa_l, ka_l, va_l, m_l, ob_l = project(h_lat)
    qa_c, ka_c, va_c, m_c, ob_c = project(h_ctx)
    q_l = apply_rope(gqa_q(qa_l), cos, sin)
    k_l = apply_rope(ka_l, cos, sin)
    k_all = jnp.concatenate([kv_layout(ka_c), kv_layout(k_l)], axis=2)
    v_all = jnp.concatenate([kv_layout(va_c), kv_layout(va_l)], axis=2)
    oa_l = merge_heads(blocked_attention(q_layout(q_l, A_KV_HEADS), k_all, v_all, scale))
    hb_c, hb_l = mlstm_bidirectional(m_c, m_l)
    out_l = jnp.concatenate([oa_l, finish_b(hb_l, ob_l)], axis=-1) @ w_out
    out_c = None
    if need_ctx:
        oa_c = merge_heads(blocked_attention(q_layout(gqa_q(qa_c), A_KV_HEADS),
                                             kv_layout(ka_c), kv_layout(va_c), scale))
        out_c = jnp.concatenate([oa_c, finish_b(hb_c, ob_c)], axis=-1) @ w_out
    return out_l, out_c

def odd_mixer(h_lat, h_ctx, need_ctx, lam_init, w_in, w_out, g_qc, g_kc, lam_p, g_sub,
              g_cq, w_uq, g_ckv, w_ukv, g_qd, g_kd, rope_c, rope_d):
    sizes = (C_WIDTH, C_WIDTH, C_WIDTH, D_Q_LORA, D_KV_LORA, D_ROPE)
    c_scale = C_HEAD_DIM ** -0.5
    d_scale = (D_NOPE + D_ROPE) ** -0.5

    def keys_values(zp):
        _, kc, vc, _, ckv, kr = zp
        bsz, n = kc.shape[:2]
        kc = rms_norm(kc.reshape(bsz, n, 2 * C_HEADS, C_HEAD_DIM), g_kc)
        vc = vc.reshape(bsz, n, C_HEADS, C_V_DIM)
        kv = (rms_norm(ckv, g_ckv) @ w_ukv).reshape(bsz, n, D_HEADS, D_NOPE + D_V_DIM)
        k_rope = jnp.broadcast_to(kr[:, :, None, :], (bsz, n, D_HEADS, D_ROPE))
        kd = rms_norm(jnp.concatenate([kv[..., :D_NOPE], k_rope], axis=-1), g_kd)
        return kc, vc, kd, kv[..., D_NOPE:]

    def queries(zp):
        qc, _, _, cq, _, _ = zp
        bsz, n = qc.shape[:2]
        qc = rms_norm(qc.reshape(bsz, n, 2 * C_HEADS, C_HEAD_DIM), g_qc)
        qd = rms_norm((rms_norm(cq, g_cq) @ w_uq).reshape(bsz, n, D_HEADS, D_NOPE + D_ROPE), g_qd)
        return qc, qd

    def diff_heads(t):
        bsz, n, _, d = t.shape
        t = t.reshape(bsz, n, C_HEADS, 2, d).transpose(0, 2, 3, 1, 4)
        return t[:, :, 0], t[:, :, 1]

    lq1, lk1, lq2, lk2 = lam_p.astype(jnp.float32)
    lam = jnp.exp(jnp.sum(lq1 * lk1)) - jnp.exp(jnp.sum(lq2 * lk2)) + lam_init

    def diff_attend(qc, k1, k2, v):
        q1, q2 = diff_heads(qc)
        o = blocked_diff_attention(q1, q2, k1, k2, v, lam, c_scale).transpose(0, 2, 1, 3)
        bsz, n = o.shape[:2]
        return (rms_norm(o, g_sub) * (1.0 - lam_init)).reshape(bsz, n, C_WIDTH)

    def rope_tail(t):
        return jnp.concatenate([t[..., :D_NOPE], apply_rope(t[..., D_NOPE:], *rope_d)], axis=-1)

    z_l = split_cols(h_lat @ w_in, sizes)
    z_c = split_cols(h_ctx @ w_in, sizes)
    kc_c, vc_c, kd_c, vd_c = keys_values(z_c)
    kc_l, vc_l, kd_l, vd_l = keys_values(z_l)
    qc_l, qd_l = queries(z_l)
    qc_l = apply_rope(qc_l, *rope_c)
    kc_l = apply_rope(kc_l, *rope_c)
    qd_l = rope_tail(qd_l)
    kd_l = rope_tail(kd_l)
    k1_c, k2_c = diff_heads(kc_c)
    k1_l, k2_l = diff_heads(kc_l)
    k1_all = jnp.concatenate([k1_c, k1_l], axis=2)
    k2_all = jnp.concatenate([k2_c, k2_l], axis=2)
    vc_all = jnp.concatenate([kv_layout(vc_c), kv_layout(vc_l)], axis=2)
    kd_all = jnp.concatenate([kv_layout(kd_c), kv_layout(kd_l)], axis=2)
    vd_all = jnp.concatenate([kv_layout(vd_c), kv_layout(vd_l)], axis=2)
    oc_l = diff_attend(qc_l, k1_all, k2_all, vc_all)
    od_l = merge_heads(blocked_attention(q_layout(qd_l, D_HEADS), kd_all, vd_all, d_scale))
    out_l = jnp.concatenate([oc_l, od_l], axis=-1) @ w_out
    out_c = None
    if need_ctx:
        qc_c, qd_c = queries(z_c)
        oc_c = diff_attend(qc_c, k1_c, k2_c, kv_layout(vc_c))
        od_c = merge_heads(blocked_attention(q_layout(qd_c, D_HEADS), kv_layout(kd_c), kv_layout(vd_c), d_scale))
        out_c = jnp.concatenate([oc_c, od_c], axis=-1) @ w_out
    return out_l, out_c

def moe(tokens, w_router, b_router, w1, w3, w2):
    T, d = tokens.shape
    per = N_EXPERTS // N_GROUPS
    scores = jax.nn.sigmoid((tokens @ w_router).astype(jnp.float32))
    sel = scores + b_router.astype(jnp.float32)
    grp = lax.top_k(sel.reshape(T, N_GROUPS, per), 2)[0].sum(-1)
    g_idx = jnp.argmax(grp, axis=-1)
    in_group = (jnp.arange(N_EXPERTS) // per)[None, :] == g_idx[:, None]
    _, e_idx = lax.top_k(jnp.where(in_group, sel, -jnp.inf), TOP_K)
    gate = jnp.take_along_axis(scores, e_idx, axis=-1)
    gate = gate / jnp.sum(gate, axis=-1, keepdims=True)
    n_assign = T * TOP_K
    e_flat = e_idx.reshape(-1)
    tok_flat = jnp.repeat(jnp.arange(T, dtype=jnp.int32), TOP_K)
    order = jnp.argsort(e_flat)
    se, st = e_flat[order], tok_flat[order]
    counts = jnp.zeros((N_EXPERTS,), jnp.int32).at[e_flat].add(1)
    start = jnp.cumsum(counts) - counts
    padded = (counts + MOE_BLOCK - 1) // MOE_BLOCK * MOE_BLOCK
    pend = jnp.cumsum(padded)
    pstart = pend - padded
    dest = pstart[se] + jnp.arange(n_assign, dtype=jnp.int32) - start[se]
    n_rows = -(-n_assign // MOE_BLOCK) * MOE_BLOCK + N_EXPERTS * MOE_BLOCK
    nb = n_rows // MOE_BLOCK
    row_tok = jnp.full((n_rows,), T, jnp.int32).at[dest].set(st)
    xin = jnp.concatenate([tokens, jnp.zeros((1, d), tokens.dtype)], axis=0)[row_tok]
    blk_e = jnp.minimum(jnp.searchsorted(pend, jnp.arange(nb, dtype=jnp.int32) * MOE_BLOCK, side='right'),
                        N_EXPERTS - 1)

    def expert_block(args):
        xb, e = args
        return (jax.nn.silu(xb @ w1[e]) * (xb @ w3[e])) @ w2[e]

    y = lax.map(expert_block, (xin.reshape(nb, MOE_BLOCK, d), blk_e)).reshape(n_rows, d)
    dest_assign = jnp.zeros((n_assign,), jnp.int32).at[order].set(dest)
    return jnp.einsum('tk,tkd->td', gate.astype(tokens.dtype), y[dest_assign].reshape(T, TOP_K, d))

def setup_inputs(seed: int = 0) -> dict:
    key = jax.random.key(seed)
    ks = iter(jax.random.split(key, 40))
    nrm = lambda shape, s: jax.random.normal(next(ks), shape, jnp.float32) * s
    gain = lambda shape: 1.0 + nrm(shape, 0.05)
    ne, no = (DEPTH + 1) // 2, DEPTH // 2
    D = D_MODEL
    gate_base = jnp.repeat(jnp.array([0.0, 3.0, 0.0, 3.0], jnp.float32), B_HEADS)
    return {
        "x": nrm((BATCH, SEQ, D), 1.0),
        "c": nrm((BATCH, D), 1.0),
        "ctx": nrm((BATCH, CTX_LEN, D), 1.0),
        "c_ctx": nrm((D,), 1.0),
        "w_ada": nrm((DEPTH, D, 6 * D), 0.5 * D ** -0.5),
        "b_ada": nrm((DEPTH, 6 * D), 0.01),
        "g_mix": gain((DEPTH, D)),
        "g_ffn": gain((DEPTH, D)),
        "e_w_in": nrm((ne, D, IN_EVEN), D ** -0.5),
        "e_w_out": nrm((ne, MIX_EVEN, D), MIX_EVEN ** -0.5),
        "e_g_q": gain((ne, A_HEAD_DIM)),
        "e_g_k": gain((ne, A_HEAD_DIM)),
        "e_conv_w": nrm((ne, B_CONV, 2 * B_WIDTH), B_CONV ** -0.5),
        "e_conv_b": nrm((ne, 2 * B_WIDTH), 0.01),
        "e_b_gates": gate_base + nrm((ne, 4 * B_HEADS), 0.1),
        "e_g_h": gain((ne, B_WIDTH)),
        "o_w_in": nrm((no, D, IN_ODD), D ** -0.5),
        "o_w_out": nrm((no, MIX_ODD, D), MIX_ODD ** -0.5),
        "o_g_qc": gain((no, C_HEAD_DIM)),
        "o_g_kc": gain((no, C_HEAD_DIM)),
        "o_lam": nrm((no, 4, C_HEAD_DIM), 0.1),
        "o_g_sub": gain((no, C_V_DIM)),
        "o_g_cq": gain((no, D_Q_LORA)),
        "o_w_uq": nrm((no, D_Q_LORA, D_HEADS * (D_NOPE + D_ROPE)), D_Q_LORA ** -0.5),
        "o_g_ckv": gain((no, D_KV_LORA)),
        "o_w_ukv": nrm((no, D_KV_LORA, D_HEADS * (D_NOPE + D_V_DIM)), D_KV_LORA ** -0.5),
        "o_g_qd": gain((no, D_NOPE + D_ROPE)),
        "o_g_kd": gain((no, D_NOPE + D_ROPE)),
        "w_router": nrm((D, N_EXPERTS), D ** -0.5),
        "b_router": nrm((N_EXPERTS,), 0.01),
        "w1": nrm((DEPTH, N_EXPERTS, D, D_EXPERT), D ** -0.5),
        "w3": nrm((DEPTH, N_EXPERTS, D, D_EXPERT), D ** -0.5),
        "w2": nrm((DEPTH, N_EXPERTS, D_EXPERT, D), D_EXPERT ** -0.5),
    }

def reference(x, c, ctx, c_ctx, w_ada, b_ada, g_mix, g_ffn,
              e_w_in, e_w_out, e_g_q, e_g_k, e_conv_w, e_conv_b, e_b_gates, e_g_h,
              o_w_in, o_w_out, o_g_qc, o_g_kc, o_lam, o_g_sub, o_g_cq, o_w_uq, o_g_ckv, o_w_ukv,
              o_g_qd, o_g_kd, w_router, b_router, w1, w3, w2):
    bsz, n_lat, d = x.shape
    rope_64 = axial_rope_tables(n_lat, A_HEAD_DIM)
    rope_d = axial_rope_tables(n_lat, D_ROPE)
    x_lat, x_ctx = x, ctx
    for layer in range(DEPTH):
        last = layer == DEPTH - 1
        j = layer // 2
        mod_l = jax.nn.silu(c) @ w_ada[layer] + b_ada[layer]
        mod_c = jax.nn.silu(c_ctx) @ w_ada[layer] + b_ada[layer]
        sh1, sc1, g1, sh2, sc2, g2 = [m[:, None, :] for m in jnp.split(mod_l, 6, axis=-1)]
        sh1c, sc1c, g1c, sh2c, sc2c, g2c = jnp.split(mod_c, 6, axis=-1)
        h_l = modulate(x_lat, g_mix[layer], sh1, sc1)
        h_c = modulate(x_ctx, g_mix[layer], sh1c, sc1c)
        if layer % 2 == 0:
            o_l, o_c = even_mixer(h_l, h_c, not last, e_w_in[j], e_w_out[j], e_g_q[j], e_g_k[j],
                                  e_conv_w[j], e_conv_b[j], e_b_gates[j], e_g_h[j], rope_64)
        else:
            lam_init = 0.8 - 0.6 * math.exp(-0.3 * layer)
            o_l, o_c = odd_mixer(h_l, h_c, not last, lam_init, o_w_in[j], o_w_out[j], o_g_qc[j], o_g_kc[j],
                                 o_lam[j], o_g_sub[j], o_g_cq[j], o_w_uq[j], o_g_ckv[j], o_w_ukv[j],
                                 o_g_qd[j], o_g_kd[j], rope_64, rope_d)
        x_lat = x_lat + g1 * o_l
        f_l = modulate(x_lat, g_ffn[layer], sh2, sc2).reshape(-1, d)
        if last:
            y = moe(f_l, w_router, b_router, w1[layer], w3[layer], w2[layer])
            x_lat = x_lat + g2 * y.reshape(x_lat.shape)
        else:
            x_ctx = x_ctx + g1c * o_c
            f_c = modulate(x_ctx, g_ffn[layer], sh2c, sc2c).reshape(-1, d)
            n_ctx_tok = f_c.shape[0]
            y = moe(jnp.concatenate([f_c, f_l], axis=0), w_router, b_router, w1[layer], w3[layer], w2[layer])
            x_ctx = x_ctx + g2c * y[:n_ctx_tok].reshape(x_ctx.shape)
            x_lat = x_lat + g2 * y[n_ctx_tok:].reshape(x_lat.shape)
    return x_lat


_drawn_inputs = setup_inputs


def setup_inputs(seed=0):
    import zlib

    import numpy as np

    out = dict(_drawn_inputs(seed))
    spreads = {}
    factors = {'e_g_q': 7.242,
     'e_g_k': 8.0,
     'e_conv_b': 5.099,
     'e_g_h': 2.801,
     'o_g_qc': 4.214,
     'o_g_kc': 4.124,
     'o_lam': 3.081,
     'o_g_sub': 4.499,
     'o_g_cq': 8.0,
     'o_g_ckv': 5.297,
     'o_g_qd': 8.0,
     'o_g_kd': 7.951}
    for name, (base, spread) in spreads.items():
        noise = np.random.default_rng([zlib.crc32(name.encode()), seed]).standard_normal(out[name].shape)
        drawn = base * np.exp(spread * noise) if base else spread * noise
        out[name] = __import__('jax').numpy.asarray(drawn.astype(out[name].dtype))
    for name, factor in factors.items():
        out[name] = (out[name] * factor).astype(out[name].dtype)
    return out
```

```python
from contextlib import ExitStack

import numpy as np
import concourse.bass as bass
from concourse import mybir

F32 = mybir.dt.float32
I32 = mybir.dt.int32
U32 = mybir.dt.uint32
ALU = mybir.AluOpType
ACT = mybir.ActivationFunctionType
AX = mybir.AxisListType

P = 128
D = 1024
KD = D // P
SEQ, CTX = 1024, 256
T = SEQ + CTX
NT, NTC = T // P, CTX // P
NTL = NT - NTC
PAIRS = NT // 2
GRID_W = 64
EPS = 1e-6
AH, AD, AKV = 8, 64, 2
BH, BD = 4, 128
AW, AKW, BW = AH * AD, AKV * AD, BH * BD
IN_EVEN = AW + 2 * AKW + 4 * BW + 4 * BH
CH, CD, CV = 4, 64, 128
DH, DQL, DKL, DN, DR, DV = 4, 256, 128, 64, 32, 128
DK = DN + DR
CW = CH * CV
IN_ODD = 3 * CW + DQL + DKL + DR
LAM_INIT = 0.8 - 0.6 * float(np.exp(-0.3))
NE, NG, DE = 32, 4, 512
PER = NE // NG
MAXB = 2 * T // P + NE - 1
BIG = 1e30


class Count:

    def __init__(self, nc, name):
        self.sem, self.base, self.k = nc.alloc_semaphore(name), 0, 0

    def up(self, k=1):
        self.k += k
        return self.sem, k

    def now(self):
        return self.sem, self.base + self.k

    def turn(self, i, per):
        if i is None:
            return
        self.start = self.base + self.k if not hasattr(self, "start") or self.start is None else self.start
        self.base, self.k, self.per = self.start + i * per, 0, per

    def turned(self, turns):
        assert self.k == self.per, (self.k, self.per)
        self.base, self.k, self.start = self.start + turns * self.per, 0, None


def rstd(dve, c, out, v, s1, s2):
    dve.wait_ge(*c.now())
    dve.tensor_scalar(s1.bitcast(I32), v.bitcast(I32), 1, None, ALU.logical_shift_right).then_inc(*c.up())
    dve.wait_ge(*c.now())
    dve.tensor_scalar(out.bitcast(I32), s1.bitcast(I32), -1.0, float(0x5F3759DF), ALU.mult, ALU.add).then_inc(*c.up())
    for _ in range(3):
        dve.wait_ge(*c.now())
        dve.tensor_tensor(s1, out, out, ALU.mult).then_inc(*c.up())
        dve.wait_ge(*c.now())
        dve.tensor_tensor(s2, s1, v, ALU.mult).then_inc(*c.up())
        dve.wait_ge(*c.now())
        dve.tensor_scalar(s1, s2, -0.5, 1.5, ALU.mult, ALU.add).then_inc(*c.up())
        dve.wait_ge(*c.now())
        dve.tensor_tensor(out, out, s1, ALU.mult).then_inc(*c.up())


RSTD_N = 14

COLS_A = 96
COL_C, COL_CC, COL_GMIX, COL_GFFN, COL_CW, COL_CB = 0, 8, 16, 32, 48, 72
COLS_B = 80
V_SH1, V_SC1, V_G1, V_SH2, V_SC2, V_G2 = range(6)


class Shared:
    pass


def modulation(nc, g, A):
    NB = 4
    NCH = 2 * 6 * D // 512
    with nc.cleanup_on_exit():
        wa = nc.alloc_sbuf_tensor("wa", [P, NB, KD, 512], F32)
        rows_a = nc.alloc_sbuf_tensor("rows_a", [COLS_A, P], F32)
        rows_b = nc.alloc_sbuf_tensor("rows_b", [COLS_B, P], F32)
        ba = nc.alloc_sbuf_tensor("ba", [P, COLS_A], F32)
        th = nc.alloc_sbuf_tensor("th", [P, 2 * KD], F32)
        cs = nc.alloc_sbuf_tensor("cs", [P, 2, KD], F32)
        ps_cols = nc.alloc_psum_tensor("ps_cols", [P, 512], F32)
        mrow = nc.alloc_sbuf_tensor("mrow", [P, 2, 512], F32)
        ps_mod = nc.alloc_psum_tensor("ps_mod", [P, 2, 512], F32)
        ps_mt = nc.alloc_psum_tensor("ps_mt", [P, 2, 512], F32)
        vec_in = nc.alloc_semaphore("vec_in")
        const_in = nc.alloc_semaphore("const_in")
        x_copied = nc.alloc_semaphore("x_copied")
        w_in = [nc.alloc_semaphore(f"w_in{b}") for b in range(NB)]
        turned = nc.alloc_semaphore("turned")
        tanh_done = nc.alloc_semaphore("tanh_done")
        silu_done = nc.alloc_semaphore("silu_done")
        mod_mm = nc.alloc_semaphore("mod_mm")
        rows_clear = nc.alloc_semaphore("rows_clear")
        row_out = nc.alloc_semaphore("row_out")
        mod_turned = nc.alloc_semaphore("mod_turned")
        c = Count(nc, "dve_step")
        mod_out = nc.alloc_semaphore("mod_out")
        w_view = A["w_ada"].rearrange("l (k p) n -> p l k n", p=P)
        with nc.Block() as block:

            @block.sync
            def _(sp):
                sp.dma_start(g.consts[:, :], A["consts"]).then_inc(const_in, 16)
                sp.dma_start(rows_a[:, :], A["b_ada"].rearrange("l (a p) -> (l a) p", p=P)).then_inc(vec_in, 16)
                for at, name, pat in ((COL_C, "c", "a (k p) -> (a k) p"), (COL_CC, "c_ctx", "(k p) -> k p"),
                                      (COL_GMIX, "g_mix", "a (k p) -> (a k) p"), (COL_GFFN, "g_ffn", "a (k p) -> (a k) p"),
                                      (COL_CW, "e_conv_w", "a w (k p) -> (a w k) p"), (COL_CB, "e_conv_b", "a (k p) -> (a k) p")):
                    src = A[name].rearrange(pat, p=P)
                    sp.dma_start(rows_b[at:at + src.shape[0], :], src).then_inc(vec_in, 16)
                with sp.Fori(0, NCH // NB) as i:
                    for b in range(NB):
                        sp.wait_ge(mod_mm, i * NB + b + 1)
                        layer = i // (NCH // NB // 2)
                        col = (i % (NCH // NB // 2)) * (NB * 512) + b * 512
                        sp.dma_start(wa[:, b, :, :], w_view[:, bass.ds(layer, 1), :, bass.ds(col, 512)].rearrange("p l k n -> p (l k) n")).then_inc(w_in[b], 16)
                for name, dst in g.broadcasts:
                    sp.dma_start(dst, A[name].partition_broadcast(P)).then_inc(const_in, 16)
                sp.dma_start(g.rope[:, :, :], A["rope"].rearrange("(t p) r -> p t r", p=P)).then_inc(const_in, 16)
                sp.wait_ge(const_in, 16 * (2 + len(g.broadcasts)))

            @block.gpsimd
            def _(pool):
                pool.dma_start(g.x_dram[0:CTX, :], A["ctx"].rearrange("b t d -> (b t) d")).then_inc(x_copied, 16)
                pool.dma_start(g.x_dram[CTX:T, :], A["x"].rearrange("b t d -> (b t) d")).then_inc(x_copied, 16)
                pool.wait_ge(x_copied, 32)

            @block.tensor
            def _(pe):
                pe.sem_inc(mod_mm, NB)
                pe.wait_ge(const_in, 16)
                pe.wait_ge(vec_in, 16 * 7)
                pe.transpose(ps_cols[:, 0:COLS_A], rows_a[:, :], g.ident[0:COLS_A, 0:COLS_A])
                pe.transpose(ps_cols[:, 128:128 + COLS_B], rows_b[:, :], g.ident[0:COLS_B, 0:COLS_B]).then_inc(turned, 1)
                pe.wait_ge(silu_done, 1)
                with pe.Fori(0, NCH // NB) as i:
                    for b in range(NB):
                        pe.wait_ge(w_in[b], i * 16 + 16)
                        pe.wait_ge(row_out, i * NB + b + 1)
                        for k in range(KD):
                            mm = pe.matmul(ps_mod[0:2, b % 2, :], cs[:, :, k], wa[:, b, k, :], start=k == 0, stop=k == KD - 1)
                        mm.then_inc(mod_mm, 1)
                        pe.wait_ge(row_out, i * NB + b + 3)
                        pe.wait_ge(mod_out, i * NB + b + 1)
                        for m in range(4):
                            mm = pe.transpose(ps_mt[:, b % 2, m * P:(m + 1) * P], mrow[:, b % 2, m * P:(m + 1) * P], g.ident)
                        mm.then_inc(mod_turned, 1)

            @block.scalar
            def _(act):
                act.wait_ge(c.sem, 2)
                act.activation(th[:, :], g.cols[:, 0:2 * KD], ACT.Tanh, scale=0.5).then_inc(tanh_done, 1)
                act.wait_ge(rows_clear, 1)
                act.sem_inc(row_out, 2)
                with act.Fori(0, NCH // NB) as i:
                    for b in range(NB):
                        act.wait_ge(mod_mm, i * NB + b + 1 + NB)
                        act.wait_ge(mod_out, i * NB + b + 1)
                        act.copy(mrow[0:2, b % 2, :], ps_mod[0:2, b % 2, :]).then_inc(row_out, 1)

            @block.vector
            def _(dve):
                dve.memset(mrow[:, :, :], 0.0).then_inc(rows_clear, 1)
                dve.sem_inc(mod_out, 2)
                dve.wait_ge(turned, 1)
                dve.tensor_copy(ba[:, :], ps_cols[:, 0:COLS_A]).then_inc(*c.up())
                dve.tensor_copy(g.cols[:, :], ps_cols[:, 128:128 + COLS_B]).then_inc(*c.up())
                dve.wait_ge(*c.now())
                dve.wait_ge(tanh_done, 1)
                dve.scalar_tensor_tensor(out=th[:, :], in0=th[:, :], scalar=1.0, in1=g.cols[:, 0:2 * KD], op0=ALU.add, op1=ALU.mult).then_inc(*c.up())
                dve.wait_ge(*c.now())
                dve.tensor_scalar(cs[:, :, :].rearrange("p a k -> p (a k)"), th[:, :], 0.5, None, ALU.mult).then_inc(silu_done, 1)
                with dve.Fori(0, NCH // NB) as i:
                    for b in range(NB):
                        dve.wait_ge(mod_turned, i * NB + b + 1)
                        at = i * (NB * 4) + b * 4
                        dve.tensor_tensor(g.mod[:, bass.ds(at, 4), :], ps_mt[:, b % 2, :].rearrange("p (m w) -> p m w", w=P)[:, :, 0:2],
                                          ba[:, bass.ds(at, 4)].unsqueeze(2).to_broadcast([P, 4, 2]), ALU.add).then_inc(mod_out, 1)
                dve.wait_ge(mod_out, NCH + 2)
                for layer in range(2):
                    for n, (v, gain) in enumerate(((V_SC1, COL_GMIX), (V_SC2, COL_GFFN))):
                        a = layer * 48 + v * KD
                        dve.scalar_tensor_tensor(out=g.gain[:, layer, n, :, :], in0=g.mod[:, a:a + KD, :], scalar=1.0,
                                                 in1=g.cols[:, gain + layer * KD:gain + layer * KD + KD].unsqueeze(2).to_broadcast([P, KD, 2]),
                                                 op0=ALU.add, op1=ALU.mult).then_inc(*c.up())


def head_norm_rope(dve, c, g, S, n, hd, gain, rope, src, dst):
    x3 = src.rearrange("p (n d) -> p n d", n=n)
    sq3, nrm3 = S.sq[:, 0:n * hd].rearrange("p (n d) -> p n d", n=n), S.nrm[:, 0:n * hd].rearrange("p (n d) -> p n d", n=n)
    dve.wait_ge(*c.now())
    dve.tensor_tensor(sq3, x3, x3, ALU.mult).then_inc(*c.up())
    dve.wait_ge(*c.now())
    dve.tensor_reduce(S.ss[:, 0:n], sq3, AX.X, ALU.add).then_inc(*c.up())
    dve.wait_ge(*c.now())
    dve.tensor_scalar(S.ss[:, 0:n], S.ss[:, 0:n], 1.0 / hd, EPS, ALU.mult, ALU.add).then_inc(*c.up())
    rstd(dve, c, S.r[:, 0:n], S.ss[:, 0:n], S.s1[:, 0:n], S.s2[:, 0:n])
    dve.wait_ge(*c.now())
    dve.tensor_tensor(nrm3, x3, S.r[:, 0:n].unsqueeze(2).to_broadcast([P, n, hd]), ALU.mult).then_inc(*c.up())
    dve.wait_ge(*c.now())
    gained = nrm3 if rope else dst.rearrange("p (n d) -> p n d", n=n)
    dve.tensor_tensor(gained, nrm3, gain, ALU.mult).then_inc(*c.up())


HEAD_NORM_N = 3 + RSTD_N + 2


def rope_pairs(dve, c, S, x3, out3, cos, sin):
    a, b = S.ra[:, 0:x3.shape[1], 0:cos.shape[2]], S.rb[:, 0:x3.shape[1], 0:cos.shape[2]]
    for first, second, op, at in ((cos, sin, ALU.subtract, 0), (sin, cos, ALU.add, 1)):
        dve.wait_ge(*c.now())
        dve.tensor_tensor(a, x3[:, :, 0::2], first, ALU.mult).then_inc(*c.up())
        dve.tensor_tensor(b, x3[:, :, 1::2], second, ALU.mult).then_inc(*c.up())
        dve.wait_ge(*c.now())
        dve.tensor_tensor(out3[:, :, at::2], a, b, op).then_inc(*c.up())


ROPE_N = 6


def mod_pairs(dve, c, g, layer, sel):
    for pair in range(PAIRS):
        w = 1 if pair == 0 else 0
        dve.tensor_copy(sel[:, pair, 0, :], g.gain[:, layer, 0, :, w]).then_inc(*c.up())
        dve.tensor_copy(sel[:, pair, 1, :], g.mod[:, layer * 48 + V_SH1 * KD:layer * 48 + V_SH1 * KD + KD, w]).then_inc(*c.up())


def even_project(nc, g, A, L):
    QK = AW + AKW
    Z0 = AW + 2 * AKW
    V0 = Z0 + 2 * BW
    with nc.cleanup_on_exit():
        w = nc.alloc_sbuf_tensor("w", [P, KD, IN_EVEN], F32)
        x = nc.alloc_sbuf_tensor("x", [P, 2, D], F32)
        hT = nc.alloc_sbuf_tensor("hT", [P, 2, KD, P], F32)
        S = Shared()
        qk = nc.alloc_sbuf_tensor("qk", [P, QK], F32)
        S.sq = nc.alloc_sbuf_tensor("sq", [P, QK], F32)
        S.nrm = nc.alloc_sbuf_tensor("nrm", [P, QK], F32)
        qkr = S.sq
        S.ra = nc.alloc_sbuf_tensor("ra", [P, AH + AKV, AD // 2], F32)
        S.rb = nc.alloc_sbuf_tensor("rb", [P, AH + AKV, AD // 2], F32)
        vo = nc.alloc_sbuf_tensor("vo", [P, 2 * BW], F32)
        S.ss = nc.alloc_sbuf_tensor("hn_ss", [P, 16], F32)
        S.r = nc.alloc_sbuf_tensor("hn_r", [P, 16], F32)
        S.s1 = nc.alloc_sbuf_tensor("hn_s1", [P, 16], F32)
        S.s2 = nc.alloc_sbuf_tensor("hn_s2", [P, 16], F32)
        xs = nc.alloc_sbuf_tensor("xs", [P, 2, 8], F32)
        sel = nc.alloc_sbuf_tensor("sel", [P, PAIRS, 2, KD], F32)
        now = nc.alloc_sbuf_tensor("now", [P, 2, KD], F32)
        gqk = nc.alloc_sbuf_tensor("gqk", [P, AH + AKV, AD], F32)
        ps_ab = nc.alloc_psum_tensor("ps_ab", [P, 2, 2, 512], F32)
        ps_r = nc.alloc_psum_tensor("ps_r", [P, 4, 512], F32)

        def s(name):
            return nc.alloc_semaphore("ep_" + name)

        w_in, x_sq, xh_ready = s("w_in"), s("x_sq"), s("xh_ready")
        x_in = [s("x_in0"), s("x_in1")]
        t_done, h_act, h_dve = s("t_done"), s("h_act"), s("h_dve")
        r_done, r_act, r_dve = s("r_done"), s("r_act"), s("r_dve")
        z_done, z_act, z_dve = s("z_done"), s("z_act"), s("z_dve")
        qk_ready, qt_done, qt_act, qt_dve, vo_out, now_ready = s("qk_ready"), s("qt_done"), s("qt_act"), s("qt_dve"), s("vo_out"), s("now_ready")
        zeros = nc.alloc_sbuf_tensor("zeros", [P, 512], F32)
        zeroed, filled = s("zeroed"), s("filled")
        c = Count(nc, "ep_dve_step")
        with nc.Block() as block:

            @block.sync
            def _(sp):
                for k in range(KD):
                    sp.dma_start(w[:, k, :], A["e_w_in"][0, k * P:(k + 1) * P, :]).then_inc(w_in, 16)
                with sp.Fori(0, PAIRS) as i:
                    for h in range(2):
                        sp.wait_ge(t_done, i * 4 + 2 * h + 2)
                        sp.dma_start(x[:, h, :], g.x_dram[bass.ds(i * 256 + h * P, P), :]).then_inc(x_in[h], 16)

            @block.gpsimd
            def _(pool):
                pool.memset(zeros[:, :], 0.0).then_inc(zeroed, 1)
                pool.wait_ge(zeroed, 1)
                rows = g.y_dram.rearrange("(b p) d -> p b d", p=P)
                for half in range(2):
                    pool.dma_start(rows[:, :, half * 512:(half + 1) * 512],
                                   zeros[:, :].unsqueeze(1).to_broadcast([P, MAXB, 512])).then_inc(filled, 16)
                pool.wait_ge(filled, 32)

            @block.tensor
            def _(pe):
                pe.sem_inc(t_done, 4)
                pe.sem_inc(qt_done, 1)

                def transposes(i, h):
                    pe.wait_ge(xh_ready, i * 2 + h + 1)
                    pe.wait_ge(qt_act, i * 2 + h + 1)
                    pe.wait_ge(qt_dve, i * 2 + h + 1)
                    for half in range(2):
                        for k in range(4 * half, 4 * half + 4):
                            mm = pe.transpose(ps_ab[:, h, half, (k % 4) * P:(k % 4) * P + P], x[:, h, k * P:(k + 1) * P], g.ident)
                        mm.then_inc(t_done, 1)

                def rows(i, h):
                    pe.wait_ge(h_act, i * 2 + h + 1)
                    pe.wait_ge(h_dve, i * 2 + h + 1)
                    for n, cols in enumerate(((0, AW), (AW, Z0), (V0, V0 + BW), (V0 + BW, V0 + 2 * BW))):
                        if n == 1:
                            pe.wait_ge(r_dve, i * 2 + h + 1)
                        else:
                            pe.wait_ge(r_act, i * 6 + 3 * h + (1, 0, 2, 3)[n])
                        for k in range(KD):
                            mm = pe.matmul(ps_r[:, n, 0:cols[1] - cols[0]], hT[:, h, k, :], w[:, k, cols[0]:cols[1]],
                                           start=k == 0, stop=k == KD - 1)
                        if n == 1:
                            for k in range(KD):
                                mm = pe.matmul(ps_r[:, n, 256:384], hT[:, h, k, :], w[:, k, IN_EVEN - P:IN_EVEN],
                                               start=k == 0, stop=k == KD - 1)
                        mm.then_inc(r_done, 1)

                def channels(i, h):
                    for half in range(2):
                        for cc in range(4 * half, 4 * half + 4):
                            for k in range(KD):
                                mm = pe.matmul(ps_ab[:, h, half, (cc % 4) * P:(cc % 4) * P + P], w[:, k, Z0 + cc * P:Z0 + (cc + 1) * P],
                                               hT[:, h, k, :], start=k == 0, stop=k == KD - 1)
                        mm.then_inc(z_done, 1)

                def turn_qk(i, h):
                    pe.wait_ge(qk_ready, i * 2 + h + 2)
                    pe.wait_ge(z_act, i * 2 + h + 1)
                    pe.wait_ge(z_dve, i * 2 + h + 1)
                    for j in range(4):
                        pe.transpose(ps_ab[:, h, 0, j * P:(j + 1) * P], qkr[:, j * P:(j + 1) * P], g.ident)
                    pe.transpose(ps_ab[:, h, 1, 0:P], qkr[:, AW:AW + P], g.ident).then_inc(qt_done, 1)

                pe.wait_ge(w_in, 16 * KD)
                with pe.Fori(0, PAIRS) as i:
                    transposes(i, 0)
                    transposes(i, 1)
                    rows(i, 0)
                    channels(i, 0)
                    rows(i, 1)
                    turn_qk(i, 0)
                    channels(i, 1)
                    turn_qk(i, 1)

            @block.scalar
            def _(act):
                act.sem_inc(qt_act, 2)
                act.sem_inc(r_act, 3)

                def squares(i, h):
                    act.wait_ge(x_in[h], i * 16 + 16)
                    act.wait_ge(qt_act, i * 2 + h + 1)
                    act.wait_ge(qt_dve, i * 2 + h + 1)
                    act.activation(ps_ab[:, h, :, :].rearrange("p a n -> p (a n)"), x[:, h, :], ACT.Square,
                                   accum_out=xs[:, h, 0:1]).then_inc(x_sq, 1)

                def modulate(i, h):
                    act.wait_ge(t_done, i * 4 + 2 * h + 5)
                    for k in range(4):
                        m = act.activation(hT[:, h, k, :], ps_ab[:, h, 0, k * P:(k + 1) * P], ACT.Identity,
                                           scale=now[:, 0, k:k + 1], bias=now[:, 1, k:k + 1])
                    m.then_inc(h_act, 1)

                def rows_out(i, h):
                    act.wait_ge(r_done, i * 8 + 4 * h + 1)
                    act.wait_ge(qk_ready, i * 2 + h + 1)
                    act.copy(qk[:, 0:AW].rearrange("p (h k d) -> p k h d", k=AKV, d=AD),
                             ps_r[:, 0, :].rearrange("p (k h d) -> p k h d", k=AKV, d=AD)).then_inc(r_act, 1)
                    act.wait_ge(r_done, i * 8 + 4 * h + 3)
                    act.wait_ge(vo_out, i * 32 + 16 * h + 16)
                    act.copy(vo[:, 0:BW], ps_r[:, 2, :]).then_inc(r_act, 1)
                    act.wait_ge(r_done, i * 8 + 4 * h + 4)
                    act.activation(vo[:, BW:2 * BW], ps_r[:, 3, :], ACT.Tanh, scale=0.5).then_inc(r_act, 1)
                    act.wait_ge(r_act, i * 6 + 3 * h + 6)
                    act.dma_start(g.vo_dram[bass.ds(i * 256 + h * P, P), :], vo[:, :]).then_inc(vo_out, 16)

                def channels_out(i, h):
                    act.wait_ge(z_done, i * 4 + 2 * h + 1)
                    act.copy(L.zT[:, 0:4, bass.ds(i * 256 + h * P, P)],
                             ps_ab[:, h, 0, :].rearrange("p (a n) -> p a n", n=P)).then_inc(z_act, 1)

                def q_out(i, h):
                    act.wait_ge(qt_done, i * 2 + h + 2)
                    act.copy(L.qT[:, :, bass.ds(i * 256 + h * P, P)],
                             ps_ab[:, h, 0, :].rearrange("p (a n) -> p a n", n=P)).then_inc(qt_act, 1)

                act.sem_inc(vo_out, 16)
                act.sem_inc(qk_ready, 1)
                with act.Fori(0, PAIRS) as i:
                    squares(i, 0)
                    squares(i, 1)
                    act.wait_ge(now_ready, i + 1)
                    modulate(i, 0)
                    modulate(i, 1)
                    rows_out(i, 0)
                    channels_out(i, 0)
                    rows_out(i, 1)
                    q_out(i, 0)
                    channels_out(i, 1)
                    q_out(i, 1)
                act.wait_ge(vo_out, 16 * NT + 16)

            @block.vector
            def _(dve):
                dve.sem_inc(qt_dve, 2)
                dve.sem_inc(r_dve, 1)
                dve.tensor_copy(gqk[:, 0:AH, :], g.bc["e_g_q"].unsqueeze(1).to_broadcast([P, AH, AD])).then_inc(*c.up())
                dve.tensor_copy(gqk[:, AH:, :], g.bc["e_g_k"].unsqueeze(1).to_broadcast([P, AKV, AD])).then_inc(*c.up())
                mod_pairs(dve, c, g, 0, sel)

                def normalise(i, h):
                    dve.wait_ge(x_sq, i * 2 + h + 1)
                    dve.tensor_scalar(xs[:, h, 1:2], xs[:, h, 0:1], 1.0 / D, EPS, ALU.mult, ALU.add).then_inc(*c.up())
                    rstd(dve, c, xs[:, h, 2:3], xs[:, h, 1:2], xs[:, h, 3:4], xs[:, h, 4:5])
                    dve.wait_ge(*c.now())
                    dve.tensor_scalar(x[:, h, :], x[:, h, :], xs[:, h, 2:3], None, ALU.mult).then_inc(xh_ready, 1)

                def modulate(i, h):
                    dve.wait_ge(t_done, i * 4 + 2 * h + 6)
                    for k in range(4, 8):
                        m = dve.tensor_scalar(hT[:, h, k, :], ps_ab[:, h, 1, (k - 4) * P:(k - 3) * P],
                                              now[:, 0, k:k + 1], now[:, 1, k:k + 1], ALU.mult, ALU.add)
                    m.then_inc(h_dve, 1)

                def rows_out(i, h):
                    dve.wait_ge(r_done, i * 8 + 4 * h + 2)
                    dve.tensor_copy(qk[:, AW:QK], ps_r[:, 1, 0:AKW]).then_inc(*c.up())
                    dve.tensor_copy(L.v[:, bass.ds(i * 2 + h, 1), :], ps_r[:, 1, AKW:2 * AKW].unsqueeze(1)).then_inc(*c.up())
                    dve.tensor_tensor(L.gates[:, bass.ds(i * 2 + h, 1), :], ps_r[:, 1, 3 * P - 4 * BH:3 * P].unsqueeze(1),
                                      g.bc["e_b_gates"].unsqueeze(1), ALU.add).then_inc(r_dve, 1)
                    dve.wait_ge(r_act, i * 6 + 3 * h + 4)
                    dve.wait_ge(qt_done, i * 2 + h + 1)
                    head_norm_rope(dve, c, g, S, AH + AKV, AD, gqk[:, :, :], True, qk[:, :], None)
                    n3 = S.nrm[:, :].rearrange("p (n d) -> p n d", d=AD)
                    o3 = qkr[:, :].rearrange("p (n d) -> p n d", d=AD)
                    cos = g.rope[:, bass.ds(i * 2 + h, 1), 0:32].to_broadcast([P, AH + AKV, 32])
                    sin = g.rope[:, bass.ds(i * 2 + h, 1), 32:64].to_broadcast([P, AH + AKV, 32])
                    rope_pairs(dve, c, S, n3, o3, cos, sin)
                    dve.wait_ge(*c.now())
                    dve.sem_inc(qk_ready, 1)

                def channels_out(i, h):
                    dve.wait_ge(z_done, i * 4 + 2 * h + 2)
                    dve.tensor_copy(L.zT[:, 4:8, bass.ds(i * 256 + h * P, P)],
                                    ps_ab[:, h, 1, :].rearrange("p (a n) -> p a n", n=P)).then_inc(z_dve, 1)

                def k_out(i, h):
                    dve.wait_ge(qt_done, i * 2 + h + 2)
                    dve.tensor_copy(L.kT[:, bass.ds(i * 256 + h * P, P)], ps_ab[:, h, 1, 0:P]).then_inc(qt_dve, 1)

                with dve.Fori(0, PAIRS) as i:
                    c.turn(i, 1 + 2 * (1 + RSTD_N) + 2 * (2 + HEAD_NORM_N + ROPE_N))
                    dve.wait_ge(x_sq, i * 2 + 1)
                    dve.wait_ge(*c.now())
                    dve.tensor_copy(now[:, :, :], sel[:, bass.ds(i, 1), :, :].rearrange("p o a k -> p (o a) k")).then_inc(*c.up())
                    dve.wait_ge(*c.now())
                    dve.sem_inc(now_ready, 1)
                    normalise(i, 0)
                    normalise(i, 1)
                    modulate(i, 0)
                    modulate(i, 1)
                    rows_out(i, 0)
                    channels_out(i, 0)
                    rows_out(i, 1)
                    k_out(i, 0)
                    channels_out(i, 1)
                    k_out(i, 1)
                c.turned(PAIRS)



def even_mlstm(nc, g, A, L):
    NC = 64

    def s(name):
        return nc.alloc_semaphore("ml_" + name)

    with nc.cleanup_on_exit():
        tab = nc.alloc_sbuf_tensor("ml_tab", [P, 12, P], F32)
        lf, ig, bcum, a_row, mx_row, g_row, ai_row, ai_col, a_col, g_col, em_col, dec = (tab[:, n, :] for n in range(12))
        cols4 = tab[:, 8:12, :]
        cur = nc.alloc_sbuf_tensor("ml_cur", [P, 4, 4, BH], F32)
        m_row = nc.alloc_sbuf_tensor("ml_m_row", [1, 4, P], F32)
        m_col = nc.alloc_sbuf_tensor("ml_m_col", [P, 4], F32)
        halfw = nc.alloc_sbuf_tensor("ml_halfw", [P, 32], F32)
        arena = nc.alloc_sbuf_tensor("ml_arena", [P, 4 * T], F32)
        yb = arena[:, 0:2 * T].rearrange("p (a t) -> p a t", a=2)
        tb = arena[:, 2 * T:4 * T].rearrange("p (a t) -> p a t", a=2)
        bc = arena[:, 0:4 * 2 * BH * P].rearrange("p (b n f) -> p b n f", b=4, n=2)
        row_dram = nc.dram_tensor("ml_rows", (2, 2, NC, P), F32, kind="Internal").ap()
        qs = nc.alloc_sbuf_tensor("ml_qs", [P, 4, BH, P], F32)
        ks = nc.alloc_sbuf_tensor("ml_ks", [P, 4, BH, P], F32)
        qa = nc.alloc_sbuf_tensor("ml_qa", [P, 4, BH, P], F32)
        tm = nc.alloc_sbuf_tensor("ml_tm", [P, 4, BH, P], F32)
        vv = nc.alloc_sbuf_tensor("ml_vv", [P, 4, BH, P + 4], F32)
        wt = nc.alloc_sbuf_tensor("ml_wt", [P, 2, BH, P], F32)
        sw = nc.alloc_sbuf_tensor("ml_sw", [P, 2, BH, P], F32)
        kg = nc.alloc_sbuf_tensor("ml_kg", [P, 2, BH, P], F32)
        C = nc.alloc_sbuf_tensor("ml_C", [P, 2, BH, P + 4], F32)
        dn = nc.alloc_sbuf_tensor("ml_dn", [P, 3, BH], F32)
        ps_s = nc.alloc_psum_tensor("ml_ps_s", [P, 2, 512], F32)
        ps_k = nc.alloc_psum_tensor("ml_ps_k", [P, 2, 512], F32)
        ps_n = nc.alloc_psum_tensor("ml_ps_n", [P, 2, 512], F32)
        ps_c = nc.alloc_psum_tensor("ml_ps_c", [P, 2, 512], F32)
        c = Count(nc, "ml_dve_step")
        conv_out, tanh_done, gate_abs, gate_exp, gate_ln, lf_ready = (s("conv_out"), s("tanh_done"), s("gate_abs"),
                                                                      s("gate_exp"), s("gate_ln"), s("lf_ready"))
        gp, gd, ga = s("gate_pe"), s("gate_dve"), s("gate_act")
        rows_out, tabs_ready, act_ln = s("rows_out"), s("tabs_ready"), s("act_ln")
        loaded = [s(f"loaded{b}") for b in range(4)]
        staged, s_done, k_done, n_done, c_done = s("staged"), s("s_done"), s("k_done"), s("n_done"), s("c_done")
        w_ready, sw_ready, kg_ready, h_out, c_out, z_ready = (s("w_ready"), s("sw_ready"), s("kg_ready"), s("h_out"),
                                                              s("c_out"), s("z_ready"))

        def place(ps, h):
            return ps[:, 0, h * 129:(h + 1) * 129] if h < 3 else ps[:, 1, 0:129]

        def turns(eng, body):
            body(0, 0, lambda par: (par, 1 - par))
            with eng.Fori(0, NTL // 2) as i:
                body(i + 1, i * 2 + 2, lambda par: (i * 2 + 2 + par, i * (-2) + 9 - par))

        with nc.Block() as block:

            @block.sync
            def _(sp):
                sp.wait_ge(gd, 6)
                sp.dma_start(row_dram[0].rearrange("d r t -> (d r) t"), mx_row).then_inc(rows_out, 16)
                sp.wait_ge(ga, 1)
                sp.dma_start(row_dram[1].rearrange("d r t -> (d r) t"), ai_row).then_inc(rows_out, 16)
                sp.wait_ge(rows_out, 32)
                sp.wait_ge(z_ready, 1)

                def body(it, step, tiles):
                    for par in range(2):
                        for d in range(2):
                            b = 2 * par + d
                            tok, row = tiles(par)[d] * P, step * 4 + 4 * par
                            sp.wait_ge(c_done, it * 4 + b + 1)
                            sp.wait_ge(staged, (it * 4 + b) * 5 + 5)
                            for n in range(2):
                                src = row_dram[n, d:d + 1, bass.ds(row, BH), :].rearrange("d r t -> d (r t)")
                                sp.dma_start(bc[:, b, n, :], src.to_broadcast([P, BH * P])).then_inc(loaded[b], 16)
                            sp.dma_start(vv[:, b, :, 0:P], g.vo_dram[bass.ds(tok, P), 0:BW].rearrange("p (h e) -> p h e", e=P)).then_inc(loaded[b], 16)

                turns(sp, body)

            @block.gpsimd
            def _(pool):
                pool.sem_inc(staged, 20)
                pool.wait_ge(z_ready, 1)
                pool.wait_ge(tabs_ready, 1)

                def body(it, step, tiles):
                    for par in range(2):
                        for d in range(2):
                            b, tile = 2 * par + d, tiles(par)[d]
                            pool.wait_ge(loaded[b], it * 48 + 48)
                            pool.wait_ge(c_done, it * 4 + b + 1)
                            pool.wait_ge(w_ready, it * 4 + b + 1)
                            pool.wait_ge(c_out, it * 4 + b + 1)
                            pool.tensor_copy(cur[:, b, :, :], cols4[:, :, bass.ds(step * 4 + 4 * par + d * NC, BH)]).then_inc(staged, 1)
                            q = L.zT[:, 0:4, bass.ds(tile * P, P)]
                            pool.tensor_copy(qs[:, b, :, :], q).then_inc(staged, 1)
                            pool.tensor_copy(ks[:, b, :, :], L.zT[:, 4:8, bass.ds(tile * P, P)]).then_inc(staged, 1)
                            pool.tensor_tensor(tm[:, b, :, :], g.consts[:, (4 + d) * P:(5 + d) * P].unsqueeze(1).to_broadcast([P, BH, P]),
                                               bc[:, b, 0, :].rearrange("p (h t) -> p h t", t=P), ALU.subtract).then_inc(staged, 1)
                            pool.tensor_tensor(qa[:, b, :, :], q, bc[:, b, 1, :].rearrange("p (h t) -> p h t", t=P), ALU.mult).then_inc(staged, 1)

                turns(pool, body)

            @block.tensor
            def _(pe):
                pe.wait_ge(lf_ready, 1)
                pe.matmul(ps_s[:, 0, 0:NC], g.consts[:, 2 * P:3 * P], lf[:, 0:NC], start=True, stop=True)
                pe.matmul(ps_s[:, 1, 0:NC], g.consts[:, 3 * P:4 * P], lf[:, NC:2 * NC], start=True, stop=True)
                pe.matmul(ps_k[0:1, 0, 0:P], g.ones[:, 0:1], lf, start=True, stop=True).then_inc(gp, 1)
                pe.wait_ge(gd, 1)
                pe.transpose(ps_k[:, 1, 0:P], a_col, g.ident).then_inc(gp, 1)
                pe.wait_ge(gd, 2)
                pe.transpose(ps_n[0:1, 0, 0:P], m_col[:, 0:1], g.ident).then_inc(gp, 1)
                pe.wait_ge(gd, 3)
                pe.matmul(ps_n[:, 1, 0:1], m_row[0:1, 2, :], g.ident[0:1, 0:1], start=True, stop=True).then_inc(gp, 1)
                pe.wait_ge(gd, 6)
                pe.transpose(ps_c[:, 0, 0:P], mx_row, g.ident).then_inc(gp, 1)
                pe.wait_ge(ga, 2)
                pe.transpose(ps_c[:, 1, 0:P], g_row, g.ident)
                pe.transpose(ps_c[:, 1, P:2 * P], ai_row, g.ident).then_inc(gp, 1)
                pe.wait_ge(gd, 8)
                pe.matmul(ps_s[:, 0, 0:P], g.ident[:, P - 1:P].to_broadcast([P, P]), ai_col, start=True, stop=True)
                pe.matmul(ps_s[:, 1, 0:P], g.ident[:, 0:1].to_broadcast([P, P]), ai_col, start=True, stop=True).then_inc(gp, 1)
                pe.sem_inc(c_done, 4)

                def body(it, step, tiles):
                    for par in range(2):
                        for d in range(2):
                            b = 2 * par + d
                            u = it * 4 + b
                            pe.wait_ge(staged, u * 5 + 25)
                            pe.wait_ge(sw_ready, u + 1)
                            for h in range(BH):
                                mm = pe.matmul(ps_s[:, d, h * P:(h + 1) * P], ks[:, b, h, :], qs[:, b, h, :], start=True, stop=True)
                            mm.then_inc(s_done, 1)
                            pe.wait_ge(kg_ready, u + 1)
                            for h in range(BH):
                                mm = pe.transpose(ps_k[:, d, h * P:(h + 1) * P], ks[:, b, h, :], g.ident)
                            mm.then_inc(k_done, 1)
                        for d in range(2):
                            b = 2 * par + d
                            u = it * 4 + b
                            pe.wait_ge(sw_ready, u + 3)
                            pe.wait_ge(h_out, u + 1)
                            pe.wait_ge(c_out, u + 4)
                            for h in range(BH):
                                pe.matmul(place(ps_n, h), sw[:, d, h, :], vv[:, b, h, 0:129], start=True, stop=False)
                                mm = pe.matmul(place(ps_n, h), qa[:, b, h, :], C[:, d, h, 0:129], start=False, stop=True)
                            mm.then_inc(n_done, 1)
                            pe.wait_ge(kg_ready, u + 3)
                            for h in range(BH):
                                mm = pe.matmul(place(ps_c, h), kg[:, d, h, :], vv[:, b, h, 0:129], start=True, stop=True)
                            mm.then_inc(c_done, 1)

                turns(pe, body)

            @block.scalar
            def _(act):
                act.wait_ge(gate_abs, 1)
                act.activation(a_col, bcum, ACT.Exp, scale=-1.0).then_inc(gate_exp, 1)
                act.wait_ge(gate_exp, 1)
                act.activation(g_col, a_col, ACT.Ln, bias=g.ones[:, 0:1]).then_inc(gate_ln, 1)
                act.wait_ge(gd, 6)
                act.activation(ai_row, mx_row, ACT.Exp, scale=-1.0, bias=m_col[:, 1:2]).then_inc(ga, 1)
                act.activation(g_row, a_row, ACT.Exp, bias=m_col[:, 2:3]).then_inc(ga, 1)
                act.wait_ge(gd, 7)
                act.activation(em_col, em_col, ACT.Exp, scale=-1.0).then_inc(ga, 1)
                with act.Fori(0, 4) as i:
                    for par in range(2):
                        act.wait_ge(conv_out, i * 2 + par + 1)
                        act.activation(tb[:, par, :], yb[:, par, :], ACT.Tanh).then_inc(tanh_done, 1)
                act.wait_ge(tabs_ready, 1)
                act.sem_inc(w_ready, 4)
                act.sem_inc(kg_ready, 2)

                def body(it, step, tiles):
                    for par in range(2):
                        for d in range(2):
                            b = 2 * par + d
                            u = it * 4 + b
                            act.wait_ge(staged, u * 5 + 25)
                            act.wait_ge(sw_ready, u + 1)
                            for h in range(BH):
                                w = act.activation(wt[:, d, h, :], tm[:, b, h, :], ACT.Exp, bias=cur[:, b, 0, h:h + 1])
                            w.then_inc(w_ready, 1)
                        for d in range(2):
                            b = 2 * par + d
                            u = it * 4 + b
                            act.wait_ge(k_done, u + 1)
                            act.wait_ge(c_done, u + 3)
                            for h in range(BH):
                                w = act.activation(kg[:, d, h, :], ps_k[:, d, h * P:(h + 1) * P], ACT.Copy, scale=cur[:, b, 1, h:h + 1])
                            w.then_inc(kg_ready, 1)

                turns(act, body)

            @block.vector
            def _(dve):
                def own():
                    dve.wait_ge(*c.now())

                dve.tensor_scalar(halfw[:, :], g.cols[:, COL_CW:COL_CW + 32], 0.5, None, ALU.mult).then_inc(*c.up())
                dve.memset(tab[:, :, :], 0.0).then_inc(*c.up())
                dve.memset(L.hb[:, :, :], 0.0).then_inc(*c.up())
                dve.memset(C[:, :, :, :], 0.0).then_inc(*c.up())
                dve.memset(vv[:, :, :, P:P + 4], 1.0).then_inc(*c.up())
                dve.memset(m_row[:, :, :], 0.0).then_inc(*c.up())
                own()
                for dst, at in ((ig, 0), (dec, 4)):
                    v = [dst[:, d * NC:d * NC + 40].rearrange("p (s h) -> p s h", h=BH) for d in range(2)]
                    dve.tensor_copy(v[0], L.gates[:, :, at:at + 4]).then_inc(*c.up())
                    dve.tensor_copy(v[1][:, 0:2, :], L.gates[:, 1::-1, at + 8:at + 12]).then_inc(*c.up())
                    dve.tensor_copy(v[1][:, 2:10, :], L.gates[:, 9:1:-1, at + 8:at + 12]).then_inc(*c.up())
                own()
                dve.scalar_tensor_tensor(out=bcum, in0=dec, scalar=-1.0, in1=dec, op0=ALU.mult, op1=ALU.max).then_inc(gate_abs, 1)
                dve.wait_ge(gate_ln, 1)
                dve.scalar_tensor_tensor(out=lf, in0=dec, scalar=0.0, in1=g_col, op0=ALU.min, op1=ALU.subtract).then_inc(lf_ready, 1)
                dve.wait_ge(gp, 1)
                dve.tensor_copy(bcum[:, 0:NC], ps_s[:, 0, 0:NC]).then_inc(*c.up())
                dve.tensor_copy(bcum[:, NC:2 * NC], ps_s[:, 1, 0:NC]).then_inc(*c.up())
                dve.tensor_copy(m_row[0:1, 0, :], ps_k[0:1, 0, 0:P]).then_inc(*c.up())
                own()
                dve.tensor_tensor(a_col, ig, bcum, ALU.subtract).then_inc(gd, 1)
                dve.wait_ge(gp, 2)
                dve.tensor_copy(a_row, ps_k[:, 1, 0:P]).then_inc(*c.up())
                dve.tensor_reduce(m_col[:, 0:1], ps_k[:, 1, 0:P], AX.X, ALU.max).then_inc(gd, 1)
                dve.wait_ge(gp, 3)
                dve.tensor_copy(m_row[0:1, 1, :], ps_n[0:1, 0, 0:P]).then_inc(*c.up())
                last, top, m, tmp = (m_row[0:1, n, :].rearrange("o (d r) -> o d r", d=2) for n in range(4))
                for st in range(9):
                    a, b = slice(st * 4, st * 4 + 4), slice(st * 4 + 4, st * 4 + 8)
                    own()
                    dve.tensor_tensor(tmp[:, :, a], m[:, :, a], top[:, :, a], ALU.max).then_inc(*c.up())
                    own()
                    dve.tensor_tensor(m[:, :, b], tmp[:, :, a], last[:, :, a], ALU.add).then_inc(*c.up())
                own()
                dve.sem_inc(gd, 1)
                dve.wait_ge(gp, 4)
                dve.tensor_copy(m_col[:, 1:2], ps_n[:, 1, 0:1]).then_inc(*c.up())
                own()
                dve.tensor_tensor_scan(mx_row[0:NC, :], a_row[0:NC, :], a_row[0:NC, :], m_col[0:NC, 1:2], ALU.max, ALU.max).then_inc(gd, 1)
                dve.tensor_tensor_scan(mx_row[NC:P, ::-1], a_row[NC:P, ::-1], a_row[NC:P, ::-1], m_col[NC:P, 1:2], ALU.max, ALU.max).then_inc(gd, 1)
                dve.wait_ge(gd, 5)
                dve.tensor_scalar(m_col[0:NC, 2:3], mx_row[0:NC, P - 1:P], -1.0, None, ALU.mult).then_inc(*c.up())
                dve.tensor_scalar(m_col[NC:P, 2:3], mx_row[NC:P, 0:1], -1.0, None, ALU.mult).then_inc(*c.up())
                own()
                dve.sem_inc(gd, 1)
                dve.wait_ge(gp, 5)
                dve.tensor_tensor(em_col, ps_c[:, 0, 0:P], bcum, ALU.add).then_inc(gd, 1)
                dve.wait_ge(gp, 6)
                dve.tensor_copy(g_col, ps_c[:, 1, 0:P]).then_inc(*c.up())
                dve.tensor_copy(ai_col, ps_c[:, 1, P:2 * P]).then_inc(gd, 1)
                dve.wait_ge(gp, 7)
                dve.tensor_copy(dec[:, 0:NC], ps_s[:, 0, 0:NC]).then_inc(*c.up())
                dve.tensor_copy(dec[:, NC:P], ps_s[:, 1, NC:P]).then_inc(*c.up())
                own()
                dve.wait_ge(ga, 3)
                dve.sem_inc(tabs_ready, 1)

                def convolve(i, par):
                    cc = i * 2 + par
                    y, z = yb[:, par, :], L.zT[:, bass.ds(cc, 1), :]
                    y3 = y.unsqueeze(1)
                    own()
                    dve.tensor_scalar(y3, z, halfw[:, bass.ds(cc + 8, 1)], halfw[:, bass.ds(cc + 24, 1)], ALU.mult, ALU.add).then_inc(*c.up())
                    for a, n in ((0, CTX), (CTX, SEQ)):
                        own()
                        dve.scalar_tensor_tensor(out=y3[:, :, a + 1:a + n], in0=z[:, :, a:a + n - 1], scalar=halfw[:, bass.ds(cc, 1)],
                                                 in1=y3[:, :, a + 1:a + n], op0=ALU.mult, op1=ALU.add).then_inc(*c.up())
                    for a, n in ((0, CTX), (CTX, SEQ)):
                        own()
                        dve.scalar_tensor_tensor(out=y3[:, :, a:a + n - 1], in0=z[:, :, a + 1:a + n], scalar=halfw[:, bass.ds(cc + 16, 1)],
                                                 in1=y3[:, :, a:a + n - 1], op0=ALU.mult, op1=ALU.add).then_inc(*c.up())
                    own()
                    dve.sem_inc(conv_out, 1)

                def gate_channels(i, par):
                    z = L.zT[:, bass.ds(i * 2 + par, 1), :]
                    dve.wait_ge(tanh_done, i * 2 + par + 1)
                    dve.scalar_tensor_tensor(out=z, in0=tb[:, par, :].unsqueeze(1), scalar=1.0, in1=yb[:, par, :].unsqueeze(1),
                                             op0=ALU.add, op1=ALU.mult).then_inc(*c.up())

                with dve.Fori(0, 4) as i:
                    c.turn(i, 12)
                    convolve(i, 0)
                    convolve(i, 1)
                    gate_channels(i, 0)
                    gate_channels(i, 1)
                c.turned(4)
                own()
                dve.tensor_scalar(L.zT[:, 0:4, :], L.zT[:, 0:4, :], BD ** -0.5, None, ALU.mult).then_inc(*c.up())
                own()
                dve.sem_inc(z_ready, 1)
                dve.sem_inc(sw_ready, 2)
                dve.sem_inc(n_done, 2)
                dve.sem_inc(h_out, 1)
                dve.sem_inc(c_out, 4)

                def body(it, step, tiles):
                    if not isinstance(it, int):
                        c.turn(it - 1, 4 * 5)
                    for par in range(2):
                        for d in range(2):
                            u = it * 4 + 2 * par + d
                            dve.wait_ge(s_done, u + 1)
                            dve.wait_ge(w_ready, u + 5)
                            dve.wait_ge(n_done, u + 1)
                            dve.tensor_tensor(sw[:, d, :, :], ps_s[:, d, :].rearrange("p (h t) -> p h t", t=P), wt[:, d, :, :], ALU.mult).then_inc(sw_ready, 1)
                        for d in range(2):
                            b = 2 * par + d
                            u = it * 4 + b
                            tile = tiles(par)[d]
                            dve.wait_ge(n_done, u + 3)
                            dve.tensor_copy(dn[:, 0, 0:3], ps_n[:, 0, 0:387].rearrange("p (h e) -> p h e", e=129)[:, :, 128]).then_inc(*c.up())
                            dve.tensor_copy(dn[:, 0, 3:4], ps_n[:, 1, 128:129]).then_inc(*c.up())
                            own()
                            dve.scalar_tensor_tensor(out=dn[:, 1, :], in0=dn[:, 0, :], scalar=-1.0, in1=dn[:, 0, :], op0=ALU.mult, op1=ALU.max).then_inc(*c.up())
                            own()
                            dve.tensor_tensor(dn[:, 2, :], dn[:, 1, :], cur[:, b, 2, :], ALU.max).then_inc(*c.up())
                            own()
                            dve.reciprocal(dn[:, 1, :], dn[:, 2, :]).then_inc(*c.up())
                            own()
                            for h in range(BH):
                                o = L.hb[:, bass.ds(tile, 1), h * P:(h + 1) * P]
                                w = dve.scalar_tensor_tensor(out=o, in0=place(ps_n, h)[:, 0:P].unsqueeze(1), scalar=dn[:, 1, h:h + 1], in1=o, op0=ALU.mult, op1=ALU.add)
                            w.then_inc(h_out, 1)
                            dve.wait_ge(c_done, u + 5)
                            for h in range(BH):
                                w = dve.scalar_tensor_tensor(out=C[:, d, h, 0:129], in0=C[:, d, h, 0:129], scalar=cur[:, b, 3, h:h + 1],
                                                             in1=place(ps_c, h), op0=ALU.mult, op1=ALU.add)
                            w.then_inc(c_out, 1)
                    if not isinstance(it, int):
                        c.turned(NTL // 2)

                turns(dve, body)



class Job:

    def __init__(self, parts, v, cols, out, t2):
        self.parts, self.v, self.cols, self.out, self.t2 = parts, v, cols, out, t2


def attend(nc, g, tag, sections, neg_lam=None):

    def s(name):
        return nc.alloc_semaphore(tag + name)

    with nc.cleanup_on_exit():
        pe4 = nc.alloc_sbuf_tensor(tag + "exps", [P, 4, T], F32)
        pT = nc.alloc_sbuf_tensor(tag + "pT", [P, 2, T], F32)
        st = nc.alloc_sbuf_tensor(tag + "stats", [P, 4, 8], F32)
        ps_s = nc.alloc_psum_tensor(tag + "ps_s", [P, 2, 3 * 512], F32)
        ps_t = nc.alloc_psum_tensor(tag + "ps_t", [P, 512], F32)
        ps_o = nc.alloc_psum_tensor(tag + "ps_o", [P, 512], F32)
        c = Count(nc, tag + "dve_step")
        staged, s_done, m_ready, e_done = s("staged"), s("s_done"), s("m_ready"), s("e_done")
        mixed, t_done, t_out, o_done, o_out = s("mixed"), s("t_done"), s("t_out"), s("o_done"), s("o_out")

        def walk(eng, visit, own=None, per_job=0):
            J = Pn = G = Q = 0
            for sec in sections:
                nj, npart, ng = len(sec.jobs), sum(len(j.parts) for j in sec.jobs), len(sec.jobs) * len(sec.groups)
                if sec.turns == 1:
                    visit(sec, 0, J, Pn, G, Q)
                else:
                    with eng.Fori(0, sec.turns) as i:
                        if own:
                            own.turn(i, per_job * nj + (npart - nj) * 4)
                        visit(sec, i, i * nj + J, i * npart + Pn, i * ng + G, i + Q)
                    if own:
                        own.turned(sec.turns)
                J, Pn, G, Q = J + sec.turns * nj, Pn + sec.turns * npart, G + sec.turns * ng, Q + sec.turns

        with nc.Block() as block:

            @block.gpsimd
            def _(pool):
                def visit(sec, it, J, Pn, G, Q):
                    pool.wait_ge(s_done, Pn + 1)
                    for dst, src in sec.stage:
                        pool.tensor_copy(dst, src(it)).then_inc(staged, 1)

                walk(pool, visit)

            @block.tensor
            def _(pe):
                pe.sem_inc(s_done, 1)

                def visit(sec, it, J, Pn, G, Q):
                    jobs, groups = sec.jobs, sec.groups
                    first = [sum(len(j.parts) for j in jobs[:n]) for n in range(len(jobs) + 1)]
                    keys = sec.ntiles * P
                    pe.wait_ge(staged, sec.staged_before + it * len(sec.stage) + len(sec.stage))

                    def scores(n, part):
                        q, k = jobs[n].parts[part]
                        p = first[n] + part
                        pe.wait_ge(e_done, Pn + p + 1)
                        for a in range(0, keys, 512):
                            b = min(a + 512, keys)
                            mm = pe.matmul(ps_s[:, p % 2, a:b], q, k[:, a:b], start=True, stop=True)
                        mm.then_inc(s_done, 1)

                    def turn(n, gi):
                        p = first[n]
                        if gi == 0:
                            if len(jobs[n].parts) == 1:
                                pe.wait_ge(e_done, Pn + p + 3)
                            else:
                                pe.wait_ge(mixed, J + n + 1)
                        pe.wait_ge(t_out, G + n * len(groups) + gi + 1)
                        for m, kt in enumerate(groups[gi]):
                            mm = pe.transpose(ps_t[:, m * P:(m + 1) * P], pe4[:, p % 4, kt * P:(kt + 1) * P], g.ident)
                        mm.then_inc(t_done, 1)

                    def values(n, gi):
                        if gi == 0:
                            pe.wait_ge(o_out, J + n + 1)
                        pe.wait_ge(t_out, G + n * len(groups) + gi + 2)
                        for kt in groups[gi]:
                            mm = pe.matmul(ps_o[:, 0:P], pT[:, n % 2, kt * P:(kt + 1) * P], jobs[n].v[:, kt, :],
                                           start=kt == 0, stop=kt == sec.ntiles - 1)
                        if gi == len(groups) - 1:
                            mm.then_inc(o_done, 1)

                    for part in range(len(jobs[0].parts)):
                        scores(0, part)
                    for n in range(len(jobs)):
                        more = len(jobs[n + 1].parts) if n + 1 < len(jobs) else 0
                        if more:
                            scores(n + 1, 0)
                        if n and more == 2:
                            values(n - 1, 0)
                            scores(n + 1, 1)
                        elif more == 2:
                            scores(n + 1, 1)
                        for gi in range(len(groups)):
                            turn(n, gi)
                            if n and not (more == 2 and gi == 0):
                                values(n - 1, gi)
                    for gi in range(len(groups)):
                        values(len(jobs) - 1, gi)

                walk(pe, visit)

            @block.scalar
            def _(act):
                act.sem_inc(e_done, 2)

                def visit(sec, it, J, Pn, G, Q):
                    jobs, groups = sec.jobs, sec.groups
                    first = [sum(len(j.parts) for j in jobs[:n]) for n in range(len(jobs) + 1)]
                    keys = sec.ntiles * P

                    def exps(n):
                        for part in range(len(jobs[n].parts)):
                            p = first[n] + part
                            act.wait_ge(m_ready, Pn + p + 1)
                            if len(jobs[n].parts) == 1:
                                act.wait_ge(o_done, J + n + 1)
                            elif n < 2:
                                act.wait_ge(o_out, J + 1)
                            else:
                                act.wait_ge(t_done, G + (n - 1) * len(groups))
                            act.activation(pe4[:, p % 4, 0:keys], ps_s[:, p % 2, 0:keys], ACT.Exp, scale=sec.scale,
                                           bias=st[:, p % 4, 1:2], accum_out=st[:, p % 4, 2:3]).then_inc(e_done, 1)

                    exps(0)
                    for n in range(len(jobs)):
                        if n + 1 < len(jobs):
                            exps(n + 1)
                        act.wait_ge(t_done, G + n * len(groups) + 1)
                        act.wait_ge(o_done, J + n + 3)
                        w = len(groups[0]) * P
                        act.copy(pT[:, n % 2, 0:w], ps_t[:, 0:w]).then_inc(t_out, 1)

                walk(act, visit)

            @block.vector
            def _(dve):
                dve.sem_inc(o_done, 4)
                dve.sem_inc(t_out, 1)
                dve.sem_inc(o_out, 1)

                def own():
                    dve.wait_ge(*c.now())

                def visit(sec, it, J, Pn, G, Q):
                    jobs, groups = sec.jobs, sec.groups
                    first = [sum(len(j.parts) for j in jobs[:n]) for n in range(len(jobs) + 1)]
                    keys = sec.ntiles * P
                    if len(jobs[0].parts) == 1:
                        dve.sem_inc(mixed, len(jobs))

                    def maxima(n):
                        for part in range(len(jobs[n].parts)):
                            p = first[n] + part
                            dve.wait_ge(s_done, Pn + p + 2)
                            dve.tensor_reduce(st[:, p % 4, 0:1], ps_s[:, p % 2, 0:keys], AX.X, ALU.max).then_inc(*c.up())
                            own()
                            dve.tensor_scalar(st[:, p % 4, 1:2], st[:, p % 4, 0:1], -sec.scale, None, ALU.mult).then_inc(m_ready, 1)

                    def mix(n):
                        a, b = first[n] % 4, (first[n] + 1) % 4
                        dve.wait_ge(e_done, Pn + first[n] + 4)
                        dve.reciprocal(st[:, a, 3:4], st[:, a, 2:3]).then_inc(*c.up())
                        dve.reciprocal(st[:, b, 3:4], st[:, b, 2:3]).then_inc(*c.up())
                        own()
                        dve.tensor_scalar(st[:, b, 4:5], st[:, b, 3:4], neg_lam, None, ALU.mult).then_inc(*c.up())
                        own()
                        dve.tensor_scalar(pe4[:, b, 0:keys], pe4[:, b, 0:keys], st[:, b, 4:5], None, ALU.mult).then_inc(*c.up())
                        own()
                        dve.scalar_tensor_tensor(out=pe4[:, a, 0:keys], in0=pe4[:, a, 0:keys], scalar=st[:, a, 3:4],
                                                 in1=pe4[:, b, 0:keys], op0=ALU.mult, op1=ALU.add).then_inc(mixed, 1)

                    def weights_out(n):
                        for gi in range(1, len(groups)):
                            dve.wait_ge(t_done, G + n * len(groups) + gi + 1)
                            dve.wait_ge(o_done, J + n + 3)
                            a, w = groups[gi][0] * P, len(groups[gi]) * P
                            dve.tensor_copy(pT[:, n % 2, a:a + w], ps_t[:, 0:w]).then_inc(t_out, 1)

                    def result(n):
                        a = first[n] % 4
                        dve.wait_ge(o_done, J + n + 5)
                        if len(jobs[n].parts) == 1:
                            dve.reciprocal(st[:, a, 3:4], st[:, a, 2:3]).then_inc(*c.up())
                            own()
                            dve.tensor_scalar(jobs[n].out(it), ps_o[:, jobs[n].cols].unsqueeze(1), st[:, a, 3:4], None, ALU.mult).then_inc(o_out, 1)
                        else:
                            dve.tensor_copy(jobs[n].out(it), ps_o[:, jobs[n].cols].unsqueeze(1)).then_inc(o_out, 1)

                    maxima(0)
                    for n in range(len(jobs)):
                        if len(jobs[n].parts) == 2:
                            mix(n)
                        if n + 1 < len(jobs):
                            maxima(n + 1)
                        weights_out(n)
                        if n:
                            result(n - 1)
                    result(len(jobs) - 1)

                walk(dve, visit, c, 2)


class Section:
    def __init__(self, turns, ntiles, scale, jobs, stage, staged_before):
        self.turns, self.ntiles, self.scale, self.jobs, self.stage = turns, ntiles, scale, jobs, stage
        self.groups = [list(range(a, min(a + 4, ntiles))) for a in range(0, ntiles, 4)]
        self.staged_before = staged_before


def even_attend(nc, g, A, L):
    with nc.cleanup_on_exit():
        q = nc.alloc_sbuf_tensor("ea_q", [P, 2, 4, P], F32)

        def jobs(tile0):
            out = []
            for t2 in range(2):
                for hd in range(AH):
                    kv, rows = hd // 4, slice(64 * (hd // 4), 64 * (hd // 4) + 64)
                    out.append(Job([(q[rows, t2, hd % 4, :], L.kT[rows, :])], L.v, slice(kv * AD, kv * AD + AD),
                                   lambda it, t2=t2, hd=hd: L.cat[:, bass.ds(it * 2 + tile0 + t2, 1), hd * AD:(hd + 1) * AD], t2))
            return out

        def stage(tile0):
            return [(q[:, t2, :, :], lambda it, t2=t2: L.qT[:, :, bass.ds(it * 256 + (tile0 + t2) * P, P)]) for t2 in range(2)]

        attend(nc, g, "ea_", [Section(1, NTC, AD ** -0.5, jobs(0), stage(0), 0),
                              Section(NTL // 2, NT, AD ** -0.5, jobs(NTC), stage(NTC), 2)])


def broadcast_rows(pe, g, ps, col, done):
    for k in range(KD):
        mm = pe.matmul(ps[:, k * P:(k + 1) * P], col[:, k:k + 1].to_broadcast([P, P]), g.ident, start=True, stop=True)
    mm.then_inc(done, 1)


def mix_out(nc, g, A, layer, M, R):
    tag = f"mo{layer}_"

    def s(name):
        return nc.alloc_semaphore(tag + name)

    with nc.cleanup_on_exit():
        w = nc.alloc_sbuf_tensor(tag + "w", [P, KD, D], F32)
        wr = nc.alloc_sbuf_tensor(tag + "wr", [P, KD, P], F32)
        kinds = sorted({sec[2] for sec in M.sections})
        rows = nc.alloc_sbuf_tensor(tag + "rows", [P, 3 * len(kinds), D], F32)
        x = M.room[:, 0:2 * D].rearrange("p (h d) -> p h d", h=2)
        cr = M.room[:, 2 * D:4 * D].rearrange("p (h d) -> p h d", h=2)
        og = M.room[:, 4 * D:5 * D].rearrange("p (h d) -> p h d", h=2)
        cT = nc.alloc_sbuf_tensor(tag + "cT", [P, 2, KD, P], F32)
        f = nc.alloc_sbuf_tensor(tag + "f", [P, 2, D], F32)
        fT = cT
        S = Shared()
        S.sq = nc.alloc_sbuf_tensor(tag + "sq", [P, BW], F32)
        S.nrm = nc.alloc_sbuf_tensor(tag + "nrm", [P, BW], F32)
        S.ss = nc.alloc_sbuf_tensor(tag + "ss", [P, 16], F32)
        S.r = nc.alloc_sbuf_tensor(tag + "r", [P, 16], F32)
        S.s1 = nc.alloc_sbuf_tensor(tag + "s1", [P, 16], F32)
        S.s2 = nc.alloc_sbuf_tensor(tag + "s2", [P, 16], F32)
        xs = nc.alloc_sbuf_tensor(tag + "xs", [P, 2, 8], F32)
        lg = nc.alloc_sbuf_tensor(tag + "lg", [P, 2, NE], F32)
        ps_c = nc.alloc_psum_tensor(tag + "ps_c", [P, 2, 512], F32)
        ps_o = nc.alloc_psum_tensor(tag + "ps_o", [P, D], F32)
        ps_f = nc.alloc_psum_tensor(tag + "ps_f", [P, 2, 512], F32)
        ps_r = nc.alloc_psum_tensor(tag + "ps_r", [P, 512], F32)
        ps_q = nc.alloc_psum_tensor(tag + "ps_q", [P, 512], F32)
        c = Count(nc, tag + "dve_step")
        w_in, r_in, wr_clear, row_mm, row_out = s("w_in"), s("r_in"), s("wr_clear"), s("row_mm"), s("row_out")
        x_in, og_in = [s("x_in0"), s("x_in1")], [s("og_in0"), s("og_in1")]
        x_st, f_st = [s("x_st0"), s("x_st1")], [s("f_st0"), s("f_st1")]
        copied, prepared, c_done, c_act, c_dve = s("copied"), s("prepared"), s("c_done"), s("c_act"), s("c_dve")
        o_done, x_new, x_sq, f_ready = s("o_done"), s("x_new"), s("x_sq"), s("f_ready")
        f_done, f_act, f_dve, r_done, r_out = s("f_done"), s("f_act"), s("f_dve"), s("r_done"), s("r_out")

        def turns(eng, body, own=None, per=0):
            n = 0
            for count, tile0, kind in M.sections:
                if count == 1:
                    body(n, lambda h: tile0 + h, kind)
                else:
                    with eng.Fori(0, count) as i:
                        if own:
                            own.turn(i, per)
                        body(i + n, lambda h: i * 2 + (tile0 + h), kind)
                    if own:
                        own.turned(count)
                n += count
            return n

        with nc.Block() as block:

            @block.sync
            def _(sp):
                for k in range(KD):
                    sp.dma_start(w[:, k, :], M.w_out[k * P:(k + 1) * P, :]).then_inc(w_in, 16)
                sp.wait_ge(wr_clear, 1)
                sp.dma_start(wr[:, :, 0:NE], A["w_router"].rearrange("(k p) e -> p k e", p=P)).then_inc(r_in, 16)

                def body(it, tile, kind):
                    for h in range(2):
                        sp.wait_ge(x_st[h], it * 16 + 16)
                        sp.wait_ge(f_st[h], it * 16 + 16)
                        sp.dma_start(x[:, h, :], M.x_rows(tile(h))).then_inc(x_in[h], 16)
                        if M.gate_rows:
                            sp.dma_start(og[:, h, :], M.gate_rows(tile(h))).then_inc(og_in[h], 16)

                turns(sp, body)

            @block.gpsimd
            def _(pool):
                def body(it, tile, kind):
                    for h in range(2):
                        pool.wait_ge(c_done, it * 4 + 2 * h + 2)
                        pool.tensor_copy(cr[:, h, M.copy_to:M.copy_to + 512].unsqueeze(1), M.copy_from(tile(h))).then_inc(copied, 1)

                turns(pool, body)

            @block.tensor
            def _(pe):
                n = 0
                for kind in kinds:
                    for col in (g.mod[:, layer * 48 + V_G1 * KD:layer * 48 + V_G1 * KD + KD, kind],
                                g.gain[:, layer, 1, :, kind],
                                g.mod[:, layer * 48 + V_SH2 * KD:layer * 48 + V_SH2 * KD + KD, kind]):
                        if n > 1:
                            pe.wait_ge(row_out, n - 1)
                        broadcast_rows(pe, g, (ps_o, ps_c[:, :, :].rearrange("p a n -> p (a n)"))[n % 2], col, row_mm)
                        n += 1
                pe.wait_ge(row_out, n)
                pe.wait_ge(w_in, 16 * KD)
                pe.wait_ge(r_in, 16)
                pe.sem_inc(c_done, 4)
                pe.sem_inc(r_done, 1)
                pe.sem_inc(f_done, 1)

                def body(it, tile, kind):
                    def cat(h):
                        pe.wait_ge(copied, it * 2 + h + 1)
                        pe.wait_ge(prepared, it * 2 + h + 1)
                        pe.wait_ge(c_act, it * 2 + h + 1)
                        pe.wait_ge(c_dve, it * 2 + h + 1)
                        for half in range(2):
                            for k in range(4 * half, 4 * half + 4):
                                mm = pe.transpose(ps_c[:, half, (k % 4) * P:(k % 4) * P + P], cr[:, h, k * P:(k + 1) * P], g.ident)
                            mm.then_inc(c_done, 1)
                        pe.wait_ge(c_act, it * 2 + h + 2)
                        pe.wait_ge(c_dve, it * 2 + h + 2)
                        pe.wait_ge(x_new, it * 2 + h + 2)
                        for half in range(2):
                            for k in range(KD):
                                mm = pe.matmul(ps_o[:, half * 512:(half + 1) * 512], cT[:, h, k, :], w[:, k, half * 512:(half + 1) * 512],
                                               start=k == 0, stop=k == KD - 1)
                        mm.then_inc(o_done, 1)

                    def router(h):
                        pe.wait_ge(f_ready, it * 2 + h + 1)
                        pe.wait_ge(f_act, it * 2 + h + 1)
                        pe.wait_ge(f_dve, it * 2 + h + 1)
                        for half in range(2):
                            for k in range(4 * half, 4 * half + 4):
                                mm = pe.transpose(ps_f[:, half, (k % 4) * P:(k % 4) * P + P], f[:, h, k * P:(k + 1) * P], g.ident)
                            mm.then_inc(f_done, 1)
                        pe.wait_ge(f_act, it * 2 + h + 2)
                        pe.wait_ge(f_dve, it * 2 + h + 2)
                        pe.wait_ge(r_out, it * 2 + h + 1)
                        for k in range(KD):
                            mm = pe.matmul(ps_r[:, 0:P], fT[:, h, k, :], wr[:, k, :], start=k == 0, stop=k == KD - 1)
                        mm.then_inc(r_done, 1)

                    cat(0)
                    cat(1)
                    router(0)
                    router(1)

                turns(pe, body)

            @block.scalar
            def _(act):
                act.sem_inc(c_act, 1)
                act.sem_inc(f_act, 1)
                act.sem_inc(r_out, 1)
                for h in range(2):
                    act.sem_inc(x_st[h], 16)
                    act.sem_inc(f_st[h], 16)

                def body(it, tile, kind):
                    for h in range(2):
                        act.wait_ge(c_done, it * 4 + 2 * h + 5)
                        act.wait_ge(r_done, it * 2 + 1)
                        act.copy(cT[:, h, 0:4, :], ps_c[:, 0, :].rearrange("p (k t) -> p k t", t=P)).then_inc(c_act, 1)
                    for h in range(2):
                        act.wait_ge(x_new, it * 2 + h + 3)
                        act.activation(f[:, h, :], x[:, h, :], ACT.Square, accum_out=xs[:, h, 0:1]).then_inc(x_sq, 1)
                        act.dma_start(M.x_rows(tile(h)), x[:, h, :]).then_inc(x_st[h], 16)
                    for h in range(2):
                        act.wait_ge(f_ready, it * 2 + h + 1)
                        act.dma_start(R.f_dram[bass.ds(tile(h) * P, P), :], f[:, h, :]).then_inc(f_st[h], 16)
                    for h in range(2):
                        act.wait_ge(f_done, it * 4 + 2 * h + 2)
                        act.wait_ge(o_done, it * 2 + h + 1)
                        act.copy(fT[:, h, 0:4, :], ps_f[:, 0, :].rearrange("p (k t) -> p k t", t=P)).then_inc(f_act, 1)
                        act.wait_ge(r_done, it * 2 + h + 2)
                        act.activation(lg[:, h, :], ps_r[:, 0:NE], ACT.Tanh, scale=0.5).then_inc(r_out, 1)

                n = turns(act, body)
                for h in range(2):
                    act.wait_ge(x_st[h], n * 16 + 16)
                    act.wait_ge(f_st[h], n * 16 + 16)

            @block.vector
            def _(dve):
                def own():
                    dve.wait_ge(*c.now())

                dve.memset(wr[:, :, :], 0.0).then_inc(wr_clear, 1)
                for n in range(3 * len(kinds)):
                    dve.wait_ge(row_mm, n + 1)
                    dve.tensor_copy(rows[:, n, :], (ps_o[:, :], ps_c[:, :, :].rearrange("p a n -> p (a n)"))[n % 2]).then_inc(row_out, 1)
                dve.sem_inc(c_dve, 1)
                dve.sem_inc(f_dve, 1)
                dve.sem_inc(x_new, 2)
                dve.sem_inc(*c.up())

                def body(it, tile, kind):
                    base = 3 * kinds.index(kind)
                    for h in range(2):
                        dve.wait_ge(c_done, it * 4 + 2 * h + 2)
                        M.prep(dve, c, S, it, h, tile(h), cr[:, h, :], og[:, h, :], og_in[h])
                        own()
                        dve.sem_inc(prepared, 1)
                    for h in range(2):
                        dve.wait_ge(c_done, it * 4 + 2 * h + 6)
                        dve.wait_ge(r_done, it * 2 + 1)
                        dve.tensor_copy(cT[:, h, 4:8, :], ps_c[:, 1, :].rearrange("p (k t) -> p k t", t=P)).then_inc(c_dve, 1)
                    for h in range(2):
                        dve.wait_ge(o_done, it * 2 + h + 1)
                        dve.wait_ge(x_in[h], it * 16 + 16)
                        dve.wait_ge(f_st[h], it * 16 + 16)
                        dve.wait_ge(f_done, it * 4 + 1)
                        dve.tensor_tensor(f[:, h, :], ps_o[:, :], rows[:, base, :], ALU.mult).then_inc(*c.up())
                        own()
                        dve.tensor_tensor(x[:, h, :], x[:, h, :], f[:, h, :], ALU.add).then_inc(x_new, 1)
                    for h in range(2):
                        dve.wait_ge(x_sq, it * 2 + h + 1)
                        dve.tensor_scalar(xs[:, h, 1:2], xs[:, h, 0:1], 1.0 / D, EPS, ALU.mult, ALU.add).then_inc(*c.up())
                        rstd(dve, c, xs[:, h, 2:3], xs[:, h, 1:2], xs[:, h, 3:4], xs[:, h, 4:5])
                        own()
                        dve.scalar_tensor_tensor(out=f[:, h, :], in0=x[:, h, :], scalar=xs[:, h, 2:3], in1=rows[:, base + 1, :],
                                                 op0=ALU.mult, op1=ALU.mult).then_inc(*c.up())
                        own()
                        dve.tensor_tensor(f[:, h, :], f[:, h, :], rows[:, base + 2, :], ALU.add).then_inc(f_ready, 1)
                    for h in range(2):
                        dve.wait_ge(f_done, it * 4 + 2 * h + 3)
                        dve.wait_ge(o_done, it * 2 + h + 1)
                        dve.tensor_copy(fT[:, h, 4:8, :], ps_f[:, 1, :].rearrange("p (k t) -> p k t", t=P)).then_inc(f_dve, 1)
                        dve.wait_ge(r_out, it * 2 + h + 2)
                        dve.tensor_scalar(R.scores[:, bass.ds(tile(h), 1), :], lg[:, h, :].unsqueeze(1), 0.5, 0.5, ALU.mult, ALU.add).then_inc(*c.up())

                turns(dve, body, c, 2 * (M.prep_n + 1 + 1 + RSTD_N + 1 + 1))


def even_mix(g, A, L, h_dram=None):
    M = Shared()
    M.sections = [(1, 0, 1), (NTL // 2, NTC, 0)]
    M.room = L.zT[:, 4:8, :].rearrange("p a t -> p (a t)")
    M.w_out = A["e_w_out"][0]
    M.x_rows = lambda t: g.x_dram[bass.ds(t * P, P), :]
    M.gate_rows = lambda t: g.vo_dram[bass.ds(t * P, P), BW:2 * BW]
    M.copy_to, M.copy_from = 0, lambda t: L.cat[:, bass.ds(t, 1), :]
    M.prep_n = HEAD_NORM_N + 2

    def prep(dve, c, S, it, h, tile, cr, og, og_in):
        src = L.hb[:, bass.ds(tile, 1), :].rearrange("p o n -> p (o n)")
        gain = g.bc["e_g_h"].rearrange("p (n d) -> p n d", d=BD)
        head_norm_rope(dve, c, g, S, BH, BD, gain, True, src, None)
        dve.wait_ge(og_in, it * 16 + 16)
        dve.wait_ge(*c.now())
        dve.tensor_scalar(S.sq[:, :], og, 0.5, 0.5, ALU.mult, ALU.add).then_inc(*c.up())
        dve.wait_ge(*c.now())
        dve.tensor_tensor(cr[:, AW:AW + BW], S.nrm[:, :], S.sq[:, :], ALU.mult).then_inc(*c.up())

    M.prep = prep
    return M


def odd_project(nc, g, A, L):
    QK = 2 * CW
    NH = QK // CD
    RUNS = ((0, CW), (CW, QK), (QK, QK + CW), (QK + CW, IN_ODD))

    def s(name):
        return nc.alloc_semaphore("op_" + name)

    with nc.cleanup_on_exit():
        w = nc.alloc_sbuf_tensor("op_w", [P, KD, IN_ODD], F32)
        x = nc.alloc_sbuf_tensor("op_x", [P, 2, D], F32)
        hT = nc.alloc_sbuf_tensor("op_hT", [P, 2, KD, P], F32)
        qk = nc.alloc_sbuf_tensor("op_qk", [P, QK], F32)
        S = Shared()
        S.sq, S.nrm, gains = L.spare[:, 0:QK], L.spare[:, QK:2 * QK], L.spare[:, 2 * QK:3 * QK]
        gqk = gains.rearrange("p (n d) -> p n d", d=CD)
        qkr = S.sq
        S.ra = nc.alloc_sbuf_tensor("op_ra", [P, NH, CD // 2], F32)
        S.rb = nc.alloc_sbuf_tensor("op_rb", [P, NH, CD // 2], F32)
        S.ss = nc.alloc_sbuf_tensor("op_ss", [P, 16], F32)
        S.r = nc.alloc_sbuf_tensor("op_r", [P, 16], F32)
        S.s1 = nc.alloc_sbuf_tensor("op_s1", [P, 16], F32)
        S.s2 = nc.alloc_sbuf_tensor("op_s2", [P, 16], F32)
        xs = nc.alloc_sbuf_tensor("op_xs", [P, 2, 8], F32)
        sel = nc.alloc_sbuf_tensor("op_sel", [P, PAIRS, 2, KD], F32)
        now = nc.alloc_sbuf_tensor("op_now", [P, 2, KD], F32)
        ps_ab = nc.alloc_psum_tensor("op_ps_ab", [P, 2, 2, 512], F32)
        ps_r = nc.alloc_psum_tensor("op_ps_r", [P, 4, 512], F32)
        w_in, x_sq, xh_ready, g_in = s("w_in"), s("x_sq"), s("xh_ready"), s("g_in")
        x_in = [s("x_in0"), s("x_in1")]
        t_done, h_act, h_dve = s("t_done"), s("h_act"), s("h_dve")
        r_done, r_act, r_dve = s("r_done"), s("r_act"), s("r_dve")
        qk_ready, qt_done, qt_act, qt_dve, now_ready = s("qk_ready"), s("qt_done"), s("qt_act"), s("qt_dve"), s("now_ready")
        c = Count(nc, "op_dve_step")
        with nc.Block() as block:

            @block.sync
            def _(sp):
                for k in range(KD):
                    sp.dma_start(w[:, k, :], A["o_w_in"][0, k * P:(k + 1) * P, :]).then_inc(w_in, 16)
                for name, (at, width) in GO.items():
                    src = A[name].rearrange("a b d -> a (b d)") if name == "o_lam" else A[name]
                    sp.dma_start(L.go[:, at:at + width], src.partition_broadcast(P)).then_inc(g_in, 16)
                with sp.Fori(0, PAIRS) as i:
                    for h in range(2):
                        sp.wait_ge(t_done, i * 4 + 2 * h + 2)
                        sp.dma_start(x[:, h, :], g.x_dram[bass.ds(i * 256 + h * P, P), :]).then_inc(x_in[h], 16)

            @block.tensor
            def _(pe):
                pe.sem_inc(t_done, 4)
                pe.sem_inc(qt_done, 1)

                def transposes(i, h):
                    pe.wait_ge(xh_ready, i * 2 + h + 1)
                    pe.wait_ge(qt_act, i * 2 + h + 1)
                    pe.wait_ge(qt_dve, i * 2 + h + 1)
                    for half in range(2):
                        for k in range(4 * half, 4 * half + 4):
                            mm = pe.transpose(ps_ab[:, h, half, (k % 4) * P:(k % 4) * P + P], x[:, h, k * P:(k + 1) * P], g.ident)
                        mm.then_inc(t_done, 1)

                def rows(i, h):
                    pe.wait_ge(h_act, i * 2 + h + 1)
                    pe.wait_ge(h_dve, i * 2 + h + 1)
                    for n, (a, b) in enumerate(RUNS):
                        pe.wait_ge((r_act, r_dve)[n % 2], i * 4 + 2 * h + 1 + n // 2)
                        for k in range(KD):
                            mm = pe.matmul(ps_r[:, n, 0:b - a], hT[:, h, k, :], w[:, k, a:b], start=k == 0, stop=k == KD - 1)
                        mm.then_inc(r_done, 1)

                def turn_qk(i, h):
                    pe.wait_ge(qk_ready, i * 2 + h + 2)
                    for half in range(2):
                        for j in range(4):
                            mm = pe.transpose(ps_ab[:, h, half, j * P:(j + 1) * P], qkr[:, half * CW + j * P:half * CW + (j + 1) * P], g.ident)
                    mm.then_inc(qt_done, 1)

                pe.wait_ge(w_in, 16 * KD)
                with pe.Fori(0, PAIRS) as i:
                    transposes(i, 0)
                    transposes(i, 1)
                    rows(i, 0)
                    rows(i, 1)
                    turn_qk(i, 0)
                    turn_qk(i, 1)

            @block.scalar
            def _(act):
                act.sem_inc(qt_act, 2)
                act.sem_inc(r_act, 2)
                act.sem_inc(qk_ready, 1)

                def squares(i, h):
                    act.wait_ge(x_in[h], i * 16 + 16)
                    act.wait_ge(qt_act, i * 2 + h + 1)
                    act.wait_ge(qt_dve, i * 2 + h + 1)
                    act.activation(ps_ab[:, h, :, :].rearrange("p a n -> p (a n)"), x[:, h, :], ACT.Square,
                                   accum_out=xs[:, h, 0:1]).then_inc(x_sq, 1)

                def modulate(i, h):
                    act.wait_ge(t_done, i * 4 + 2 * h + 5)
                    for k in range(4):
                        m = act.activation(hT[:, h, k, :], ps_ab[:, h, 0, k * P:(k + 1) * P], ACT.Identity,
                                           scale=now[:, 0, k:k + 1], bias=now[:, 1, k:k + 1])
                    m.then_inc(h_act, 1)

                def rows_out(i, h):
                    act.wait_ge(r_done, i * 8 + 4 * h + 1)
                    act.wait_ge(qk_ready, i * 2 + h + 1)
                    act.copy(qk[:, 0:CW], ps_r[:, 0, :]).then_inc(r_act, 1)
                    act.wait_ge(r_done, i * 8 + 4 * h + 3)
                    act.copy(L.vc[:, bass.ds(i * 2 + h, 1), :], ps_r[:, 2:3, :]).then_inc(r_act, 1)

                def q_out(i, h):
                    act.wait_ge(qt_done, i * 2 + h + 2)
                    act.copy(L.qcT[:, :, bass.ds(i * 256 + h * P, P)],
                             ps_ab[:, h, 0, :].rearrange("p (a n) -> p a n", n=P)).then_inc(qt_act, 1)

                with act.Fori(0, PAIRS) as i:
                    squares(i, 0)
                    squares(i, 1)
                    act.wait_ge(now_ready, i + 1)
                    modulate(i, 0)
                    modulate(i, 1)
                    rows_out(i, 0)
                    rows_out(i, 1)
                    q_out(i, 0)
                    q_out(i, 1)

            @block.vector
            def _(dve):
                dve.sem_inc(qt_dve, 2)
                dve.sem_inc(r_dve, 2)
                dve.wait_ge(g_in, 16 * len(GO))
                dve.tensor_copy(gqk[:, 0:NH // 2, :], L.gain["o_g_qc"].unsqueeze(1).to_broadcast([P, NH // 2, CD])).then_inc(*c.up())
                dve.tensor_copy(gqk[:, NH // 2:, :], L.gain["o_g_kc"].unsqueeze(1).to_broadcast([P, NH // 2, CD])).then_inc(*c.up())
                mod_pairs(dve, c, g, 1, sel)

                def normalise(i, h):
                    dve.wait_ge(x_sq, i * 2 + h + 1)
                    dve.tensor_scalar(xs[:, h, 1:2], xs[:, h, 0:1], 1.0 / D, EPS, ALU.mult, ALU.add).then_inc(*c.up())
                    rstd(dve, c, xs[:, h, 2:3], xs[:, h, 1:2], xs[:, h, 3:4], xs[:, h, 4:5])
                    dve.wait_ge(*c.now())
                    dve.tensor_scalar(x[:, h, :], x[:, h, :], xs[:, h, 2:3], None, ALU.mult).then_inc(xh_ready, 1)

                def modulate(i, h):
                    dve.wait_ge(t_done, i * 4 + 2 * h + 6)
                    for k in range(4, 8):
                        m = dve.tensor_scalar(hT[:, h, k, :], ps_ab[:, h, 1, (k - 4) * P:(k - 3) * P],
                                              now[:, 0, k:k + 1], now[:, 1, k:k + 1], ALU.mult, ALU.add)
                    m.then_inc(h_dve, 1)

                def rows_out(i, h):
                    dve.wait_ge(r_done, i * 8 + 4 * h + 2)
                    dve.tensor_copy(qk[:, CW:QK], ps_r[:, 1, :]).then_inc(r_dve, 1)
                    dve.wait_ge(r_done, i * 8 + 4 * h + 4)
                    dve.tensor_copy(L.zl[:, bass.ds(i * 2 + h, 1), :], ps_r[:, 3:4, 0:IN_ODD - 3 * CW]).then_inc(r_dve, 1)
                    dve.wait_ge(r_act, i * 4 + 2 * h + 3)
                    dve.wait_ge(r_dve, i * 4 + 2 * h + 4)
                    dve.wait_ge(qt_done, i * 2 + h + 1)
                    head_norm_rope(dve, c, g, S, NH, CD, gqk, True, qk[:, :], None)
                    n3 = S.nrm.rearrange("p (n d) -> p n d", d=CD)
                    o3 = qkr.rearrange("p (n d) -> p n d", d=CD)
                    cos = g.rope[:, bass.ds(i * 2 + h, 1), 0:32].to_broadcast([P, NH, 32])
                    sin = g.rope[:, bass.ds(i * 2 + h, 1), 32:64].to_broadcast([P, NH, 32])
                    rope_pairs(dve, c, S, n3, o3, cos, sin)
                    dve.wait_ge(*c.now())
                    dve.sem_inc(qk_ready, 1)

                def k_out(i, h):
                    dve.wait_ge(qt_done, i * 2 + h + 2)
                    dve.tensor_copy(L.kcT[:, :, bass.ds(i * 256 + h * P, P)],
                                    ps_ab[:, h, 1, :].rearrange("p (a n) -> p a n", n=P)).then_inc(qt_dve, 1)

                with dve.Fori(0, PAIRS) as i:
                    c.turn(i, 1 + 2 * (1 + RSTD_N) + 2 * (HEAD_NORM_N + ROPE_N))
                    dve.wait_ge(x_sq, i * 2 + 1)
                    dve.wait_ge(*c.now())
                    dve.tensor_copy(now[:, :, :], sel[:, bass.ds(i, 1), :, :].rearrange("p o a k -> p (o a) k")).then_inc(*c.up())
                    dve.wait_ge(*c.now())
                    dve.sem_inc(now_ready, 1)
                    normalise(i, 0)
                    normalise(i, 1)
                    modulate(i, 0)
                    modulate(i, 1)
                    rows_out(i, 0)
                    rows_out(i, 1)
                    k_out(i, 0)
                    k_out(i, 1)
                c.turned(PAIRS)


def odd_latent(nc, g, A, L):
    NH = 2 * DH
    QW = DH * DK

    def s(name):
        return nc.alloc_semaphore("ol_" + name)

    with nc.cleanup_on_exit():
        wuq = nc.alloc_sbuf_tensor("ol_wuq", [P, DQL // P, QW], F32)
        wukv = nc.alloc_sbuf_tensor("ol_wukv", [P, DH * (DN + DV)], F32)
        zs = nc.alloc_sbuf_tensor("ol_zs", [P, 2, DQL + DKL], F32)
        zT = nc.alloc_sbuf_tensor("ol_zT", [P, 2, 3, P], F32)
        qk = nc.alloc_sbuf_tensor("ol_qk", [P, 2, NH, DK], F32)
        qkr = nc.alloc_sbuf_tensor("ol_qkr", [P, 2, NH, P], F32)
        gqk = nc.alloc_sbuf_tensor("ol_gqk", [P, 2, NH, DK], F32)
        S = Shared()
        S.sq, S.nrm = L.spare[:, 0:2 * NH * DK], L.spare[:, 2 * NH * DK:4 * NH * DK]
        S.ra = nc.alloc_sbuf_tensor("ol_ra", [P, NH, DR // 2], F32)
        S.rb = nc.alloc_sbuf_tensor("ol_rb", [P, NH, DR // 2], F32)
        S.ss, S.r, S.s1, S.s2 = (nc.alloc_sbuf_tensor("ol_" + n, [P, 2 * NT], F32) for n in ("ss", "r", "s1", "s2"))
        e12 = nc.alloc_sbuf_tensor("ol_e12", [P, 2], F32)
        ps_t = nc.alloc_psum_tensor("ol_ps_t", [P, 512], F32)
        ps_u = nc.alloc_psum_tensor("ol_ps_u", [P, 3, 512], F32)
        ps_x = nc.alloc_psum_tensor("ol_ps_x", [P, 2, 2, 512], F32)
        c = Count(nc, "ol_dve_step")
        w_in, lam_sum, lam_exp = s("w_in"), s("lam_sum"), s("lam_exp")
        zs_ready, t_done, t_out, u_done, u_act, u_dve = s("zs_ready"), s("t_done"), s("t_out"), s("u_done"), s("u_act"), s("u_dve")
        qk_ready, x_done, x_act, x_dve = s("qk_ready"), s("x_done"), s("x_act"), s("x_dve")
        with nc.Block() as block:

            @block.sync
            def _(sp):
                sp.dma_start(wuq[:, :, :], A["o_w_uq"][0].rearrange("(k p) n -> p k n", p=P)).then_inc(w_in, 16)
                sp.dma_start(wukv[:, :], A["o_w_ukv"][0]).then_inc(w_in, 16)

            @block.tensor
            def _(pe):
                pe.sem_inc(t_done, 2)
                pe.sem_inc(u_done, 2)
                pe.sem_inc(x_done, 1)
                pe.wait_ge(w_in, 32)
                with pe.Fori(0, PAIRS) as i:
                    for h in range(2):
                        pe.wait_ge(zs_ready, i * 2 + h + 1)
                        pe.wait_ge(t_out, i * 2 + h + 1)
                        for k in range(3):
                            mm = pe.transpose(ps_t[:, k * P:(k + 1) * P], zs[:, h, k * P:(k + 1) * P], g.ident)
                        mm.then_inc(t_done, 1)
                    for h in range(2):
                        pe.wait_ge(t_out, i * 2 + h + 2)
                        pe.wait_ge(u_act, i * 2 + h + 1)
                        pe.wait_ge(u_dve, i * 2 + h + 1)
                        for k in range(2):
                            pe.matmul(ps_u[:, 0, 0:QW], zT[:, h, k, :], wuq[:, k, :], start=k == 0, stop=k == 1)
                        for n in range(2):
                            mm = pe.matmul(ps_u[:, 1 + n, 0:2 * (DN + DV)], zT[:, h, 2, :], wukv[:, n * 2 * (DN + DV):(n + 1) * 2 * (DN + DV)],
                                           start=True, stop=True)
                        mm.then_inc(u_done, 1)
                    for h in range(2):
                        pe.wait_ge(qk_ready, i + 2)
                        pe.wait_ge(x_act, i * 2 + h + 1)
                        pe.wait_ge(x_dve, i * 2 + h + 1)
                        for n in range(NH):
                            mm = pe.transpose(ps_x[:, h, n // 4, (n % 4) * P:(n % 4) * P + P], qkr[:, h, n, :], g.ident)
                        mm.then_inc(x_done, 1)

            @block.scalar
            def _(act):
                act.sem_inc(x_act, 2)
                act.sem_inc(t_out, 1)
                act.sem_inc(u_act, 1)
                act.wait_ge(lam_sum, 1)
                act.activation(e12[:, :], e12[:, :], ACT.Exp).then_inc(lam_exp, 1)
                with act.Fori(0, PAIRS) as i:
                    for h in range(2):
                        act.wait_ge(t_done, i * 2 + h + 3)
                        act.wait_ge(u_done, i * 2 + h + 1)
                        act.copy(zT[:, h, :, :], ps_t[:, 0:3 * P].rearrange("p (k t) -> p k t", t=P)).then_inc(t_out, 1)
                    for h in range(2):
                        act.wait_ge(u_done, i * 2 + h + 3)
                        act.wait_ge(qk_ready, i + 1)
                        act.copy(qk[:, h, 0:DH, :], ps_u[:, 0, 0:QW].rearrange("p (n d) -> p n d", d=DK))
                        kv = ps_u[:, 1, 0:2 * (DN + DV)].rearrange("p (n d) -> p n d", d=DN + DV)
                        act.copy(qk[:, h, DH:DH + 2, 0:DN], kv[:, :, 0:DN])
                        act.copy(L.vd[:, bass.ds(i * 2 + h, 1), 0:2 * DV].rearrange("p o (n d) -> p (o n) d", d=DV), kv[:, :, DN:]).then_inc(u_act, 1)
                    for h in range(2):
                        act.wait_ge(x_done, i * 2 + h + 2)
                        act.copy(L.qdT[:, :, bass.ds(i * 256 + h * P, P)],
                                 ps_x[:, h, 0, :].rearrange("p (a n) -> p a n", n=P)).then_inc(x_act, 1)

            @block.vector
            def _(dve):
                def own():
                    dve.wait_ge(*c.now())

                dve.sem_inc(x_dve, 2)
                dve.sem_inc(u_dve, 1)
                dve.sem_inc(qk_ready, 1)
                dve.memset(qkr[:, :, :, :], 0.0).then_inc(*c.up())
                for h in range(2):
                    dve.tensor_copy(gqk[:, h, 0:DH, :], L.gain["o_g_qd"].unsqueeze(1).to_broadcast([P, DH, DK])).then_inc(*c.up())
                    dve.tensor_copy(gqk[:, h, DH:, :], L.gain["o_g_kd"].unsqueeze(1).to_broadcast([P, DH, DK])).then_inc(*c.up())
                lam = L.gain["o_lam"].rearrange("p (a b d) -> p a b d", a=2, b=2)
                prod = S.sq[:, 0:2 * CD].rearrange("p (a d) -> p a d", a=2)
                dve.tensor_tensor(prod, lam[:, :, 0, :], lam[:, :, 1, :], ALU.mult).then_inc(*c.up())
                own()
                dve.tensor_reduce(e12[:, :], prod, AX.X, ALU.add).then_inc(lam_sum, 1)
                dve.tensor_scalar(L.gain["o_g_sub"], L.gain["o_g_sub"], 1.0 - LAM_INIT, None, ALU.mult).then_inc(*c.up())
                dve.wait_ge(lam_exp, 1)
                dve.tensor_tensor(L.neg_lam[:, :], e12[:, 1:2], e12[:, 0:1], ALU.subtract).then_inc(*c.up())
                own()
                dve.tensor_scalar(L.neg_lam[:, :], L.neg_lam[:, :], LAM_INIT, None, ALU.subtract).then_inc(*c.up())
                own()
                sq = L.spare[:, 0:NT * (DQL + DKL)].rearrange("p (t n) -> p t n", t=NT)
                dve.tensor_tensor(sq, L.zl[:, :, 0:DQL + DKL], L.zl[:, :, 0:DQL + DKL], ALU.mult).then_inc(*c.up())
                parts = ((0, DQL), (DQL, DKL))
                for n, (a, width) in enumerate(parts):
                    own()
                    dve.tensor_reduce(S.ss[:, n * NT:(n + 1) * NT], sq[:, :, a:a + width], AX.X, ALU.add).then_inc(*c.up())
                    own()
                    dve.tensor_scalar(S.ss[:, n * NT:(n + 1) * NT], S.ss[:, n * NT:(n + 1) * NT], 1.0 / width, EPS, ALU.mult, ALU.add).then_inc(*c.up())
                rstd(dve, c, S.r[:, :], S.ss[:, :], S.s1[:, :], S.s2[:, :])
                own()
                for n, (a, width) in enumerate(parts):
                    part = L.zl[:, :, a:a + width]
                    dve.tensor_tensor(part, part, S.r[:, n * NT:(n + 1) * NT].unsqueeze(2).to_broadcast([P, NT, width]), ALU.mult).then_inc(*c.up())
                flat = "p t n d -> p (t n d)"
                with dve.Fori(0, PAIRS) as i:
                    c.turn(i, 4 + 6 + HEAD_NORM_N + 2 + 2 * ROPE_N)
                    for h in range(2):
                        dve.wait_ge(t_done, i * 2 + h + 1)
                        own()
                        dve.tensor_tensor(zs[:, h:h + 1, 0:DQL], L.zl[:, bass.ds(i * 2 + h, 1), 0:DQL], L.gain["o_g_cq"].unsqueeze(1), ALU.mult).then_inc(*c.up())
                        dve.tensor_tensor(zs[:, h:h + 1, DQL:], L.zl[:, bass.ds(i * 2 + h, 1), DQL:DQL + DKL], L.gain["o_g_ckv"].unsqueeze(1), ALU.mult).then_inc(*c.up())
                        own()
                        dve.sem_inc(zs_ready, 1)
                    for h in range(2):
                        dve.wait_ge(u_done, i * 2 + h + 3)
                        kv = ps_u[:, 2, 0:2 * (DN + DV)].rearrange("p (n d) -> p n d", d=DN + DV)
                        dve.tensor_copy(qk[:, h, DH + 2:NH, 0:DN], kv[:, :, 0:DN]).then_inc(*c.up())
                        dve.tensor_copy(L.vd[:, bass.ds(i * 2 + h, 1), 2 * DV:].rearrange("p o (n d) -> p (o n) d", d=DV), kv[:, :, DN:]).then_inc(*c.up())
                        dve.tensor_copy(qk[:, h, DH:NH, DN:DK], L.zl[:, bass.ds(i * 2 + h, 1), DQL + DKL:].to_broadcast([P, DH, DR])).then_inc(*c.up())
                        own()
                        dve.sem_inc(u_dve, 1)
                    dve.wait_ge(u_act, i * 2 + 3)
                    dve.wait_ge(x_done, i * 2 + 1)
                    head_norm_rope(dve, c, g, S, 2 * NH, DK, gqk[:, :, :, :].rearrange("p t n d -> p (t n) d"), True, qk[:, :, :, :].rearrange(flat), None)
                    n4 = S.nrm.rearrange("p (t n d) -> p t n d", t=2, d=DK)
                    own()
                    for h in range(2):
                        dve.tensor_copy(qkr[:, h, :, 0:DN], n4[:, h, :, 0:DN]).then_inc(*c.up())
                        cos = g.rope[:, bass.ds(i * 2 + h, 1), 64:80].to_broadcast([P, NH, 16])
                        sin = g.rope[:, bass.ds(i * 2 + h, 1), 80:96].to_broadcast([P, NH, 16])
                        rope_pairs(dve, c, S, n4[:, h, :, DN:DK], qkr[:, h, :, DN:DK], cos, sin)
                    own()
                    dve.sem_inc(qk_ready, 1)
                    for h in range(2):
                        dve.wait_ge(x_done, i * 2 + h + 2)
                        dve.tensor_copy(L.kdT[:, :, bass.ds(i * 256 + h * P, P)],
                                        ps_x[:, h, 1, :].rearrange("p (a n) -> p a n", n=P)).then_inc(x_dve, 1)
                c.turned(PAIRS)


def odd_attend(nc, g, A, L):
    with nc.cleanup_on_exit():
        q = nc.alloc_sbuf_tensor("oa_q", [P, 2, 4, P], F32)

        def out(t2, at):
            return lambda it: L.cat[:, bass.ds(it * 2 + t2, 1), at:at + P]

        mla = [Job([(q[:, t2, hd, :], L.kdT[:, hd, :])], L.vd[:, :, hd * DV:(hd + 1) * DV], slice(0, DV), out(t2, CW + hd * DV), t2)
               for t2 in range(2) for hd in range(DH)]
        diff = [Job([(q[rows, t2, hd, :], L.kcT[rows, hd, :]) for rows in (slice(0, 64), slice(64, 128))],
                    L.vc[:, :, hd * CV:(hd + 1) * CV], slice(0, CV), out(t2, hd * CV), t2)
                for t2 in range(2) for hd in range(CH)]

        def stage(qT):
            return [(q[:, t2, :, :], lambda it, t2=t2: qT[:, :, bass.ds(it * 256 + (NTC + t2) * P, P)]) for t2 in range(2)]

        attend(nc, g, "oa_", [Section(NTL // 2, NT, DK ** -0.5, mla, stage(L.qdT), 0),
                              Section(NTL // 2, NT, CD ** -0.5, diff, stage(L.qcT), NTL)], L.neg_lam[:, :])


def odd_mix(g, A, L):
    M = Shared()
    M.sections = [(NTL // 2, 0, 0)]
    M.room = L.room[:, :]
    M.w_out = A["o_w_out"][0]
    M.x_rows = lambda t: g.x_dram[bass.ds(t * P + CTX, P), :]
    M.gate_rows = None
    M.copy_to, M.copy_from = CW, lambda t: L.cat[:, bass.ds(t, 1), CW:]
    M.prep_n = HEAD_NORM_N

    def prep(dve, c, S, it, h, tile, cr, og, og_in):
        src = L.cat[:, bass.ds(tile, 1), 0:CW].rearrange("p o n -> p (o n)")
        gain = L.gain["o_g_sub"].unsqueeze(1).to_broadcast([P, CH, CV])
        head_norm_rope(dve, c, g, S, CH, CV, gain, None, src, cr[:, 0:CW])

    M.prep = prep
    return M


def route(nc, g, layer, R, nt):
    tag = f"rt{layer}_"
    n, m = nt * NE, nt * NG

    def s(name):
        return nc.alloc_semaphore(tag + name)

    with nc.cleanup_on_exit():
        def sb(name, cols, dt=F32):
            return nc.alloc_sbuf_tensor(tag + name, [P, cols], dt)

        sel, one1, one2, key, tmp = (sb(x, n) for x in ("sel", "one1", "one2", "key", "tmp"))
        m1, m2, top, best = (sb(x, m) for x in ("m1", "m2", "top", "best"))
        down, number = sb("down", PER), sb("number", NE)
        gs = sb("gs", 4 * nt)
        blocks, ends, ones_e = sb("blocks", NE), sb("ends", NE), sb("ones_e", NE)
        blk_i = sb("blk_i", NE, I32)
        place, place_i, lo, hi = sb("place", 2 * nt), sb("place_i", 2 * nt, I32), sb("lo", 2 * nt, I32), sb("hi", 2 * nt, I32)
        lo_f, hi_f = sb("lo_f", 2 * nt), sb("hi_f", 2 * nt)
        slot_i = sb("slot_i", 2 * nt, I32)
        tok = sb("tok", nt, I32)
        zero = sb("zero", MAXB, I32)
        ps_a = nc.alloc_psum_tensor(tag + "ps_a", [P, 512], F32)
        ps_b = nc.alloc_psum_tensor(tag + "ps_b", [P, 512], F32)
        c = Count(nc, tag + "dve_step")
        consts, tok_ready, assigned, counted, placed, cleared, scattered, listed = (
            s("consts"), s("tok_ready"), s("assigned"), s("counted"), s("placed"), s("cleared"), s("scattered"), s("listed"))

        def ge(ap):
            return ap[:, 0:n].rearrange("p (a e) -> p a e", e=PER)

        def te(ap):
            return ap[:, 0:n].rearrange("p (t e) -> p t e", e=NE)

        with nc.Block() as block:

            @block.gpsimd
            def _(pool):
                pool.iota(down[:, :], pattern=[[-1, PER]], base=PER, channel_multiplier=0,
                          allow_small_or_imprecise_dtypes=True).then_inc(consts, 1)
                pool.iota(number[:, :], pattern=[[1, NE]], base=0, channel_multiplier=0,
                          allow_small_or_imprecise_dtypes=True).then_inc(consts, 1)
                pool.memset(zero[:, :], 0).then_inc(consts, 1)
                pool.iota(tok[:, :], pattern=[[P, nt]], base=0, channel_multiplier=1).then_inc(tok_ready, 1)
                pool.wait_ge(tok_ready, 1)
                pool.wait_ge(cleared, 16)
                pool.wait_ge(placed, 1)
                for k in range(2 * nt):
                    pool.indirect_dma_start(out=R.list_dram, out_offset=bass.IndirectOffsetOnAxis(slot_i[:, k:k + 1].bitcast(U32), 0),
                                            in_=tok[:, k // 2:k // 2 + 1], in_offset=None).then_inc(scattered, 16)

            @block.sync
            def _(sp):
                sp.wait_ge(consts, 3)
                sp.dma_start(R.list_dram.rearrange("(p b) o -> p (b o)", p=P), zero[:, :]).then_inc(cleared, 16)
                sp.wait_ge(scattered, 16 * 2 * nt)
                sp.dma_start(R.list[:, :], R.list_dram.rearrange("(p b) o -> p (b o)", p=P)).then_inc(listed, 16)
                sp.wait_ge(listed, 16)

            @block.tensor
            def _(pe):
                pe.wait_ge(assigned, 1)
                pe.matmul(ps_a[:, 0:n], g.consts[:, 2 * P:3 * P], tmp[:, 0:n], start=True, stop=True)
                pe.matmul(ps_b[:, 0:n], g.ones, tmp[:, 0:n], start=True, stop=True).then_inc(counted, 1)

            @block.vector
            def _(dve):
                def own():
                    dve.wait_ge(*c.now())

                dve.memset(ones_e[:, :], 1.0).then_inc(*c.up())
                dve.tensor_tensor(te(sel), R.scores[:, 0:nt, :], g.bc["b_router"].unsqueeze(1).to_broadcast([P, nt, NE]), ALU.add).then_inc(*c.up())
                dve.wait_ge(consts, 3)

                def first_of(src3, top2, one3, count, groups):
                    wide = [P, groups, count]
                    own()
                    dve.tensor_reduce(top2, src3, AX.X, ALU.max).then_inc(*c.up())
                    own()
                    dve.tensor_tensor(one3, src3, top2.unsqueeze(2).to_broadcast(wide), ALU.is_equal).then_inc(*c.up())
                    own()
                    key3 = key[:, 0:groups * count].rearrange("p (a e) -> p a e", e=count)
                    dve.tensor_tensor(key3, one3, down[:, PER - count:PER].unsqueeze(1).to_broadcast(wide), ALU.mult).then_inc(*c.up())
                    own()
                    dve.tensor_reduce(best[:, 0:groups], key3, AX.X, ALU.max).then_inc(*c.up())
                    own()
                    dve.tensor_tensor(one3, key3, best[:, 0:groups].unsqueeze(2).to_broadcast(wide), ALU.is_equal).then_inc(*c.up())

                first_of(ge(sel), m1[:, 0:m], ge(one1), PER, m)
                own()
                dve.scalar_tensor_tensor(out=tmp[:, 0:n], in0=one1[:, 0:n], scalar=-BIG, in1=sel[:, 0:n], op0=ALU.mult, op1=ALU.add).then_inc(*c.up())
                first_of(ge(tmp), m2[:, 0:m], ge(one2), PER, m)
                own()
                dve.tensor_tensor(m1[:, 0:m], m1[:, 0:m], m2[:, 0:m], ALU.add).then_inc(*c.up())
                first_of(m1[:, 0:m].rearrange("p (t g) -> p t g", g=NG), gs[:, 0:nt], m2[:, 0:m].rearrange("p (t g) -> p t g", g=NG), NG, nt)
                for one in (one1, one2):
                    own()
                    dve.tensor_tensor(ge(one), ge(one), m2[:, 0:m].unsqueeze(2).to_broadcast([P, m, PER]), ALU.mult).then_inc(*c.up())
                own()
                dve.tensor_tensor(tmp[:, 0:n], one1[:, 0:n], one2[:, 0:n], ALU.add).then_inc(assigned, 1)
                for k, one in enumerate((one1, one2)):
                    own()
                    dve.tensor_tensor(te(key), te(one), R.scores[:, 0:nt, :], ALU.mult).then_inc(*c.up())
                    own()
                    dve.tensor_reduce(gs[:, k * nt:(k + 1) * nt], te(key), AX.X, ALU.add).then_inc(*c.up())
                own()
                dve.tensor_tensor(gs[:, 2 * nt:3 * nt], gs[:, 0:nt], gs[:, nt:2 * nt], ALU.add).then_inc(*c.up())
                own()
                dve.reciprocal(gs[:, 3 * nt:4 * nt], gs[:, 2 * nt:3 * nt]).then_inc(*c.up())
                own()
                for k in range(2):
                    dve.tensor_tensor(R.gate[:, 0:nt, k], gs[:, k * nt:(k + 1) * nt], gs[:, 3 * nt:4 * nt], ALU.mult).then_inc(*c.up())
                dve.wait_ge(counted, 1)
                dve.tensor_tensor(key[:, 0:n], ps_a[:, 0:n], tmp[:, 0:n], ALU.subtract).then_inc(*c.up())
                dve.memset(sel[:, 0:NE], 0.0).then_inc(*c.up())
                for t in range(1, nt):
                    own()
                    dve.tensor_tensor(sel[:, t * NE:(t + 1) * NE], sel[:, (t - 1) * NE:t * NE], ps_b[:, (t - 1) * NE:t * NE], ALU.add).then_inc(*c.up())
                own()
                dve.tensor_tensor(blocks[:, :], sel[:, n - NE:n], ps_b[:, n - NE:n], ALU.add).then_inc(*c.up())
                own()
                dve.tensor_scalar(blk_i[:, :], blocks[:, :], float(P - 1), None, ALU.add).then_inc(*c.up())
                own()
                dve.tensor_scalar(blk_i[:, :], blk_i[:, :], 7, None, ALU.logical_shift_right).then_inc(*c.up())
                own()
                dve.tensor_scalar(blocks[:, :], blk_i[:, :], 1.0, None, ALU.max).then_inc(*c.up())
                own()
                dve.tensor_tensor_scan(ends[:, :], ones_e[:, :], blocks[:, :], 0.0, ALU.mult, ALU.add).then_inc(*c.up())
                own()
                dve.tensor_tensor(ends[:, :], ends[:, :], blocks[:, :], ALU.subtract).then_inc(*c.up())
                own()
                dve.tensor_tensor(R.table[:, 0, :], ends[:, :], number[:, :], ALU.subtract).then_inc(*c.up())
                dve.tensor_scalar(R.table[:, 1, :], blocks[:, :], -1.0, None, ALU.add).then_inc(*c.up())
                dve.tensor_tensor(key[:, 0:n], key[:, 0:n], sel[:, 0:n], ALU.add).then_inc(*c.up())
                own()
                dve.scalar_tensor_tensor(out=te(key), in0=ends[:, :].unsqueeze(1).to_broadcast([P, nt, NE]), scalar=float(P), in1=te(key),
                                         op0=ALU.mult, op1=ALU.add).then_inc(*c.up())
                pl = place[:, :].rearrange("p (t k) -> p t k", k=2)
                for k, one in enumerate((one1, one2)):
                    own()
                    dve.tensor_tensor(te(one), te(one), te(key), ALU.mult).then_inc(*c.up())
                    own()
                    dve.tensor_reduce(pl[:, :, k], te(one), AX.X, ALU.add).then_inc(*c.up())
                own()
                dve.tensor_copy(R.dest[:, 0:2 * nt], place[:, :]).then_inc(*c.up())
                own()
                dve.tensor_scalar(lo[:, :], R.dest[:, 0:2 * nt], P - 1, None, ALU.bitwise_and).then_inc(*c.up())
                dve.tensor_scalar(hi[:, :], R.dest[:, 0:2 * nt], 7, None, ALU.logical_shift_right).then_inc(*c.up())
                own()
                dve.tensor_copy(lo_f[:, :], lo[:, :]).then_inc(*c.up())
                dve.tensor_copy(hi_f[:, :], hi[:, :]).then_inc(*c.up())
                own()
                dve.scalar_tensor_tensor(out=slot_i[:, :], in0=lo_f[:, :], scalar=float(MAXB), in1=hi_f[:, :], op0=ALU.mult, op1=ALU.add).then_inc(*c.up())
                own()
                dve.sem_inc(placed, 1)


def experts(nc, g, A, layer, R):
    tag = f"ex{layer}_"
    KE = DE // P

    def s(name):
        return nc.alloc_semaphore(tag + name)

    with nc.cleanup_on_exit():
        w1 = nc.alloc_sbuf_tensor(tag + "w1", [P, 2, KD, DE], F32)
        w3 = nc.alloc_sbuf_tensor(tag + "w3", [P, 2, KD, DE], F32)
        w2 = nc.alloc_sbuf_tensor(tag + "w2", [P, 2, KE, D], F32)
        idx = nc.alloc_sbuf_tensor(tag + "idx", [P, 3], I32)
        xg = nc.alloc_sbuf_tensor(tag + "xg", [P, 3, D], F32)
        xT = nc.alloc_sbuf_tensor(tag + "xT", [P, 3, KD, P], F32)
        th = nc.alloc_sbuf_tensor(tag + "th", [P, 2, P], F32)
        hT = nc.alloc_sbuf_tensor(tag + "hT", [P, 3, KE, P], F32)
        y = nc.alloc_sbuf_tensor(tag + "y", [P, 3, D], F32)
        ps_x = nc.alloc_psum_tensor(tag + "ps_x", [P, 2, 512], F32)
        ps_h = nc.alloc_psum_tensor(tag + "ps_h", [P, 4, 512], F32)
        ps_y = nc.alloc_psum_tensor(tag + "ps_y", [P, 2, 512], F32)
        w13_in, w2_in = [s("w13_in0"), s("w13_in1")], [s("w2_in0"), s("w2_in1")]
        w_used, written = s("w_used"), s("written")
        idx_done, idx_seen, gathered = s("idx_done"), s("idx_seen"), [s("gathered0"), s("gathered1"), s("gathered2")]
        t_done, x_act, x_dve, h_done, th_done, th_used, h_ready = (s("t_done"), s("x_act"), s("x_dve"), s("h_done"),
                                                                  s("th_done"), s("th_used"), s("h_ready"))
        y_done, y_act, y_dve, y_st = s("y_done"), s("y_act"), s("y_dve"), [s("y_st0"), s("y_st1"), s("y_st2")]

        def walk(eng, block_of, expert_end=None):
            with eng.Fori(0, NE // 2) as i:
                for h in range(2):
                    e = i * 2 + h
                    before = eng.value_load(R.table[0:1, 0, bass.ds(e, 1)], min_val=0, max_val=MAXB - NE)
                    more = eng.value_load(R.table[0:1, 1, bass.ds(e, 1)], min_val=0, max_val=T // P - 1)
                    first = before + e
                    block_of(i, e, h, h, first, 2, i)
                    with eng.If(more > 0):
                        with eng.Fori(0, more) as b:
                            gb = nc.s_assert_within(first + b + 1, 1, MAXB - 1, skip_runtime_bounds_check_because="the experts have MAXB blocks at most")
                            block_of(i, e, h, 2, gb, 1, before + b)
                    if expert_end:
                        expert_end(i, e, h)

        with nc.Block() as block:

            @block.sync
            def _(sp):
                with sp.Fori(0, NE // 2) as i:
                    for h in range(2):
                        sp.wait_ge(w_used, i * 2 + h + 1)
                        for dst, name in ((w1, "w1"), (w3, "w3")):
                            sp.dma_start(dst[:, h, :, :], A[name][layer, bass.ds(i * 2 + h, 1), :, :].rearrange("o (k p) n -> p (o k) n", p=P)).then_inc(w13_in[h], 16)
                        sp.dma_start(w2[:, h, :, :], A["w2"][layer, bass.ds(i * 2 + h, 1), :, :].rearrange("o (k p) n -> p (o k) n", p=P)).then_inc(w2_in[h], 16)

            @block.gpsimd
            def _(pool):
                def block_of(i, e, h, b3, gb, lag, use):
                    pool.wait_ge(t_done, gb * 2 + (2 if lag == 2 else 4))
                    pool.tensor_copy(idx[:, b3:b3 + 1], R.list[:, bass.ds(gb, 1)]).then_inc(idx_done, 1)
                    pool.wait_ge(idx_done, gb + 1)
                    pool.sem_inc(idx_seen, 1)
                    pool.indirect_dma_start(out=xg[:, b3, :], out_offset=None, in_=R.f_dram,
                                            in_offset=bass.IndirectOffsetOnAxis(idx[:, b3:b3 + 1].bitcast(U32), 0)).then_inc(gathered[b3], 16)

                walk(pool, block_of)

            @block.tensor
            def _(pe):
                pe.sem_inc(t_done, 4)
                pe.sem_inc(w_used, 2)

                def block_of(i, e, h, b3, gb, lag, use):
                    pe.wait_ge(gathered[b3], use * 16 + 16)
                    pe.wait_ge(x_act, gb + 1)
                    pe.wait_ge(x_dve, gb + 1)
                    for half in range(2):
                        for k in range(4 * half, 4 * half + 4):
                            mm = pe.transpose(ps_x[:, half, (k % 4) * P:(k % 4) * P + P], xg[:, b3, k * P:(k + 1) * P], g.ident)
                        mm.then_inc(t_done, 1)
                    if b3 < 2:
                        pe.wait_ge(w13_in[h], i * 32 + 32)
                    pe.wait_ge(x_act, gb + 2)
                    pe.wait_ge(x_dve, gb + 2)
                    for f in range(KE):
                        pe.wait_ge(h_ready, gb * 4 + f + 1)
                        for n, w in enumerate((w1, w3)):
                            for k in range(KD):
                                mm = pe.matmul(ps_h[:, f, n * P:(n + 1) * P], w[:, h, k, f * P:(f + 1) * P], xT[:, b3, k, :],
                                               start=k == 0, stop=k == KD - 1)
                        mm.then_inc(h_done, 1)
                    if b3 < 2:
                        pe.wait_ge(w2_in[h], i * 16 + 16)
                    pe.wait_ge(h_ready, gb * 4 + 8)
                    pe.wait_ge(y_act, gb + 1)
                    pe.wait_ge(y_dve, gb + 1)
                    for half in range(2):
                        for k in range(KE):
                            mm = pe.matmul(ps_y[:, half, :], hT[:, b3, k, :], w2[:, h, k, half * 512:(half + 1) * 512],
                                           start=k == 0, stop=k == KE - 1)
                        mm.then_inc(y_done, 1)

                def expert_end(i, e, h):
                    pe.matmul(ps_h[:, 0, 0:P], g.ident, g.ident, start=True, stop=True).then_inc(w_used, 1)

                walk(pe, block_of, expert_end)

            @block.scalar
            def _(act):
                act.sem_inc(x_act, 1)
                act.sem_inc(y_act, 1)

                def block_of(i, e, h, b3, gb, lag, use):
                    act.wait_ge(t_done, gb * 2 + 5)
                    act.wait_ge(y_done, gb * 2 + (2 if lag == 2 else 4))
                    act.copy(xT[:, b3, 0:4, :], ps_x[:, 0, :].rearrange("p (k t) -> p k t", t=P)).then_inc(x_act, 1)
                    for f in range(KE):
                        act.wait_ge(h_done, gb * 4 + f + 1)
                        act.wait_ge(th_used, gb * 4 + f + 1)
                        act.activation(th[:, f % 2, :], ps_h[:, f, 0:P], ACT.Tanh, scale=0.5).then_inc(th_done, 1)
                    act.wait_ge(y_done, gb * 2 + 5)
                    act.wait_ge(y_st[b3], use * 16 + 16)
                    act.copy(y[:, b3, 0:512], ps_y[:, 0, :]).then_inc(y_act, 1)
                    act.wait_ge(y_act, gb + 2)
                    act.wait_ge(y_dve, gb + 2)
                    act.dma_start(R.y_dram[bass.ds(gb * P, P), :], y[:, b3, :]).then_inc(y_st[b3], 16)

                for b in range(3):
                    act.sem_inc(y_st[b], 16)
                walk(act, block_of)
                before = act.value_load(R.table[0:1, 0, NE - 1:NE], min_val=0, max_val=MAXB - NE)
                more = act.value_load(R.table[0:1, 1, NE - 1:NE], min_val=0, max_val=T // P - 1)
                for b in range(2):
                    act.wait_ge(y_st[b], 16 + 16 * (NE // 2))
                act.wait_ge(y_st[2], (before + more) * 16 + 16)
                act.sem_inc(written, 1)

            @block.vector
            def _(dve):
                dve.sem_inc(x_dve, 1)
                dve.sem_inc(y_dve, 1)
                dve.sem_inc(th_used, 2)
                dve.sem_inc(h_ready, 4)
                dve.sem_inc(y_done, 4)

                def block_of(i, e, h, b3, gb, lag, use):
                    dve.wait_ge(t_done, gb * 2 + 6)
                    dve.wait_ge(y_done, gb * 2 + (2 if lag == 2 else 4))
                    dve.tensor_copy(xT[:, b3, 4:8, :], ps_x[:, 1, :].rearrange("p (k t) -> p k t", t=P)).then_inc(x_dve, 1)
                    for f in range(KE):
                        dve.wait_ge(th_done, gb * 4 + f + 1)
                        dve.scalar_tensor_tensor(out=hT[:, b3, f, :], in0=th[:, f % 2, :], scalar=1.0, in1=ps_h[:, f, 0:P],
                                                 op0=ALU.add, op1=ALU.mult).then_inc(th_used, 1)
                        dve.wait_ge(th_used, gb * 4 + f + 3)
                        dve.scalar_tensor_tensor(out=hT[:, b3, f, :], in0=hT[:, b3, f, :], scalar=0.5, in1=ps_h[:, f, P:2 * P],
                                                 op0=ALU.mult, op1=ALU.mult).then_inc(h_ready, 1)
                    dve.wait_ge(y_done, gb * 2 + 6)
                    dve.wait_ge(y_st[b3], use * 16 + 16)
                    dve.tensor_copy(y[:, b3, 512:1024], ps_y[:, 1, :]).then_inc(y_dve, 1)

                walk(dve, block_of)


def combine(nc, g, A, layer, M, R):
    tag = f"cb{layer}_"

    def s(name):
        return nc.alloc_semaphore(tag + name)

    with nc.cleanup_on_exit():
        kinds = sorted({sec[2] for sec in M.sections})
        rows = nc.alloc_sbuf_tensor(tag + "rows", [P, len(kinds), D], F32)
        x = nc.alloc_sbuf_tensor(tag + "x", [P, 4, D], F32)
        y = nc.alloc_sbuf_tensor(tag + "y", [P, 4, 2, D], F32)
        ps = nc.alloc_psum_tensor(tag + "ps", [P, 2, D], F32)
        row_mm, row_out, x_new = s("row_mm"), s("row_out"), s("x_new")
        x_in, x_st, y_in = ([s(f"{n}{b}") for b in range(4)] for n in ("x_in", "x_st", "y_in"))
        c = Count(nc, tag + "dve_step")
        pairs = []
        for count, tile0, kind in M.sections:
            pairs += [(tile0 + 2 * j, kind) for j in range(count)]

        with nc.Block() as block:

            @block.sync
            def _(sp):
                for n, (tile, kind) in enumerate(pairs):
                    for h in range(2):
                        b, use = 2 * (n % 2) + h, n // 2
                        if use:
                            sp.wait_ge(x_st[b], 16 * use)
                        sp.dma_start(x[:, b, :], M.x_rows(tile + h)).then_inc(x_in[b], 16)

            @block.gpsimd
            def _(pool):
                for n, (tile, kind) in enumerate(pairs):
                    for h in range(2):
                        b = 2 * (n % 2) + h
                        if n > 1:
                            pool.wait_ge(x_new, 2 * (n - 2) + h + 1)
                        for k in range(2):
                            pool.indirect_dma_start(out=y[:, b, k, :], out_offset=None, in_=R.y_dram,
                                                    in_offset=bass.IndirectOffsetOnAxis(R.dest[:, 2 * (tile + h) + k:2 * (tile + h) + k + 1].bitcast(U32), 0)).then_inc(y_in[b], 16)

            @block.tensor
            def _(pe):
                for n, kind in enumerate(kinds):
                    broadcast_rows(pe, g, ps[:, n, :], g.mod[:, layer * 48 + V_G2 * KD:layer * 48 + V_G2 * KD + KD, kind], row_mm)

            @block.scalar
            def _(act):
                for n, (tile, kind) in enumerate(pairs):
                    for h in range(2):
                        b = 2 * (n % 2) + h
                        act.wait_ge(x_new, 2 * n + h + 1)
                        act.dma_start(R.final(tile + h), x[:, b, :]).then_inc(x_st[b], 16)
                for b in range(4):
                    act.wait_ge(x_st[b], 16 * len(pairs[b // 2::2]))

            @block.vector
            def _(dve):
                def own():
                    dve.wait_ge(*c.now())

                for n in range(len(kinds)):
                    dve.wait_ge(row_mm, n + 1)
                    dve.tensor_copy(rows[:, n, :], ps[:, n, :]).then_inc(row_out, 1)
                dve.wait_ge(row_out, len(kinds))
                for n, (tile, kind) in enumerate(pairs):
                    for h in range(2):
                        b, use = 2 * (n % 2) + h, n // 2
                        y0, y1 = y[:, b, 0, :], y[:, b, 1, :]
                        dve.wait_ge(y_in[b], 32 * (use + 1))
                        dve.tensor_scalar(y0, y0, R.gate[:, tile + h, 0:1], None, ALU.mult).then_inc(*c.up())
                        own()
                        dve.scalar_tensor_tensor(out=y0, in0=y1, scalar=R.gate[:, tile + h, 1:2], in1=y0, op0=ALU.mult, op1=ALU.add).then_inc(*c.up())
                        own()
                        dve.tensor_tensor(y0, y0, rows[:, kinds.index(kind), :], ALU.mult).then_inc(*c.up())
                        own()
                        dve.wait_ge(x_in[b], 16 * (use + 1))
                        dve.tensor_tensor(x[:, b, :], x[:, b, :], y0, ALU.add).then_inc(x_new, 1)


def ffn(nc, g, A, layer, M, R, nt, upto):
    with nc.cleanup_on_exit():
        R.list = nc.alloc_sbuf_tensor(f"list{layer}", [P, MAXB], I32)
        R.table = nc.alloc_sbuf_tensor(f"table{layer}", [P, 2, NE], I32)
        R.dest = nc.alloc_sbuf_tensor(f"dest{layer}", [P, 2 * NT], I32)
        R.gate = nc.alloc_sbuf_tensor(f"gate{layer}", [P, NT, 2], F32)
        route(nc, g, layer, R, nt)
        if upto == 5:
            return
        experts(nc, g, A, layer, R)
        if upto == 6:
            return
        combine(nc, g, A, layer, M, R)


def build(nc, A, out, upto=99, only=None):
    g = Shared()
    g.x_dram = nc.dram_tensor("x_stream", (T, D), F32, kind="Internal").ap()
    g.consts = nc.alloc_sbuf_tensor("consts_sb", [P, NCONST], F32)
    g.ident = g.consts[:, 0:P]
    g.ones = g.consts[:, P:2 * P]
    g.cols = nc.alloc_sbuf_tensor("cols", [P, COLS_B], F32)
    g.mod = nc.alloc_sbuf_tensor("mod", [P, 96, 2], F32)
    g.gain = nc.alloc_sbuf_tensor("gain", [P, 2, 2, KD, 2], F32)
    g.rope = nc.alloc_sbuf_tensor("rope_sb", [P, NT, 96], F32)
    g.gbc = nc.alloc_sbuf_tensor("gbc", [P, GB_N], F32)
    g.broadcasts = [(n, g.gbc[:, GB[n][0]:GB[n][0] + GB[n][1]]) for n in GB]
    g.bc = {n: g.gbc[:, GB[n][0]:GB[n][0] + GB[n][1]] for n in GB}
    modulation(nc, g, A)
    if upto == 0:
        return
    g.vo_dram = nc.dram_tensor("vo_dram", (T, 2 * BW), F32, kind="Internal").ap()
    R = Shared()
    R.f_dram = nc.dram_tensor("f_dram", (T, D), F32, kind="Internal").ap()
    R.list_dram = nc.dram_tensor("list_dram", (P * MAXB, 1), I32, kind="Internal").ap()
    g.y_dram = R.y_dram = nc.dram_tensor("y_dram", (P * MAXB, D), F32, kind="Internal").ap()
    R.final = lambda t: g.x_dram[t * P:(t + 1) * P, :]
    R.scores = nc.alloc_sbuf_tensor("scores", [P, NT, NE], F32)
    with nc.cleanup_on_exit():
        L = Shared()
        L.qT = nc.alloc_sbuf_tensor("qT", [P, 4, T], F32)
        L.kT = nc.alloc_sbuf_tensor("kT", [P, T], F32)
        L.v = nc.alloc_sbuf_tensor("v", [P, NT, AKW], F32)
        L.gates = nc.alloc_sbuf_tensor("gates", [P, NT, 4 * BH], F32)
        L.zT = nc.alloc_sbuf_tensor("zT", [P, 8, T], F32)
        even_project(nc, g, A, L)
        if upto == 1:
            return
        L.hb = nc.alloc_sbuf_tensor("hb", [P, NT, BW], F32)
        if only is None or 2 in only:
            even_mlstm(nc, g, A, L)
        if upto == 2:
            return
        L.cat = L.zT[:, 0:4, :].rearrange("p a t -> p (a t)").rearrange("p (n d) -> p n d", d=AW)
        even_attend(nc, g, A, L)
        if upto == 3:
            return
        M = even_mix(g, A, L)
        mix_out(nc, g, A, 0, M, R)
        if upto == 4:
            return
    ffn(nc, g, A, 0, M, R, NT, upto)
    if upto in (5, 6, 7):
        return
    with nc.cleanup_on_exit():
        L = Shared()
        L.go = nc.alloc_sbuf_tensor("go", [P, GO_N], F32)
        L.gain = {n: L.go[:, GO[n][0]:GO[n][0] + GO[n][1]] for n in GO}
        L.neg_lam = nc.alloc_sbuf_tensor("neg_lam", [P, 1], F32)
        cat = nc.alloc_sbuf_tensor("cat1", [P, NTL * D], F32)
        L.cat = cat[:, :].rearrange("p (t d) -> p t d", d=D)
        ZL = IN_ODD - 3 * CW
        L.zl = cat[:, 0:NT * ZL].rearrange("p (t n) -> p t n", n=ZL)
        L.spare = cat[:, NT * ZL:NTL * D]
        with nc.cleanup_on_exit():
            L.qcT = nc.alloc_sbuf_tensor("qcT", [P, CH, T], F32)
            L.kcT = nc.alloc_sbuf_tensor("kcT", [P, CH, T], F32)
            L.vc = nc.alloc_sbuf_tensor("vc", [P, NT, CW], F32)
            odd_project(nc, g, A, L)
            if upto == 11:
                return
            L.qdT = nc.alloc_sbuf_tensor("qdT", [P, DH, T], F32)
            L.kdT = nc.alloc_sbuf_tensor("kdT", [P, DH, T], F32)
            L.vd = nc.alloc_sbuf_tensor("vd", [P, NT, DH * DV], F32)
            odd_latent(nc, g, A, L)
            if upto == 12:
                return
            odd_attend(nc, g, A, L)
            if upto == 13:
                return
        L.room = nc.alloc_sbuf_tensor("room", [P, 5 * D], F32)
        M = odd_mix(g, A, L)
        mix_out(nc, g, A, 1, M, R)
        if upto == 14:
            return
    R.final = lambda t: out[0, t * P:(t + 1) * P, :]
    ffn(nc, g, A, 1, M, R, NTL, upto)


def places(vectors):
    at, out = 0, {}
    for name, width in vectors:
        out[name] = (at, width)
        at += width
    return out, at


GB, GB_N = places((("e_g_q", AD), ("e_g_k", AD), ("e_g_h", BW), ("e_b_gates", 4 * BH), ("b_router", NE)))
GO, GO_N = places((("o_g_qc", CD), ("o_g_kc", CD), ("o_g_sub", CV), ("o_g_cq", DQL), ("o_g_ckv", DKL), ("o_g_qd", DK),
                   ("o_g_kd", DK), ("o_lam", 4 * CD)))

NCONST = 6 * P


def constants():
    s, j = np.indices((P, P))
    upper = (s <= j).astype(np.float32)
    lower = (s >= j).astype(np.float32)
    consts = np.concatenate([np.eye(P, dtype=np.float32), np.ones((P, P), np.float32), upper, lower,
                             (upper - 1) * np.float32(BIG), (lower - 1) * np.float32(BIG)], axis=1)
    rope = []
    for rot in (AD, DR):
        n = rot // 4
        inv = np.float32(10000.0) ** (-np.arange(n, dtype=np.float32) / np.float32(n))
        pos = np.arange(SEQ)
        ang = np.concatenate([(pos // GRID_W)[:, None] * inv, (pos % GRID_W)[:, None] * inv], axis=1).astype(np.float32)
        cos = np.concatenate([np.ones((CTX, 2 * n), np.float32), np.cos(ang)])
        sin = np.concatenate([np.zeros((CTX, 2 * n), np.float32), np.sin(ang)])
        rope += [cos, sin]
    return consts, np.concatenate(rope, axis=1).astype(np.float32)


_INS = ["x", "c", "ctx", "c_ctx", "w_ada", "b_ada", "g_mix", "g_ffn", "e_w_in", "e_w_out", "e_g_q", "e_g_k", "e_conv_w",
        "e_conv_b", "e_b_gates", "e_g_h", "o_w_in", "o_w_out", "o_g_qc", "o_g_kc", "o_lam", "o_g_sub", "o_g_cq", "o_w_uq",
        "o_g_ckv", "o_w_ukv", "o_g_qd", "o_g_kd", "w_router", "b_router", "w1", "w3", "w2"]


def kernel(**inputs):
    import concourse.bacc as _bacc
    from concourse.bass_utils import run_bass_kernel_spmd as _run

    nc = _bacc.Bacc("TRN2", target_bir_lowering=False, num_devices=1)
    consts, rope = constants()
    arrays, args = {}, {}
    for name in _INS + ["consts", "rope"]:
        a = {"consts": consts, "rope": rope}.get(name)
        a = np.ascontiguousarray(inputs[name]) if a is None else a
        arrays[f"in_{name}"] = a
        args[name] = nc.dram_tensor(f"in_{name}", a.shape, mybir.dt.from_np(a.dtype), kind="ExternalInput").ap()
    out = nc.dram_tensor("out_0", (1, SEQ, D), F32, kind="ExternalOutput").ap()
    build(nc, args, out)
    r = _run(nc, [arrays], core_ids=[0])
    return r.results[0]["out_0"]
```

```python
from contextlib import ExitStack

import numpy as np
import concourse.bass as bass
from concourse import mybir

F32 = mybir.dt.float32
I32 = mybir.dt.int32
U32 = mybir.dt.uint32
F32R = mybir.dt.float32r
ALU = mybir.AluOpType
ACT = mybir.ActivationFunctionType
AX = mybir.AxisListType

P = 128
D = 1024
KD = D // P
SEQ, CTX = 1024, 256
T = SEQ + CTX
NT, NTC = T // P, CTX // P
NTL = NT - NTC
PAIRS = NT // 2
GRID_W = 64
EPS = 1e-6
AH, AD, AKV = 8, 64, 2
BH, BD = 4, 128
AW, AKW, BW = AH * AD, AKV * AD, BH * BD
IN_EVEN = AW + 2 * AKW + 4 * BW + 4 * BH
CH, CD, CV = 4, 64, 128
DH, DQL, DKL, DN, DR, DV = 4, 256, 128, 64, 32, 128
DK = DN + DR
CW = CH * CV
IN_ODD = 3 * CW + DQL + DKL + DR
LAM_INIT = 0.8 - 0.6 * float(np.exp(-0.3))
NE, NG, DE = 32, 4, 512
PER = NE // NG
MAXB = 2 * T // P + NE - 1
BIG = 1e30


class Count:

    def __init__(self, nc, name):
        self.sem, self.base, self.k = nc.alloc_semaphore(name), 0, 0

    def up(self, k=1):
        self.k += k
        return self.sem, k

    def now(self):
        return self.sem, self.base + self.k

    def turn(self, i, per):
        if i is None:
            return
        self.start = self.base + self.k if not hasattr(self, "start") or self.start is None else self.start
        self.base, self.k, self.per = self.start + i * per, 0, per

    def turned(self, turns):
        assert self.k == self.per, (self.k, self.per)
        self.base, self.k, self.start = self.start + turns * self.per, 0, None


def rstd(dve, c, out, v, s1, s2):
    dve.wait_ge(*c.now())
    dve.tensor_scalar(s1.bitcast(I32), v.bitcast(I32), 1, None, ALU.logical_shift_right).then_inc(*c.up())
    dve.wait_ge(*c.now())
    dve.tensor_scalar(out.bitcast(I32), s1.bitcast(I32), -1.0, float(0x5F3759DF), ALU.mult, ALU.add).then_inc(*c.up())
    for _ in range(3):
        dve.wait_ge(*c.now())
        dve.tensor_tensor(s1, out, out, ALU.mult).then_inc(*c.up())
        dve.wait_ge(*c.now())
        dve.tensor_tensor(s2, s1, v, ALU.mult).then_inc(*c.up())
        dve.wait_ge(*c.now())
        dve.tensor_scalar(s1, s2, -0.5, 1.5, ALU.mult, ALU.add).then_inc(*c.up())
        dve.wait_ge(*c.now())
        dve.tensor_tensor(out, out, s1, ALU.mult).then_inc(*c.up())


RSTD_N = 14

COLS_A = 96
COL_C, COL_CC, COL_GMIX, COL_GFFN, COL_CW, COL_CB = 0, 8, 16, 32, 48, 72
COLS_B = 80
V_SH1, V_SC1, V_G1, V_SH2, V_SC2, V_G2 = range(6)


class Shared:
    pass


def modulation(nc, g, A, L):
    NB = 4
    NCH = 2 * 6 * D // 512
    RING, LOW_RING = 4, 2
    with nc.cleanup_on_exit():
        last = nc.alloc_sbuf_tensor("wa_last", [P, KD * 512], F32)
        zT, qT = (ap[:, :, :].rearrange("p a t -> p (a t)") for ap in (L.zT, L.qT))
        wa = [ap.rearrange("p (k n) -> p k n", k=KD) for ap in (zT[:, 0:KD * 512], zT[:, KD * 512:2 * KD * 512], qT[:, 0:KD * 512], last[:, :])]
        rows_a = nc.alloc_sbuf_tensor("rows_a", [COLS_A, P], F32)
        rows_b = nc.alloc_sbuf_tensor("rows_b", [COLS_B, P], F32)
        ba = nc.alloc_sbuf_tensor("ba", [P, COLS_A], F32)
        th = nc.alloc_sbuf_tensor("th", [P, 2 * KD], F32)
        cs = nc.alloc_sbuf_tensor("cs", [P, 2, KD], F32)
        cs4 = nc.alloc_sbuf_tensor("cs4", [P, 4, KD], F32R)
        hi = nc.alloc_sbuf_tensor("wa_hi", [P, RING, 512], F32R)
        lo = nc.alloc_sbuf_tensor("wa_lo", [P, LOW_RING, 512], F32R)
        both = nc.alloc_sbuf_tensor("mod_both", [P, 2, 4, 2], F32)
        ps_cols = nc.alloc_psum_tensor("ps_cols", [P, 512], F32)
        mrow = nc.alloc_sbuf_tensor("mrow", [P, 2, 512], F32)
        ps_mod = nc.alloc_psum_tensor("ps_mod", [P, 2, 512], F32)
        ps_mt = nc.alloc_psum_tensor("ps_mt", [P, 2, 512], F32)
        vec_in = nc.alloc_semaphore("vec_in")
        const_in = nc.alloc_semaphore("const_in")
        x_copied = nc.alloc_semaphore("x_copied")
        w_in = [nc.alloc_semaphore(f"w_in{b}") for b in range(NB)]
        turned = nc.alloc_semaphore("turned")
        tanh_done = nc.alloc_semaphore("tanh_done")
        silu_done = nc.alloc_semaphore("silu_done")
        used, hi_ready, lo_ready = (nc.alloc_semaphore("mod_" + n) for n in ("used", "hi_ready", "lo_ready"))
        rows_clear = nc.alloc_semaphore("rows_clear")
        row_out = nc.alloc_semaphore("row_out")
        mod_turned = nc.alloc_semaphore("mod_turned")
        c = Count(nc, "dve_step")
        mod_out = nc.alloc_semaphore("mod_out")
        w_view = A["w_ada"].rearrange("l (k p) n -> p l k n", p=P)
        with nc.Block() as block:

            @block.sync
            def _(sp):
                sp.dma_start(g.consts[:, :], A["consts"]).then_inc(const_in, 16)
                sp.dma_start(rows_a[:, :], A["b_ada"].rearrange("l (a p) -> (l a) p", p=P)).then_inc(vec_in, 16)
                for at, name, pat in ((COL_C, "c", "a (k p) -> (a k) p"), (COL_CC, "c_ctx", "(k p) -> k p"),
                                      (COL_GMIX, "g_mix", "a (k p) -> (a k) p"), (COL_GFFN, "g_ffn", "a (k p) -> (a k) p"),
                                      (COL_CW, "e_conv_w", "a w (k p) -> (a w k) p"), (COL_CB, "e_conv_b", "a (k p) -> (a k) p")):
                    src = A[name].rearrange(pat, p=P)
                    sp.dma_start(rows_b[at:at + src.shape[0], :], src).then_inc(vec_in, 16)
                with sp.Fori(0, NCH // NB) as i:
                    for b in range(NB):
                        sp.wait_ge(used, i * (NB * KD) + (b + 1) * KD)
                        layer = i // (NCH // NB // 2)
                        col = (i % (NCH // NB // 2)) * (NB * 512) + b * 512
                        sp.dma_start(wa[b][:, :, :], w_view[:, bass.ds(layer, 1), :, bass.ds(col, 512)].rearrange("p l k n -> p (l k) n")).then_inc(w_in[b], 16)
                for k in range(KD):
                    sp.dma_start(L.w[:, k, :], A["e_w_in"][0, k * P:(k + 1) * P, :]).then_inc(L.w_in, 16)
                for name, dst in g.broadcasts:
                    sp.dma_start(dst, A[name].partition_broadcast(P)).then_inc(const_in, 16)
                sp.dma_start(g.rope[:, :, :], A["rope"].rearrange("(t p) r -> p t r", p=P)).then_inc(const_in, 16)
                sp.wait_ge(const_in, 16 * (2 + len(g.broadcasts)))

            @block.gpsimd
            def _(pool):
                pool.dma_start(g.x_dram[0:CTX, :], A["ctx"].rearrange("b t d -> (b t) d")).then_inc(x_copied, 16)
                pool.dma_start(g.x_dram[CTX:T, :], A["x"].rearrange("b t d -> (b t) d")).then_inc(x_copied, 16)
                pool.wait_ge(x_copied, 32)

            @block.tensor
            def _(pe):
                pe.sem_inc(used, NB * KD)
                pe.wait_ge(const_in, 16)
                pe.wait_ge(vec_in, 16 * 7)
                pe.transpose(ps_cols[:, 0:COLS_A], rows_a[:, :], g.ident[0:COLS_A, 0:COLS_A])
                pe.transpose(ps_cols[:, 128:128 + COLS_B], rows_b[:, :], g.ident[0:COLS_B, 0:COLS_B]).then_inc(turned, 1)
                pe.wait_ge(silu_done, 1)

                def product(i, b):
                    pe.wait_ge(w_in[b], i * 16 + 16)
                    pe.wait_ge(row_out, i * NB + b + 1)
                    for k in range(KD):
                        pe.wait_ge(hi_ready, i * (NB * KD) + b * KD + k + 1)
                        pe.matmul(ps_mod[0:4, b % 2, :], cs4[:, :, k], hi[:, k % RING, :], start=k == 0, stop=False)
                        pe.wait_ge(lo_ready, i * (NB * KD) + b * KD + k + 1)
                        pe.matmul(ps_mod[0:4, b % 2, :], cs4[:, :, k], lo[:, k % LOW_RING, :], start=False, stop=k == KD - 1).then_inc(used, 1)

                def turn_row(i, b):
                    pe.wait_ge(row_out, i * NB + b + 3)
                    pe.wait_ge(mod_out, i * NB + b + 1)
                    for m in range(4):
                        mm = pe.transpose(ps_mt[:, b % 2, m * P:(m + 1) * P], mrow[:, b % 2, m * P:(m + 1) * P], g.ident)
                    mm.then_inc(mod_turned, 1)

                with pe.Fori(0, NCH // NB) as i:
                    for b in range(NB):
                        product(i, b)
                        if b:
                            turn_row(i, b - 1)
                    turn_row(i, NB - 1)

            @block.scalar
            def _(act):
                act.wait_ge(c.sem, 2)
                act.activation(th[:, :], g.cols[:, 0:2 * KD], ACT.Tanh, scale=0.5).then_inc(tanh_done, 1)
                act.wait_ge(rows_clear, 1)
                act.sem_inc(row_out, 2)

                def high(i, b):
                    act.wait_ge(w_in[b], i * 16 + 16)
                    for k in range(KD):
                        act.wait_ge(used, i * (NB * KD) + b * KD + k + (NB * KD + 1 - RING))
                        act.copy(hi[:, k % RING, :], wa[b][:, k, :]).then_inc(hi_ready, 1)

                def row(i, b):
                    act.wait_ge(used, i * (NB * KD) + (b + 1 + NB) * KD)
                    act.wait_ge(mod_out, i * NB + b + 1)
                    act.copy(mrow[0:4, b % 2, :], ps_mod[0:4, b % 2, :]).then_inc(row_out, 1)

                with act.Fori(0, NCH // NB) as i:
                    for b in range(NB):
                        high(i, b)
                        if b:
                            row(i, b - 1)
                    row(i, NB - 1)

            @block.vector
            def _(dve):
                dve.memset(mrow[:, :, :], 0.0).then_inc(rows_clear, 1)
                dve.sem_inc(mod_out, 2)
                dve.wait_ge(turned, 1)
                dve.tensor_copy(ba[:, :], ps_cols[:, 0:COLS_A]).then_inc(*c.up())
                dve.tensor_copy(g.cols[:, :], ps_cols[:, 128:128 + COLS_B]).then_inc(*c.up())
                dve.wait_ge(*c.now())
                dve.wait_ge(tanh_done, 1)
                dve.scalar_tensor_tensor(out=th[:, :], in0=th[:, :], scalar=1.0, in1=g.cols[:, 0:2 * KD], op0=ALU.add, op1=ALU.mult).then_inc(*c.up())
                dve.wait_ge(*c.now())
                dve.tensor_scalar(cs[:, :, :].rearrange("p a k -> p (a k)"), th[:, :], 0.5, None, ALU.mult).then_inc(*c.up())
                dve.wait_ge(*c.now())
                dve.tensor_copy(cs4[:, 0:2, :], cs[:, :, :]).then_inc(*c.up())
                dve.wait_ge(*c.now())
                dve.tensor_tensor(cs4[:, 2:4, :], cs[:, :, :], cs4[:, 0:2, :].bitcast(F32), ALU.subtract).then_inc(silu_done, 1)

                def low(i, b):
                    for k in range(KD):
                        dve.wait_ge(hi_ready, i * (NB * KD) + b * KD + k + 1)
                        dve.wait_ge(used, i * (NB * KD) + b * KD + k + (NB * KD + 1 - LOW_RING))
                        dve.tensor_tensor(lo[:, k % LOW_RING, :], wa[b][:, k, :], hi[:, k % RING, :].bitcast(F32), ALU.subtract).then_inc(lo_ready, 1)

                def columns(i, b):
                    dve.wait_ge(mod_turned, i * NB + b + 1)
                    at = i * (NB * 4) + b * 4
                    cols = ps_mt[:, b % 2, :].rearrange("p (m w) -> p m w", w=P)
                    dve.tensor_tensor(both[:, b % 2, :, :], cols[:, :, 0:2], ba[:, bass.ds(at, 4)].unsqueeze(2).to_broadcast([P, 4, 2]), ALU.add).then_inc(*c.up())
                    dve.wait_ge(*c.now())
                    dve.tensor_tensor(g.mod[:, bass.ds(at, 4), :], both[:, b % 2, :, :], cols[:, :, 2:4], ALU.add).then_inc(mod_out, 1)

                with dve.Fori(0, NCH // NB) as i:
                    c.turn(i, NB)
                    for b in range(NB):
                        low(i, b)
                        if b:
                            columns(i, b - 1)
                    columns(i, NB - 1)
                c.turned(NCH // NB)
                dve.wait_ge(mod_out, NCH + 2)
                for layer in range(2):
                    for n, (v, gain) in enumerate(((V_SC1, COL_GMIX), (V_SC2, COL_GFFN))):
                        a = layer * 48 + v * KD
                        dve.scalar_tensor_tensor(out=g.gain[:, layer, n, :, :], in0=g.mod[:, a:a + KD, :], scalar=1.0,
                                                 in1=g.cols[:, gain + layer * KD:gain + layer * KD + KD].unsqueeze(2).to_broadcast([P, KD, 2]),
                                                 op0=ALU.add, op1=ALU.mult).then_inc(*c.up())


def head_norm_rope(dve, c, g, S, n, hd, gain, rope, src, dst):
    x3 = src.rearrange("p (n d) -> p n d", n=n)
    sq3, nrm3 = S.sq[:, 0:n * hd].rearrange("p (n d) -> p n d", n=n), S.nrm[:, 0:n * hd].rearrange("p (n d) -> p n d", n=n)
    dve.wait_ge(*c.now())
    dve.tensor_tensor(sq3, x3, x3, ALU.mult).then_inc(*c.up())
    dve.wait_ge(*c.now())
    dve.tensor_reduce(S.ss[:, 0:n], sq3, AX.X, ALU.add).then_inc(*c.up())
    dve.wait_ge(*c.now())
    dve.tensor_scalar(S.ss[:, 0:n], S.ss[:, 0:n], 1.0 / hd, EPS, ALU.mult, ALU.add).then_inc(*c.up())
    rstd(dve, c, S.r[:, 0:n], S.ss[:, 0:n], S.s1[:, 0:n], S.s2[:, 0:n])
    dve.wait_ge(*c.now())
    dve.tensor_tensor(nrm3, x3, S.r[:, 0:n].unsqueeze(2).to_broadcast([P, n, hd]), ALU.mult).then_inc(*c.up())
    dve.wait_ge(*c.now())
    gained = nrm3 if rope else dst.rearrange("p (n d) -> p n d", n=n)
    dve.tensor_tensor(gained, nrm3, gain, ALU.mult).then_inc(*c.up())


HEAD_NORM_N = 3 + RSTD_N + 2


def rope_pairs(dve, c, S, x3, out3, cos, sin):
    a, b = S.ra[:, 0:x3.shape[1], 0:cos.shape[2]], S.rb[:, 0:x3.shape[1], 0:cos.shape[2]]
    for first, second, op, at in ((cos, sin, ALU.subtract, 0), (sin, cos, ALU.add, 1)):
        dve.wait_ge(*c.now())
        dve.tensor_tensor(a, x3[:, :, 0::2], first, ALU.mult).then_inc(*c.up())
        dve.tensor_tensor(b, x3[:, :, 1::2], second, ALU.mult).then_inc(*c.up())
        dve.wait_ge(*c.now())
        dve.tensor_tensor(out3[:, :, at::2], a, b, op).then_inc(*c.up())


ROPE_N = 6


def walk_tiles(eng, tile, c=None, per=0):
    tile(0, 0)
    tile(0, 1)
    with eng.Fori(0, PAIRS - 2) as j:
        if c:
            c.turn(j, per)
        tile(j + 1, 0)
        tile(j + 1, 1)
    if c:
        c.turned(PAIRS - 2)
    tile(PAIRS - 1, 0)
    tile(PAIRS - 1, 1)


def place_of(i, h):
    final = isinstance(i, int) and i == PAIRS - 1
    first = isinstance(i, int) and i == 0 and h == 0
    return first, final, final and h == 1, (i, 0) if h else (i - 1, 1), (i + 1, 0) if h else (i, 1)


def modulation_of(g, layer, i, h, k):
    kind = 1 if isinstance(i, int) and i == 0 else 0
    return g.gain[:, layer, 0, k:k + 1, kind], g.mod[:, layer * 48 + V_SH1 * KD + k:layer * 48 + V_SH1 * KD + k + 1, kind]


def even_project(nc, g, A, L):
    QK = AW + AKW
    Z0 = AW + 2 * AKW
    V0 = Z0 + 2 * BW
    with nc.cleanup_on_exit():
        w = L.w
        x = nc.alloc_sbuf_tensor("x", [P, 2, D], F32)
        hT = nc.alloc_sbuf_tensor("hT", [P, 2, KD, P], F32)
        S = Shared()
        qk = nc.alloc_sbuf_tensor("qk", [P, QK], F32)
        S.sq = nc.alloc_sbuf_tensor("sq", [P, QK], F32)
        S.nrm = nc.alloc_sbuf_tensor("nrm", [P, QK], F32)
        qkr = S.sq
        S.ra = nc.alloc_sbuf_tensor("ra", [P, AH + AKV, AD // 2], F32)
        S.rb = nc.alloc_sbuf_tensor("rb", [P, AH + AKV, AD // 2], F32)
        vo = nc.alloc_sbuf_tensor("vo", [P, 2 * BW], F32)
        S.ss = nc.alloc_sbuf_tensor("hn_ss", [P, 16], F32)
        S.r = nc.alloc_sbuf_tensor("hn_r", [P, 16], F32)
        S.s1 = nc.alloc_sbuf_tensor("hn_s1", [P, 16], F32)
        S.s2 = nc.alloc_sbuf_tensor("hn_s2", [P, 16], F32)
        xs = nc.alloc_sbuf_tensor("xs", [P, 2, 8], F32)
        gqk = nc.alloc_sbuf_tensor("gqk", [P, AH + AKV, AD], F32)
        ps_ab = nc.alloc_psum_tensor("ps_ab", [P, 2, 2, 512], F32)
        ps_r = nc.alloc_psum_tensor("ps_r", [P, 4, 512], F32)

        def s(name):
            return nc.alloc_semaphore("ep_" + name)

        x_sq, xh_ready = s("x_sq"), s("xh_ready")
        x_in = [s("x_in0"), s("x_in1")]
        t_done, h_act, h_dve = s("t_done"), s("h_act"), s("h_dve")
        r_done, r_act, r_dve = s("r_done"), s("r_act"), s("r_dve")
        z_done, z_act, z_dve = s("z_done"), s("z_act"), s("z_dve")
        qk_ready, qt_done, qt_act, qt_dve, vo_out = s("qk_ready"), s("qt_done"), s("qt_act"), s("qt_dve"), s("vo_out")
        zeros = nc.alloc_sbuf_tensor("zeros", [P, 512], F32)
        zeroed, filled = s("zeroed"), s("filled")
        c = Count(nc, "ep_dve_step")
        with nc.Block() as block:

            @block.sync
            def _(sp):
                for h in range(2):
                    sp.dma_start(x[:, h, :], g.x_dram[h * P:(h + 1) * P, :]).then_inc(x_in[h], 16)
                with sp.Fori(0, PAIRS - 1) as j:
                    for h in range(2):
                        sp.wait_ge(t_done, j * 4 + 2 * h + 2)
                        sp.dma_start(x[:, h, :], g.x_dram[bass.ds(j * 256 + (2 + h) * P, P), :]).then_inc(x_in[h], 16)

            @block.gpsimd
            def _(pool):
                pool.memset(zeros[:, :], 0.0).then_inc(zeroed, 1)
                pool.wait_ge(zeroed, 1)
                rows = g.y_dram.rearrange("(b p) d -> p b d", p=P)
                for half in range(2):
                    pool.dma_start(rows[:, :, half * 512:(half + 1) * 512],
                                   zeros[:, :].unsqueeze(1).to_broadcast([P, MAXB, 512])).then_inc(filled, 16)
                pool.wait_ge(filled, 32)

            @block.tensor
            def _(pe):
                pe.sem_inc(qt_done, 1)

                def transposes(i, h):
                    pe.wait_ge(xh_ready, i * 2 + h + 1)
                    if not isinstance(i, int) or i > 0:
                        pe.wait_ge(qt_act, i * 2 + h - 1)
                        pe.wait_ge(qt_dve, i * 2 + h - 1)
                    for half in range(2):
                        for k in range(4 * half, 4 * half + 4):
                            mm = pe.transpose(ps_ab[:, h, half, (k % 4) * P:(k % 4) * P + P], x[:, h, k * P:(k + 1) * P], g.ident)
                        mm.then_inc(t_done, 1)

                def rows(i, h, groups):
                    pe.wait_ge(h_act, i * 2 + h + 1)
                    pe.wait_ge(h_dve, i * 2 + h + 1)
                    for n in groups:
                        cols = ((0, AW), (AW, Z0), (V0, V0 + BW), (V0 + BW, V0 + 2 * BW))[n]
                        if n == 1:
                            pe.wait_ge(r_dve, i * 2 + h + 1)
                        else:
                            pe.wait_ge(r_act, i * 6 + 3 * h + (1, 0, 2, 3)[n])
                        for k in range(KD):
                            mm = pe.matmul(ps_r[:, n, 0:cols[1] - cols[0]], hT[:, h, k, :], w[:, k, cols[0]:cols[1]],
                                           start=k == 0, stop=k == KD - 1)
                        if n == 1:
                            for k in range(KD):
                                mm = pe.matmul(ps_r[:, n, 256:384], hT[:, h, k, :], w[:, k, IN_EVEN - P:IN_EVEN],
                                               start=k == 0, stop=k == KD - 1)
                        mm.then_inc(r_done, 1)

                def channels(i, h):
                    for half in range(2):
                        for cc in range(4 * half, 4 * half + 4):
                            for k in range(KD):
                                mm = pe.matmul(ps_ab[:, h, half, (cc % 4) * P:(cc % 4) * P + P], w[:, k, Z0 + cc * P:Z0 + (cc + 1) * P],
                                               hT[:, h, k, :], start=k == 0, stop=k == KD - 1)
                        mm.then_inc(z_done, 1)

                def turn_qk(i, h):
                    pe.wait_ge(qk_ready, i * 2 + h + 2)
                    if not place_of(i, h)[1]:
                        pe.wait_ge(x_sq, i * 2 + h + 3)
                    pe.wait_ge(z_act, i * 2 + h + 1)
                    pe.wait_ge(z_dve, i * 2 + h + 1)
                    for j in range(4):
                        pe.transpose(ps_ab[:, h, 0, j * P:(j + 1) * P], qkr[:, j * P:(j + 1) * P], g.ident)
                    pe.transpose(ps_ab[:, h, 1, 0:P], qkr[:, AW:AW + P], g.ident).then_inc(qt_done, 1)

                pe.wait_ge(L.w_in, 16 * KD)

                def tile(i, h):
                    first, final, last, before, after = place_of(i, h)
                    rows(i, h, (0, 1))
                    if not first:
                        turn_qk(*before)
                    rows(i, h, (2,))
                    if not last:
                        transposes(*after)
                    rows(i, h, (3,))
                    channels(i, h)

                transposes(0, 0)
                walk_tiles(pe, tile)
                turn_qk(PAIRS - 1, 1)

            @block.scalar
            def _(act):
                act.sem_inc(r_act, 3)

                def squares(i, h):
                    act.wait_ge(x_in[h], i * 16 + 16)
                    if not isinstance(i, int) or i > 0:
                        act.wait_ge(z_dve, i * 2 + h - 1)
                        act.wait_ge(z_act, i * 2 + h - 1)
                    act.activation(ps_ab[:, h, :, :].rearrange("p a n -> p (a n)"), x[:, h, :], ACT.Square,
                                   accum_out=xs[:, h, 0:1]).then_inc(x_sq, 1)

                def modulate(i, h):
                    act.wait_ge(t_done, i * 4 + 2 * h + 1)
                    for k in range(4):
                        gain, shift = modulation_of(g, 0, i, h, k)
                        m = act.activation(hT[:, h, k, :], ps_ab[:, h, 0, k * P:(k + 1) * P], ACT.Identity, scale=gain, bias=shift)
                    m.then_inc(h_act, 1)

                def rows_out(i, h):
                    act.wait_ge(r_done, i * 8 + 4 * h + 1)
                    act.wait_ge(qk_ready, i * 2 + h + 1)
                    act.copy(qk[:, 0:AW].rearrange("p (h k d) -> p k h d", k=AKV, d=AD),
                             ps_r[:, 0, :].rearrange("p (k h d) -> p k h d", k=AKV, d=AD)).then_inc(r_act, 1)

                def v_out(i, h):
                    act.wait_ge(r_done, i * 8 + 4 * h + 3)
                    act.wait_ge(vo_out, i * 32 + 16 * h + 16)
                    act.copy(vo[:, 0:BW], ps_r[:, 2, :]).then_inc(r_act, 1)

                def gate_out(i, h):
                    act.wait_ge(r_done, i * 8 + 4 * h + 4)
                    act.activation(vo[:, BW:2 * BW], ps_r[:, 3, :], ACT.Tanh, scale=0.5).then_inc(r_act, 1)
                    act.wait_ge(r_act, i * 6 + 3 * h + 6)
                    act.dma_start(g.vo_dram[bass.ds(i * 256 + h * P, P), :], vo[:, :]).then_inc(vo_out, 16)

                def channels_out(i, h):
                    act.wait_ge(z_done, i * 4 + 2 * h + 1)
                    act.copy(L.zT[:, 0:4, bass.ds(i * 256 + h * P, P)],
                             ps_ab[:, h, 0, :].rearrange("p (a n) -> p a n", n=P)).then_inc(z_act, 1)

                def q_out(i, h):
                    act.wait_ge(qt_done, i * 2 + h + 2)
                    act.copy(L.qT[:, :, bass.ds(i * 256 + h * P, P)],
                             ps_ab[:, h, 0, :].rearrange("p (a n) -> p a n", n=P)).then_inc(qt_act, 1)

                act.sem_inc(vo_out, 16)
                act.sem_inc(qk_ready, 1)

                def tile(i, h):
                    first, final, last, before, after = place_of(i, h)
                    rows_out(i, h)
                    if not first:
                        q_out(*before)
                    v_out(i, h)
                    if not last:
                        modulate(*after)
                    gate_out(i, h)
                    channels_out(i, h)
                    if not final:
                        squares(i + 1, h)

                squares(0, 0)
                squares(0, 1)
                modulate(0, 0)
                walk_tiles(act, tile)
                q_out(PAIRS - 1, 1)
                act.wait_ge(vo_out, 16 * NT + 16)

            @block.vector
            def _(dve):
                dve.sem_inc(r_dve, 1)
                dve.tensor_copy(gqk[:, 0:AH, :], g.bc["e_g_q"].unsqueeze(1).to_broadcast([P, AH, AD])).then_inc(*c.up())
                dve.tensor_copy(gqk[:, AH:, :], g.bc["e_g_k"].unsqueeze(1).to_broadcast([P, AKV, AD])).then_inc(*c.up())

                def normalise(i, h):
                    dve.wait_ge(x_sq, i * 2 + h + 1)
                    dve.tensor_scalar(xs[:, h, 1:2], xs[:, h, 0:1], 1.0 / D, EPS, ALU.mult, ALU.add).then_inc(*c.up())
                    rstd(dve, c, xs[:, h, 2:3], xs[:, h, 1:2], xs[:, h, 3:4], xs[:, h, 4:5])
                    dve.wait_ge(*c.now())
                    dve.tensor_scalar(x[:, h, :], x[:, h, :], xs[:, h, 2:3], None, ALU.mult).then_inc(xh_ready, 1)

                def modulate(i, h):
                    dve.wait_ge(t_done, i * 4 + 2 * h + 2)
                    for k in range(4, 8):
                        gain, shift = modulation_of(g, 0, i, h, k)
                        m = dve.tensor_scalar(hT[:, h, k, :], ps_ab[:, h, 1, (k - 4) * P:(k - 3) * P], gain, shift, ALU.mult, ALU.add)
                    m.then_inc(h_dve, 1)

                def rows_out(i, h):
                    dve.wait_ge(r_done, i * 8 + 4 * h + 2)
                    dve.tensor_copy(qk[:, AW:QK], ps_r[:, 1, 0:AKW]).then_inc(*c.up())
                    dve.tensor_copy(L.v[:, bass.ds(i * 2 + h, 1), :], ps_r[:, 1, AKW:2 * AKW].unsqueeze(1)).then_inc(*c.up())
                    dve.tensor_tensor(L.gates[:, bass.ds(i * 2 + h, 1), :], ps_r[:, 1, 3 * P - 4 * BH:3 * P].unsqueeze(1),
                                      g.bc["e_b_gates"].unsqueeze(1), ALU.add).then_inc(r_dve, 1)

                def norm_rope(i, h):
                    dve.wait_ge(r_act, i * 6 + 3 * h + 4)
                    dve.wait_ge(qt_done, i * 2 + h + 1)
                    head_norm_rope(dve, c, g, S, AH + AKV, AD, gqk[:, :, :], True, qk[:, :], None)
                    n3 = S.nrm[:, :].rearrange("p (n d) -> p n d", d=AD)
                    o3 = qkr[:, :].rearrange("p (n d) -> p n d", d=AD)
                    cos = g.rope[:, bass.ds(i * 2 + h, 1), 0:32].to_broadcast([P, AH + AKV, 32])
                    sin = g.rope[:, bass.ds(i * 2 + h, 1), 32:64].to_broadcast([P, AH + AKV, 32])
                    rope_pairs(dve, c, S, n3, o3, cos, sin)
                    dve.wait_ge(*c.now())
                    dve.sem_inc(qk_ready, 1)

                def channels_out(i, h):
                    dve.wait_ge(z_done, i * 4 + 2 * h + 2)
                    dve.tensor_copy(L.zT[:, 4:8, bass.ds(i * 256 + h * P, P)],
                                    ps_ab[:, h, 1, :].rearrange("p (a n) -> p a n", n=P)).then_inc(z_dve, 1)

                def k_out(i, h):
                    dve.wait_ge(qt_done, i * 2 + h + 2)
                    dve.tensor_copy(L.kT[:, bass.ds(i * 256 + h * P, P)], ps_ab[:, h, 1, 0:P]).then_inc(qt_dve, 1)

                def tile(i, h):
                    first, final, last, before, after = place_of(i, h)
                    rows_out(i, h)
                    if not first:
                        k_out(*before)
                    norm_rope(i, h)
                    if not last:
                        modulate(*after)
                    channels_out(i, h)
                    if not final:
                        normalise(i + 1, h)

                normalise(0, 0)
                normalise(0, 1)
                modulate(0, 0)
                walk_tiles(dve, tile, c, 2 * (1 + RSTD_N) + 2 * (2 + HEAD_NORM_N + ROPE_N))
                k_out(PAIRS - 1, 1)


def even_mlstm(nc, g, A, L):
    NC = 64

    def s(name):
        return nc.alloc_semaphore("ml_" + name)

    with nc.cleanup_on_exit():
        tab = nc.alloc_sbuf_tensor("ml_tab", [P, 12, P], F32)
        lf, ig, bcum, a_row, mx_row, g_row, ai_row, ai_col, a_col, g_col, em_col, dec = (tab[:, n, :] for n in range(12))
        cols4 = tab[:, 8:12, :]
        cur = nc.alloc_sbuf_tensor("ml_cur", [P, 4, 4, BH], F32)
        m_row = nc.alloc_sbuf_tensor("ml_m_row", [1, 4, P], F32)
        m_col = nc.alloc_sbuf_tensor("ml_m_col", [P, 4], F32)
        halfw = nc.alloc_sbuf_tensor("ml_halfw", [P, 32], F32)
        arena = nc.alloc_sbuf_tensor("ml_arena", [P, 4 * T], F32)
        yb = arena[:, 0:2 * T].rearrange("p (a t) -> p a t", a=2)
        tb = arena[:, 2 * T:4 * T].rearrange("p (a t) -> p a t", a=2)
        bc = arena[:, 0:4 * 2 * BH * P].rearrange("p (b n f) -> p b n f", b=4, n=2)
        row_dram = nc.dram_tensor("ml_rows", (2, 2, NC, P), F32, kind="Internal").ap()
        qs = nc.alloc_sbuf_tensor("ml_qs", [P, 4, BH, P], F32)
        ks = nc.alloc_sbuf_tensor("ml_ks", [P, 4, BH, P], F32)
        qa = nc.alloc_sbuf_tensor("ml_qa", [P, 4, BH, P], F32)
        tm = nc.alloc_sbuf_tensor("ml_tm", [P, 4, BH, P], F32)
        vv = nc.alloc_sbuf_tensor("ml_vv", [P, 4, BH, P + 4], F32)
        wt = nc.alloc_sbuf_tensor("ml_wt", [P, 2, BH, P], F32)
        sw = nc.alloc_sbuf_tensor("ml_sw", [P, 2, BH, P], F32)
        kg = nc.alloc_sbuf_tensor("ml_kg", [P, 2, BH, P], F32)
        C = nc.alloc_sbuf_tensor("ml_C", [P, 2, BH, P + 4], F32)
        dn = nc.alloc_sbuf_tensor("ml_dn", [P, 3, BH], F32)
        ps_s = nc.alloc_psum_tensor("ml_ps_s", [P, 2, 512], F32)
        ps_k = nc.alloc_psum_tensor("ml_ps_k", [P, 2, 512], F32)
        ps_n = nc.alloc_psum_tensor("ml_ps_n", [P, 2, 512], F32)
        ps_c = nc.alloc_psum_tensor("ml_ps_c", [P, 2, 512], F32)
        c = Count(nc, "ml_dve_step")
        conv_out, tanh_done, gate_abs, gate_exp, gate_ln, lf_ready = (s("conv_out"), s("tanh_done"), s("gate_abs"),
                                                                      s("gate_exp"), s("gate_ln"), s("lf_ready"))
        gp, gd, ga = s("gate_pe"), s("gate_dve"), s("gate_act")
        rows_out, tabs_ready, act_ln = s("rows_out"), s("tabs_ready"), s("act_ln")
        loaded = [s(f"loaded{b}") for b in range(4)]
        staged, s_done, k_done, n_done, c_done = s("staged"), s("s_done"), s("k_done"), s("n_done"), s("c_done")
        w_ready, sw_ready, kg_ready, h_out, c_out, z_ready = (s("w_ready"), s("sw_ready"), s("kg_ready"), s("h_out"),
                                                              s("c_out"), s("z_ready"))

        def place(ps, h):
            return ps[:, 0, h * 129:(h + 1) * 129] if h < 3 else ps[:, 1, 0:129]

        def turns(eng, body):
            body(0, 0, lambda par: (par, 1 - par))
            with eng.Fori(0, NTL // 2) as i:
                body(i + 1, i * 2 + 2, lambda par: (i * 2 + 2 + par, i * (-2) + 9 - par))

        with nc.Block() as block:

            @block.sync
            def _(sp):
                sp.wait_ge(gd, 6)
                sp.dma_start(row_dram[0].rearrange("d r t -> (d r) t"), mx_row).then_inc(rows_out, 16)
                sp.wait_ge(ga, 1)
                sp.dma_start(row_dram[1].rearrange("d r t -> (d r) t"), ai_row).then_inc(rows_out, 16)
                sp.wait_ge(rows_out, 32)
                sp.wait_ge(z_ready, 1)

                def body(it, step, tiles):
                    for par in range(2):
                        for d in range(2):
                            b = 2 * par + d
                            tok, row = tiles(par)[d] * P, step * 4 + 4 * par
                            sp.wait_ge(c_done, it * 4 + b + 1)
                            sp.wait_ge(staged, (it * 4 + b) * 5 + 5)
                            for n in range(2):
                                src = row_dram[n, d:d + 1, bass.ds(row, BH), :].rearrange("d r t -> d (r t)")
                                sp.dma_start(bc[:, b, n, :], src.to_broadcast([P, BH * P])).then_inc(loaded[b], 16)
                            sp.dma_start(vv[:, b, :, 0:P], g.vo_dram[bass.ds(tok, P), 0:BW].rearrange("p (h e) -> p h e", e=P)).then_inc(loaded[b], 16)

                turns(sp, body)

            @block.gpsimd
            def _(pool):
                pool.sem_inc(staged, 20)
                pool.wait_ge(z_ready, 1)
                pool.wait_ge(tabs_ready, 1)

                def body(it, step, tiles):
                    for par in range(2):
                        for d in range(2):
                            b, tile = 2 * par + d, tiles(par)[d]
                            pool.wait_ge(loaded[b], it * 48 + 48)
                            pool.wait_ge(c_done, it * 4 + b + 1)
                            pool.wait_ge(w_ready, it * 4 + b + 1)
                            pool.wait_ge(c_out, it * 4 + b + 1)
                            pool.tensor_copy(cur[:, b, :, :], cols4[:, :, bass.ds(step * 4 + 4 * par + d * NC, BH)]).then_inc(staged, 1)
                            q = L.zT[:, 0:4, bass.ds(tile * P, P)]
                            pool.tensor_copy(qs[:, b, :, :], q).then_inc(staged, 1)
                            pool.tensor_copy(ks[:, b, :, :], L.zT[:, 4:8, bass.ds(tile * P, P)]).then_inc(staged, 1)
                            pool.tensor_tensor(tm[:, b, :, :], g.consts[:, (4 + d) * P:(5 + d) * P].unsqueeze(1).to_broadcast([P, BH, P]),
                                               bc[:, b, 0, :].rearrange("p (h t) -> p h t", t=P), ALU.subtract).then_inc(staged, 1)
                            pool.tensor_tensor(qa[:, b, :, :], q, bc[:, b, 1, :].rearrange("p (h t) -> p h t", t=P), ALU.mult).then_inc(staged, 1)

                turns(pool, body)

            @block.tensor
            def _(pe):
                pe.wait_ge(lf_ready, 1)
                pe.matmul(ps_s[:, 0, 0:NC], g.consts[:, 2 * P:3 * P], lf[:, 0:NC], start=True, stop=True)
                pe.matmul(ps_s[:, 1, 0:NC], g.consts[:, 3 * P:4 * P], lf[:, NC:2 * NC], start=True, stop=True)
                pe.matmul(ps_k[0:1, 0, 0:P], g.ones[:, 0:1], lf, start=True, stop=True).then_inc(gp, 1)
                pe.wait_ge(gd, 1)
                pe.transpose(ps_k[:, 1, 0:P], a_col, g.ident).then_inc(gp, 1)
                pe.wait_ge(gd, 2)
                pe.transpose(ps_n[0:1, 0, 0:P], m_col[:, 0:1], g.ident).then_inc(gp, 1)
                pe.wait_ge(gd, 3)
                pe.matmul(ps_n[:, 1, 0:1], m_row[0:1, 2, :], g.ident[0:1, 0:1], start=True, stop=True).then_inc(gp, 1)
                pe.wait_ge(gd, 6)
                pe.transpose(ps_c[:, 0, 0:P], mx_row, g.ident).then_inc(gp, 1)
                pe.wait_ge(ga, 2)
                pe.transpose(ps_c[:, 1, 0:P], g_row, g.ident)
                pe.transpose(ps_c[:, 1, P:2 * P], ai_row, g.ident).then_inc(gp, 1)
                pe.wait_ge(gd, 8)
                pe.matmul(ps_s[:, 0, 0:P], g.ident[:, P - 1:P].to_broadcast([P, P]), ai_col, start=True, stop=True)
                pe.matmul(ps_s[:, 1, 0:P], g.ident[:, 0:1].to_broadcast([P, P]), ai_col, start=True, stop=True).then_inc(gp, 1)
                pe.sem_inc(c_done, 4)

                def body(it, step, tiles):
                    for par in range(2):
                        for d in range(2):
                            b = 2 * par + d
                            u = it * 4 + b
                            pe.wait_ge(staged, u * 5 + 25)
                            pe.wait_ge(sw_ready, u + 1)
                            for h in range(BH):
                                mm = pe.matmul(ps_s[:, d, h * P:(h + 1) * P], ks[:, b, h, :], qs[:, b, h, :], start=True, stop=True)
                            mm.then_inc(s_done, 1)
                            pe.wait_ge(kg_ready, u + 1)
                            for h in range(BH):
                                mm = pe.transpose(ps_k[:, d, h * P:(h + 1) * P], ks[:, b, h, :], g.ident)
                            mm.then_inc(k_done, 1)
                        for d in range(2):
                            b = 2 * par + d
                            u = it * 4 + b
                            pe.wait_ge(sw_ready, u + 3)
                            pe.wait_ge(h_out, u + 1)
                            pe.wait_ge(c_out, u + 4)
                            for h in range(BH):
                                pe.matmul(place(ps_n, h), sw[:, d, h, :], vv[:, b, h, 0:129], start=True, stop=False)
                                mm = pe.matmul(place(ps_n, h), qa[:, b, h, :], C[:, d, h, 0:129], start=False, stop=True)
                            mm.then_inc(n_done, 1)
                            pe.wait_ge(kg_ready, u + 3)
                            for h in range(BH):
                                mm = pe.matmul(place(ps_c, h), kg[:, d, h, :], vv[:, b, h, 0:129], start=True, stop=True)
                            mm.then_inc(c_done, 1)

                turns(pe, body)

            @block.scalar
            def _(act):
                act.wait_ge(gate_abs, 1)
                act.activation(a_col, bcum, ACT.Exp, scale=-1.0).then_inc(gate_exp, 1)
                act.wait_ge(gate_exp, 1)
                act.activation(g_col, a_col, ACT.Ln, bias=g.ones[:, 0:1]).then_inc(gate_ln, 1)
                act.wait_ge(gd, 6)
                act.activation(ai_row, mx_row, ACT.Exp, scale=-1.0, bias=m_col[:, 1:2]).then_inc(ga, 1)
                act.activation(g_row, a_row, ACT.Exp, bias=m_col[:, 2:3]).then_inc(ga, 1)
                act.wait_ge(gd, 7)
                act.activation(em_col, em_col, ACT.Exp, scale=-1.0).then_inc(ga, 1)
                with act.Fori(0, 4) as i:
                    for par in range(2):
                        act.wait_ge(conv_out, i * 2 + par + 1)
                        act.activation(tb[:, par, :], yb[:, par, :], ACT.Tanh).then_inc(tanh_done, 1)
                act.wait_ge(tabs_ready, 1)
                act.sem_inc(w_ready, 4)
                act.sem_inc(kg_ready, 2)

                def body(it, step, tiles):
                    for par in range(2):
                        for d in range(2):
                            b = 2 * par + d
                            u = it * 4 + b
                            act.wait_ge(staged, u * 5 + 25)
                            act.wait_ge(sw_ready, u + 1)
                            for h in range(BH):
                                w = act.activation(wt[:, d, h, :], tm[:, b, h, :], ACT.Exp, bias=cur[:, b, 0, h:h + 1])
                            w.then_inc(w_ready, 1)
                        for d in range(2):
                            b = 2 * par + d
                            u = it * 4 + b
                            act.wait_ge(k_done, u + 1)
                            act.wait_ge(c_done, u + 3)
                            for h in range(BH):
                                w = act.activation(kg[:, d, h, :], ps_k[:, d, h * P:(h + 1) * P], ACT.Copy, scale=cur[:, b, 1, h:h + 1])
                            w.then_inc(kg_ready, 1)

                turns(act, body)

            @block.vector
            def _(dve):
                def own():
                    dve.wait_ge(*c.now())

                dve.tensor_scalar(halfw[:, :], g.cols[:, COL_CW:COL_CW + 32], 0.5, None, ALU.mult).then_inc(*c.up())
                dve.memset(tab[:, :, :], 0.0).then_inc(*c.up())
                dve.memset(L.hb[:, :, :], 0.0).then_inc(*c.up())
                dve.memset(C[:, :, :, :], 0.0).then_inc(*c.up())
                dve.memset(vv[:, :, :, P:P + 4], 1.0).then_inc(*c.up())
                dve.memset(m_row[:, :, :], 0.0).then_inc(*c.up())
                own()
                for dst, at in ((ig, 0), (dec, 4)):
                    v = [dst[:, d * NC:d * NC + 40].rearrange("p (s h) -> p s h", h=BH) for d in range(2)]
                    dve.tensor_copy(v[0], L.gates[:, :, at:at + 4]).then_inc(*c.up())
                    dve.tensor_copy(v[1][:, 0:2, :], L.gates[:, 1::-1, at + 8:at + 12]).then_inc(*c.up())
                    dve.tensor_copy(v[1][:, 2:10, :], L.gates[:, 9:1:-1, at + 8:at + 12]).then_inc(*c.up())
                own()
                dve.scalar_tensor_tensor(out=bcum, in0=dec, scalar=-1.0, in1=dec, op0=ALU.mult, op1=ALU.max).then_inc(gate_abs, 1)
                dve.wait_ge(gate_ln, 1)
                dve.scalar_tensor_tensor(out=lf, in0=dec, scalar=0.0, in1=g_col, op0=ALU.min, op1=ALU.subtract).then_inc(lf_ready, 1)
                dve.wait_ge(gp, 1)
                dve.tensor_copy(bcum[:, 0:NC], ps_s[:, 0, 0:NC]).then_inc(*c.up())
                dve.tensor_copy(bcum[:, NC:2 * NC], ps_s[:, 1, 0:NC]).then_inc(*c.up())
                dve.tensor_copy(m_row[0:1, 0, :], ps_k[0:1, 0, 0:P]).then_inc(*c.up())
                own()
                dve.tensor_tensor(a_col, ig, bcum, ALU.subtract).then_inc(gd, 1)
                dve.wait_ge(gp, 2)
                dve.tensor_copy(a_row, ps_k[:, 1, 0:P]).then_inc(*c.up())
                dve.tensor_reduce(m_col[:, 0:1], ps_k[:, 1, 0:P], AX.X, ALU.max).then_inc(gd, 1)
                dve.wait_ge(gp, 3)
                dve.tensor_copy(m_row[0:1, 1, :], ps_n[0:1, 0, 0:P]).then_inc(*c.up())
                last, top, m, tmp = (m_row[0:1, n, :].rearrange("o (d r) -> o d r", d=2) for n in range(4))
                for st in range(9):
                    a, b = slice(st * 4, st * 4 + 4), slice(st * 4 + 4, st * 4 + 8)
                    own()
                    dve.tensor_tensor(tmp[:, :, a], m[:, :, a], top[:, :, a], ALU.max).then_inc(*c.up())
                    own()
                    dve.tensor_tensor(m[:, :, b], tmp[:, :, a], last[:, :, a], ALU.add).then_inc(*c.up())
                own()
                dve.sem_inc(gd, 1)
                dve.wait_ge(gp, 4)
                dve.tensor_copy(m_col[:, 1:2], ps_n[:, 1, 0:1]).then_inc(*c.up())
                own()
                dve.tensor_tensor_scan(mx_row[0:NC, :], a_row[0:NC, :], a_row[0:NC, :], m_col[0:NC, 1:2], ALU.max, ALU.max).then_inc(gd, 1)
                dve.tensor_tensor_scan(mx_row[NC:P, ::-1], a_row[NC:P, ::-1], a_row[NC:P, ::-1], m_col[NC:P, 1:2], ALU.max, ALU.max).then_inc(gd, 1)
                dve.wait_ge(gd, 5)
                dve.tensor_scalar(m_col[0:NC, 2:3], mx_row[0:NC, P - 1:P], -1.0, None, ALU.mult).then_inc(*c.up())
                dve.tensor_scalar(m_col[NC:P, 2:3], mx_row[NC:P, 0:1], -1.0, None, ALU.mult).then_inc(*c.up())
                own()
                dve.sem_inc(gd, 1)
                dve.wait_ge(gp, 5)
                dve.tensor_tensor(em_col, ps_c[:, 0, 0:P], bcum, ALU.add).then_inc(gd, 1)
                dve.wait_ge(gp, 6)
                dve.tensor_copy(g_col, ps_c[:, 1, 0:P]).then_inc(*c.up())
                dve.tensor_copy(ai_col, ps_c[:, 1, P:2 * P]).then_inc(gd, 1)
                dve.wait_ge(gp, 7)
                dve.tensor_copy(dec[:, 0:NC], ps_s[:, 0, 0:NC]).then_inc(*c.up())
                dve.tensor_copy(dec[:, NC:P], ps_s[:, 1, NC:P]).then_inc(*c.up())
                own()
                dve.wait_ge(ga, 3)
                dve.sem_inc(tabs_ready, 1)

                def convolve(i, par):
                    cc = i * 2 + par
                    y, z = yb[:, par, :], L.zT[:, bass.ds(cc, 1), :]
                    y3 = y.unsqueeze(1)
                    own()
                    dve.tensor_scalar(y3, z, halfw[:, bass.ds(cc + 8, 1)], halfw[:, bass.ds(cc + 24, 1)], ALU.mult, ALU.add).then_inc(*c.up())
                    for a, n in ((0, CTX), (CTX, SEQ)):
                        own()
                        dve.scalar_tensor_tensor(out=y3[:, :, a + 1:a + n], in0=z[:, :, a:a + n - 1], scalar=halfw[:, bass.ds(cc, 1)],
                                                 in1=y3[:, :, a + 1:a + n], op0=ALU.mult, op1=ALU.add).then_inc(*c.up())
                    for a, n in ((0, CTX), (CTX, SEQ)):
                        own()
                        dve.scalar_tensor_tensor(out=y3[:, :, a:a + n - 1], in0=z[:, :, a + 1:a + n], scalar=halfw[:, bass.ds(cc + 16, 1)],
                                                 in1=y3[:, :, a:a + n - 1], op0=ALU.mult, op1=ALU.add).then_inc(*c.up())
                    own()
                    dve.sem_inc(conv_out, 1)

                def gate_channels(i, par):
                    z = L.zT[:, bass.ds(i * 2 + par, 1), :]
                    dve.wait_ge(tanh_done, i * 2 + par + 1)
                    dve.scalar_tensor_tensor(out=z, in0=tb[:, par, :].unsqueeze(1), scalar=1.0, in1=yb[:, par, :].unsqueeze(1),
                                             op0=ALU.add, op1=ALU.mult).then_inc(*c.up())

                with dve.Fori(0, 4) as i:
                    c.turn(i, 12)
                    convolve(i, 0)
                    convolve(i, 1)
                    gate_channels(i, 0)
                    gate_channels(i, 1)
                c.turned(4)
                own()
                dve.tensor_scalar(L.zT[:, 0:4, :], L.zT[:, 0:4, :], BD ** -0.5, None, ALU.mult).then_inc(*c.up())
                own()
                dve.sem_inc(z_ready, 1)
                dve.sem_inc(sw_ready, 2)
                dve.sem_inc(n_done, 2)
                dve.sem_inc(h_out, 1)
                dve.sem_inc(c_out, 4)

                def body(it, step, tiles):
                    if not isinstance(it, int):
                        c.turn(it - 1, 4 * 5)
                    for par in range(2):
                        for d in range(2):
                            u = it * 4 + 2 * par + d
                            dve.wait_ge(s_done, u + 1)
                            dve.wait_ge(w_ready, u + 5)
                            dve.wait_ge(n_done, u + 1)
                            dve.tensor_tensor(sw[:, d, :, :], ps_s[:, d, :].rearrange("p (h t) -> p h t", t=P), wt[:, d, :, :], ALU.mult).then_inc(sw_ready, 1)
                        for d in range(2):
                            b = 2 * par + d
                            u = it * 4 + b
                            tile = tiles(par)[d]
                            dve.wait_ge(n_done, u + 3)
                            dve.tensor_copy(dn[:, 0, 0:3], ps_n[:, 0, 0:387].rearrange("p (h e) -> p h e", e=129)[:, :, 128]).then_inc(*c.up())
                            dve.tensor_copy(dn[:, 0, 3:4], ps_n[:, 1, 128:129]).then_inc(*c.up())
                            own()
                            dve.scalar_tensor_tensor(out=dn[:, 1, :], in0=dn[:, 0, :], scalar=-1.0, in1=dn[:, 0, :], op0=ALU.mult, op1=ALU.max).then_inc(*c.up())
                            own()
                            dve.tensor_tensor(dn[:, 2, :], dn[:, 1, :], cur[:, b, 2, :], ALU.max).then_inc(*c.up())
                            own()
                            dve.reciprocal(dn[:, 1, :], dn[:, 2, :]).then_inc(*c.up())
                            own()
                            for h in range(BH):
                                o = L.hb[:, bass.ds(tile, 1), h * P:(h + 1) * P]
                                w = dve.scalar_tensor_tensor(out=o, in0=place(ps_n, h)[:, 0:P].unsqueeze(1), scalar=dn[:, 1, h:h + 1], in1=o, op0=ALU.mult, op1=ALU.add)
                            w.then_inc(h_out, 1)
                            dve.wait_ge(c_done, u + 5)
                            for h in range(BH):
                                w = dve.scalar_tensor_tensor(out=C[:, d, h, 0:129], in0=C[:, d, h, 0:129], scalar=cur[:, b, 3, h:h + 1],
                                                             in1=place(ps_c, h), op0=ALU.mult, op1=ALU.add)
                            w.then_inc(c_out, 1)
                    if not isinstance(it, int):
                        c.turned(NTL // 2)

                turns(dve, body)



class Job:

    def __init__(self, parts, v, cols, out, t2):
        self.parts, self.v, self.cols, self.out, self.t2 = parts, v, cols, out, t2


def attend(nc, g, tag, sections, neg_lam=None):

    def s(name):
        return nc.alloc_semaphore(tag + name)

    with nc.cleanup_on_exit():
        pe4 = nc.alloc_sbuf_tensor(tag + "exps", [P, 4, T], F32)
        pT = nc.alloc_sbuf_tensor(tag + "pT", [P, 2, T], F32)
        st = nc.alloc_sbuf_tensor(tag + "stats", [P, 4, 8], F32)
        ps_s = nc.alloc_psum_tensor(tag + "ps_s", [P, 2, 3 * 512], F32)
        ps_t = nc.alloc_psum_tensor(tag + "ps_t", [P, 512], F32)
        ps_o = nc.alloc_psum_tensor(tag + "ps_o", [P, 512], F32)
        c = Count(nc, tag + "dve_step")
        staged, s_done, m_ready, e_done = s("staged"), s("s_done"), s("m_ready"), s("e_done")
        mixed, t_done, t_out, o_done, o_out = s("mixed"), s("t_done"), s("t_out"), s("o_done"), s("o_out")

        def walk(eng, visit, start=None, own=None, per_job=0):
            J = Pn = G = 0
            for sec in sections:
                nj, npart, ng = len(sec.jobs), sum(len(j.parts) for j in sec.jobs), len(sec.jobs) * len(sec.groups)
                if start:
                    start(sec, J, Pn, G)
                if sec.turns > 1:
                    with eng.Fori(0, sec.turns - 1) as i:
                        if own:
                            own.turn(i, per_job * nj + (npart - nj) * 4)
                        visit(sec, i, i * nj + J, i * npart + Pn, i * ng + G, False)
                    if own:
                        own.turned(sec.turns - 1)
                n = sec.turns - 1
                visit(sec, n, n * nj + J, n * npart + Pn, n * ng + G, True)
                J, Pn, G = J + sec.turns * nj, Pn + sec.turns * npart, G + sec.turns * ng

        def before_of(sec):
            return [sum(len(j.parts) for j in sec.jobs[:n]) for n in range(len(sec.jobs) + 1)]

        with nc.Block() as block:

            @block.gpsimd
            def _(pool):
                Pn = 0
                for sec in sections:
                    npart = sum(len(j.parts) for j in sec.jobs)
                    for dst, src in sec.stage:
                        pool.wait_ge(s_done, Pn + 1)
                        pool.tensor_copy(dst, src(0)).then_inc(staged, 1)
                    if sec.turns > 1:
                        with pool.Fori(0, sec.turns - 1) as i:
                            for t2, (dst, src) in enumerate(sec.stage):
                                pool.wait_ge(s_done, i * npart + (Pn + (t2 + 1) * npart // 2 + 1))
                                pool.tensor_copy(dst, src(i + 1)).then_inc(staged, 1)
                    Pn += sec.turns * npart

            @block.tensor
            def _(pe):
                pe.sem_inc(s_done, 1)

                def scores(sec, it, Pn, n, part):
                    jobs = sec.jobs
                    if part == 0 and n % (len(jobs) // 2) == 0:
                        pe.wait_ge(staged, it * 2 + (sec.staged_before + n // (len(jobs) // 2) + 1))
                    q, k = jobs[n % len(jobs)].parts[part]
                    keys, p = sec.ntiles * P, before_of(sec)[n] + part
                    pe.wait_ge(e_done, Pn + p + 1)
                    for a in range(0, keys, 512):
                        b = min(a + 512, keys)
                        mm = pe.matmul(ps_s[:, p % 2, a:b], q, k[:, a:b], start=True, stop=True)
                    mm.then_inc(s_done, 1)

                def start(sec, J, Pn, G):
                    for part in range(len(sec.jobs[0].parts)):
                        scores(sec, 0, Pn, 0, part)

                def visit(sec, it, J, Pn, G, final):
                    jobs, groups = sec.jobs, sec.groups
                    first = before_of(sec)

                    def turn(n, gi):
                        p = first[n]
                        if gi == 0:
                            if len(jobs[n].parts) == 1:
                                pe.wait_ge(e_done, Pn + p + 3)
                            else:
                                pe.wait_ge(mixed, J + n + 1)
                        pe.wait_ge(t_out, G + n * len(groups) + gi + 1)
                        for m, kt in enumerate(groups[gi]):
                            mm = pe.transpose(ps_t[:, m * P:(m + 1) * P], pe4[:, p % 4, kt * P:(kt + 1) * P], g.ident)
                        mm.then_inc(t_done, 1)

                    def values(n, gi):
                        if gi == 0:
                            pe.wait_ge(o_out, J + n + 1)
                        pe.wait_ge(t_out, G + n * len(groups) + gi + 2)
                        for kt in groups[gi]:
                            mm = pe.matmul(ps_o[:, 0:P], pT[:, n % 2, kt * P:(kt + 1) * P], jobs[n].v[:, kt, :],
                                           start=kt == 0, stop=kt == sec.ntiles - 1)
                        if gi == len(groups) - 1:
                            mm.then_inc(o_done, 1)

                    for n in range(len(jobs)):
                        more = len(jobs[0].parts) if n + 1 < len(jobs) or not final else 0
                        if more:
                            scores(sec, it, Pn, n + 1, 0)
                        if n and more == 2:
                            values(n - 1, 0)
                        if more == 2:
                            scores(sec, it, Pn, n + 1, 1)
                        for gi in range(len(groups)):
                            turn(n, gi)
                            if n and not (more == 2 and gi == 0):
                                values(n - 1, gi)
                    for gi in range(len(groups)):
                        values(len(jobs) - 1, gi)

                walk(pe, visit, start)

            @block.scalar
            def _(act):
                act.sem_inc(e_done, 2)

                def exps(sec, J, Pn, G, n):
                    job, keys = sec.jobs[n % len(sec.jobs)], sec.ntiles * P
                    for part in range(len(job.parts)):
                        p = before_of(sec)[n] + part
                        act.wait_ge(m_ready, Pn + p + 1)
                        if len(job.parts) == 1:
                            act.wait_ge(o_done, J + n + 1)
                        elif n < 2:
                            act.wait_ge(o_out, J + 1)
                        else:
                            act.wait_ge(t_done, G + (n - 1) * len(sec.groups))
                        act.activation(pe4[:, p % 4, 0:keys], ps_s[:, p % 2, 0:keys], ACT.Exp, scale=sec.scale,
                                       bias=st[:, p % 4, 1:2], accum_out=st[:, p % 4, 2:3]).then_inc(e_done, 1)

                def visit(sec, it, J, Pn, G, final):
                    jobs, groups = sec.jobs, sec.groups
                    for n in range(len(jobs)):
                        act.wait_ge(t_done, G + n * len(groups) + 1)
                        act.wait_ge(o_done, J + n + 3)
                        w = len(groups[0]) * P
                        act.copy(pT[:, n % 2, 0:w], ps_t[:, 0:w]).then_inc(t_out, 1)
                        if n + 1 < len(jobs) or not final:
                            exps(sec, J, Pn, G, n + 1)

                walk(act, visit, lambda sec, J, Pn, G: exps(sec, J, Pn, G, 0))

            @block.vector
            def _(dve):
                dve.sem_inc(o_done, 4)
                dve.sem_inc(t_out, 1)
                dve.sem_inc(o_out, 1)

                def own():
                    dve.wait_ge(*c.now())

                def maxima(sec, Pn, n):
                    keys = sec.ntiles * P
                    for part in range(len(sec.jobs[0].parts)):
                        p = before_of(sec)[n] + part
                        dve.wait_ge(s_done, Pn + p + 2)
                        dve.tensor_reduce(st[:, p % 4, 0:1], ps_s[:, p % 2, 0:keys], AX.X, ALU.max).then_inc(*c.up())
                        own()
                        dve.tensor_scalar(st[:, p % 4, 1:2], st[:, p % 4, 0:1], -sec.scale, None, ALU.mult).then_inc(m_ready, 1)

                def visit(sec, it, J, Pn, G, final):
                    jobs, groups = sec.jobs, sec.groups
                    first, keys = before_of(sec), sec.ntiles * P
                    if len(jobs[0].parts) == 1:
                        dve.sem_inc(mixed, len(jobs))

                    def mix(n):
                        a, b = first[n] % 4, (first[n] + 1) % 4
                        dve.wait_ge(e_done, Pn + first[n] + 4)
                        dve.reciprocal(st[:, a, 3:4], st[:, a, 2:3]).then_inc(*c.up())
                        dve.reciprocal(st[:, b, 3:4], st[:, b, 2:3]).then_inc(*c.up())
                        own()
                        dve.tensor_scalar(st[:, b, 4:5], st[:, b, 3:4], neg_lam, None, ALU.mult).then_inc(*c.up())
                        own()
                        dve.tensor_scalar(pe4[:, b, 0:keys], pe4[:, b, 0:keys], st[:, b, 4:5], None, ALU.mult).then_inc(*c.up())
                        own()
                        dve.scalar_tensor_tensor(out=pe4[:, a, 0:keys], in0=pe4[:, a, 0:keys], scalar=st[:, a, 3:4],
                                                 in1=pe4[:, b, 0:keys], op0=ALU.mult, op1=ALU.add).then_inc(mixed, 1)

                    def weights_out(n):
                        for gi in range(1, len(groups)):
                            dve.wait_ge(t_done, G + n * len(groups) + gi + 1)
                            dve.wait_ge(o_done, J + n + 3)
                            a, w = groups[gi][0] * P, len(groups[gi]) * P
                            dve.tensor_copy(pT[:, n % 2, a:a + w], ps_t[:, 0:w]).then_inc(t_out, 1)

                    def result(n):
                        a = first[n] % 4
                        dve.wait_ge(o_done, J + n + 5)
                        if len(jobs[n].parts) == 1:
                            dve.reciprocal(st[:, a, 3:4], st[:, a, 2:3]).then_inc(*c.up())
                            own()
                            dve.tensor_scalar(jobs[n].out(it), ps_o[:, jobs[n].cols].unsqueeze(1), st[:, a, 3:4], None, ALU.mult).then_inc(o_out, 1)
                        else:
                            dve.tensor_copy(jobs[n].out(it), ps_o[:, jobs[n].cols].unsqueeze(1)).then_inc(o_out, 1)

                    for n in range(len(jobs)):
                        if len(jobs[n].parts) == 2:
                            mix(n)
                        if n + 1 < len(jobs) or not final:
                            maxima(sec, Pn, n + 1)
                        weights_out(n)
                        if n:
                            result(n - 1)
                    result(len(jobs) - 1)

                walk(dve, visit, lambda sec, J, Pn, G: maxima(sec, Pn, 0), c, 2)


class Section:
    def __init__(self, turns, ntiles, scale, jobs, stage, staged_before):
        self.turns, self.ntiles, self.scale, self.jobs, self.stage = turns, ntiles, scale, jobs, stage
        self.groups = [list(range(a, min(a + 4, ntiles))) for a in range(0, ntiles, 4)]
        self.staged_before = staged_before


def even_attend(nc, g, A, L):
    with nc.cleanup_on_exit():
        q = nc.alloc_sbuf_tensor("ea_q", [P, 2, 4, P], F32)

        def jobs(tile0):
            out = []
            for t2 in range(2):
                for hd in range(AH):
                    kv, rows = hd // 4, slice(64 * (hd // 4), 64 * (hd // 4) + 64)
                    out.append(Job([(q[rows, t2, hd % 4, :], L.kT[rows, :])], L.v, slice(kv * AD, kv * AD + AD),
                                   lambda it, t2=t2, hd=hd: L.cat[:, bass.ds(it * 2 + tile0 + t2, 1), hd * AD:(hd + 1) * AD], t2))
            return out

        def stage(tile0):
            return [(q[:, t2, :, :], lambda it, t2=t2: L.qT[:, :, bass.ds(it * 256 + (tile0 + t2) * P, P)]) for t2 in range(2)]

        attend(nc, g, "ea_", [Section(1, NTC, AD ** -0.5, jobs(0), stage(0), 0),
                              Section(NTL // 2, NT, AD ** -0.5, jobs(NTC), stage(NTC), 2)])


def broadcast_rows(pe, g, ps, col, done):
    for k in range(KD):
        mm = pe.matmul(ps[:, k * P:(k + 1) * P], col[:, k:k + 1].to_broadcast([P, P]), g.ident, start=True, stop=True)
    mm.then_inc(done, 1)


def mix_out(nc, g, A, layer, M, R):
    tag = f"mo{layer}_"

    def s(name):
        return nc.alloc_semaphore(tag + name)

    with nc.cleanup_on_exit():
        w = nc.alloc_sbuf_tensor(tag + "w", [P, KD, D], F32)
        wr = nc.alloc_sbuf_tensor(tag + "wr", [P, KD, P], F32)
        kinds = sorted({sec[2] for sec in M.sections})
        rows = nc.alloc_sbuf_tensor(tag + "rows", [P, 3 * len(kinds), D], F32)
        x = M.room[:, 0:2 * D].rearrange("p (h d) -> p h d", h=2)
        cr = M.room[:, 2 * D:4 * D].rearrange("p (h d) -> p h d", h=2)
        cT = nc.alloc_sbuf_tensor(tag + "cT", [P, 2, KD, P], F32)
        f = nc.alloc_sbuf_tensor(tag + "f", [P, 2, D], F32)
        fT = cT
        nh = M.tiles * M.heads
        ss, rs, s1, s2 = (nc.alloc_sbuf_tensor(tag + n, [P, nh], F32) for n in ("ss", "rs", "s1", "s2"))
        xs = nc.alloc_sbuf_tensor(tag + "xs", [P, 2, 8], F32)
        lg = nc.alloc_sbuf_tensor(tag + "lg", [P, 2, NE], F32)
        ps_c = nc.alloc_psum_tensor(tag + "ps_c", [P, 2, 512], F32)
        ps_o = nc.alloc_psum_tensor(tag + "ps_o", [P, D], F32)
        ps_f = nc.alloc_psum_tensor(tag + "ps_f", [P, 2, 512], F32)
        ps_r = nc.alloc_psum_tensor(tag + "ps_r", [P, 512], F32)
        ps_q = nc.alloc_psum_tensor(tag + "ps_q", [P, 512], F32)
        c = Count(nc, tag + "dve_step")
        w_in, r_in, wr_clear, row_mm, row_out = s("w_in"), s("r_in"), s("wr_clear"), s("row_mm"), s("row_out")
        x_in, gate_in, normed = [s("x_in0"), s("x_in1")], s("gate_in"), s("normed")
        x_st, f_st = [s("x_st0"), s("x_st1")], [s("f_st0"), s("f_st1")]
        copied, c_done, c_act, c_dve = s("copied"), s("c_done"), s("c_act"), s("c_dve")
        o_done, x_new, x_sq, f_ready = s("o_done"), s("x_new"), s("x_sq"), s("f_ready")
        f_done, f_act, f_dve, r_done, r_out = s("f_done"), s("f_act"), s("f_dve"), s("r_done"), s("r_out")

        def turns(eng, body, own=None, per=0):
            n = 0
            for count, tile0, kind in M.sections:
                if count == 1:
                    body(n, lambda h: tile0 + h, kind)
                else:
                    with eng.Fori(0, count) as i:
                        if own:
                            own.turn(i, per)
                        body(i + n, lambda h: i * 2 + (tile0 + h), kind)
                    if own:
                        own.turned(count)
                n += count
            return n

        with nc.Block() as block:

            @block.sync
            def _(sp):
                if M.gate is not None:
                    sp.dma_start(M.gate, M.gate_rows).then_inc(gate_in, 16)
                for k in range(KD):
                    sp.dma_start(w[:, k, :], M.w_out[k * P:(k + 1) * P, :]).then_inc(w_in, 16)
                sp.wait_ge(wr_clear, 1)
                sp.dma_start(wr[:, :, 0:NE], A["w_router"].rearrange("(k p) e -> p k e", p=P)).then_inc(r_in, 16)
                sp.wait_ge(normed, 1)

                def body(it, tile, kind):
                    for h in range(2):
                        sp.wait_ge(x_st[h], it * 16 + 16)
                        sp.wait_ge(f_st[h], it * 16 + 16)
                        sp.dma_start(x[:, h, :], M.x_rows(tile(h))).then_inc(x_in[h], 16)

                turns(sp, body)

            @block.gpsimd
            def _(pool):
                pool.wait_ge(normed, 1)

                def body(it, tile, kind):
                    for h in range(2):
                        pool.wait_ge(c_done, it * 4 + 2 * h + 2)
                        for n, rows_of in enumerate(M.halves):
                            pool.tensor_copy(cr[:, h:h + 1, n * 512:(n + 1) * 512], rows_of(tile(h))).then_inc(copied, 1)

                turns(pool, body)

            @block.tensor
            def _(pe):
                n = 0
                for kind in kinds:
                    for col in (g.mod[:, layer * 48 + V_G1 * KD:layer * 48 + V_G1 * KD + KD, kind],
                                g.gain[:, layer, 1, :, kind],
                                g.mod[:, layer * 48 + V_SH2 * KD:layer * 48 + V_SH2 * KD + KD, kind]):
                        if n > 1:
                            pe.wait_ge(row_out, n - 1)
                        broadcast_rows(pe, g, (ps_o, ps_c[:, :, :].rearrange("p a n -> p (a n)"))[n % 2], col, row_mm)
                        n += 1
                pe.wait_ge(row_out, n)
                pe.wait_ge(w_in, 16 * KD)
                pe.wait_ge(r_in, 16)
                pe.sem_inc(c_done, 4)
                pe.sem_inc(r_done, 1)
                pe.sem_inc(f_done, 1)

                def body(it, tile, kind):
                    def cat(h):
                        pe.wait_ge(copied, it * 4 + 2 * h + 2)
                        pe.wait_ge(c_act, it * 2 + h + 1)
                        pe.wait_ge(c_dve, it * 2 + h + 1)
                        for half in range(2):
                            for k in range(4 * half, 4 * half + 4):
                                mm = pe.transpose(ps_c[:, half, (k % 4) * P:(k % 4) * P + P], cr[:, h, k * P:(k + 1) * P], g.ident)
                            mm.then_inc(c_done, 1)
                        pe.wait_ge(c_act, it * 2 + h + 2)
                        pe.wait_ge(c_dve, it * 2 + h + 2)
                        pe.wait_ge(x_new, it * 2 + h + 2)
                        for half in range(2):
                            for k in range(KD):
                                mm = pe.matmul(ps_o[:, half * 512:(half + 1) * 512], cT[:, h, k, :], w[:, k, half * 512:(half + 1) * 512],
                                               start=k == 0, stop=k == KD - 1)
                        mm.then_inc(o_done, 1)

                    def router(h):
                        pe.wait_ge(f_ready, it * 2 + h + 1)
                        pe.wait_ge(f_act, it * 3 + 2 * h + 1)
                        pe.wait_ge(f_dve, it + 1)
                        for half in range(2):
                            for k in range(4 * half, 4 * half + 4):
                                mm = pe.transpose(ps_f[:, half, (k % 4) * P:(k % 4) * P + P], f[:, h, k * P:(k + 1) * P], g.ident)
                            mm.then_inc(f_done, 1)
                        pe.wait_ge(f_act, it * 3 + h + 3)
                        pe.wait_ge(f_dve, it + h + 1)
                        pe.wait_ge(r_out, it * 2 + h + 1)
                        for k in range(KD):
                            mm = pe.matmul(ps_r[:, 0:P], fT[:, h, k, :], wr[:, k, :], start=k == 0, stop=k == KD - 1)
                        mm.then_inc(r_done, 1)

                    cat(0)
                    cat(1)
                    router(0)
                    router(1)

                turns(pe, body)

            @block.scalar
            def _(act):
                act.sem_inc(c_act, 1)
                act.sem_inc(f_act, 1)
                act.sem_inc(r_out, 1)
                for h in range(2):
                    act.sem_inc(x_st[h], 16)
                    act.sem_inc(f_st[h], 16)

                def body(it, tile, kind):
                    for h in range(2):
                        act.wait_ge(c_done, it * 4 + 2 * h + 5)
                        act.wait_ge(r_done, it * 2 + 1)
                        act.copy(cT[:, h, 0:4, :], ps_c[:, 0, :].rearrange("p (k t) -> p k t", t=P)).then_inc(c_act, 1)
                    for h in range(2):
                        act.wait_ge(x_new, it * 2 + h + 3)
                        act.activation(f[:, h, :], x[:, h, :], ACT.Square, accum_out=xs[:, h, 0:1]).then_inc(x_sq, 1)
                        act.dma_start(M.x_rows(tile(h)), x[:, h, :]).then_inc(x_st[h], 16)
                        if h == 0:
                            act.wait_ge(f_ready, it * 2 + 1)
                            act.dma_start(R.f_dram[bass.ds(tile(0) * P, P), :], f[:, 0, :]).then_inc(f_st[0], 16)
                    for h in range(2):
                        for half in range(2 - h):
                            act.wait_ge(f_done, it * 4 + 2 * h + half + 2)
                            act.wait_ge(o_done, it * 2 + h + 1)
                            act.copy(fT[:, h, 4 * half:4 * half + 4, :], ps_f[:, half, :].rearrange("p (k t) -> p k t", t=P)).then_inc(f_act, 1)
                        if h == 1:
                            act.dma_start(R.f_dram[bass.ds(tile(1) * P, P), :], f[:, 1, :]).then_inc(f_st[1], 16)
                        act.wait_ge(r_done, it * 2 + h + 2)
                        act.activation(lg[:, h, :], ps_r[:, 0:NE], ACT.Tanh, scale=0.5).then_inc(r_out, 1)

                n = turns(act, body)
                for h in range(2):
                    act.wait_ge(x_st[h], n * 16 + 16)
                    act.wait_ge(f_st[h], n * 16 + 16)

            @block.vector
            def _(dve):
                def own():
                    dve.wait_ge(*c.now())

                dve.memset(wr[:, :, :], 0.0).then_inc(wr_clear, 1)
                hd = M.rows.shape[2] // M.heads
                sq4, row4 = (ap.rearrange("p t (n d) -> p t n d", d=hd) for ap in (M.scratch, M.rows))
                wide = [P, M.tiles, M.heads, hd]
                dve.tensor_tensor(sq4, row4, row4, ALU.mult).then_inc(*c.up())
                own()
                dve.tensor_reduce(ss[:, :].rearrange("p (t n) -> p t n", t=M.tiles), sq4, AX.X, ALU.add).then_inc(*c.up())
                own()
                dve.tensor_scalar(ss[:, :], ss[:, :], 1.0 / hd, EPS, ALU.mult, ALU.add).then_inc(*c.up())
                rstd(dve, c, rs[:, :], ss[:, :], s1[:, :], s2[:, :])
                own()
                dve.tensor_tensor(row4, row4, rs[:, :].rearrange("p (t n) -> p t n", t=M.tiles).unsqueeze(3).to_broadcast(wide), ALU.mult).then_inc(*c.up())
                own()
                dve.tensor_tensor(row4, row4, M.gain, ALU.mult).then_inc(*c.up())
                if M.gate is not None:
                    dve.wait_ge(gate_in, 16)
                    dve.tensor_scalar(M.gate, M.gate, 0.5, 0.5, ALU.mult, ALU.add).then_inc(*c.up())
                    own()
                    dve.tensor_tensor(M.rows, M.rows, M.gate, ALU.mult).then_inc(*c.up())
                own()
                dve.sem_inc(normed, 1)
                for n in range(3 * len(kinds)):
                    dve.wait_ge(row_mm, n + 1)
                    dve.tensor_copy(rows[:, n, :], (ps_o[:, :], ps_c[:, :, :].rearrange("p a n -> p (a n)"))[n % 2]).then_inc(row_out, 1)
                dve.sem_inc(c_dve, 1)
                dve.sem_inc(f_dve, 1)
                dve.sem_inc(x_new, 2)

                def body(it, tile, kind):
                    base = 3 * kinds.index(kind)
                    for h in range(2):
                        dve.wait_ge(c_done, it * 4 + 2 * h + 6)
                        dve.wait_ge(r_done, it * 2 + 1)
                        dve.tensor_copy(cT[:, h, 4:8, :], ps_c[:, 1, :].rearrange("p (k t) -> p k t", t=P)).then_inc(c_dve, 1)
                    for h in range(2):
                        dve.wait_ge(o_done, it * 2 + h + 1)
                        dve.wait_ge(x_in[h], it * 16 + 16)
                        dve.wait_ge(f_st[h], it * 16 + 16)
                        dve.wait_ge(f_done, it * 4 + 1)
                        dve.tensor_tensor(f[:, h, :], ps_o[:, :], rows[:, base, :], ALU.mult).then_inc(*c.up())
                        own()
                        dve.tensor_tensor(x[:, h, :], x[:, h, :], f[:, h, :], ALU.add).then_inc(x_new, 1)
                        dve.wait_ge(x_sq, it * 2 + h + 1)
                        dve.tensor_scalar(xs[:, h, 1:2], xs[:, h, 0:1], 1.0 / D, EPS, ALU.mult, ALU.add).then_inc(*c.up())
                        rstd(dve, c, xs[:, h, 2:3], xs[:, h, 1:2], xs[:, h, 3:4], xs[:, h, 4:5])
                        own()
                        dve.scalar_tensor_tensor(out=f[:, h, :], in0=x[:, h, :], scalar=xs[:, h, 2:3], in1=rows[:, base + 1, :],
                                                 op0=ALU.mult, op1=ALU.mult).then_inc(*c.up())
                        own()
                        dve.tensor_tensor(f[:, h, :], f[:, h, :], rows[:, base + 2, :], ALU.add).then_inc(f_ready, 1)
                    dve.wait_ge(f_done, it * 4 + 5)
                    dve.wait_ge(o_done, it * 2 + 2)
                    dve.tensor_copy(fT[:, 1, 4:8, :], ps_f[:, 1, :].rearrange("p (k t) -> p k t", t=P)).then_inc(f_dve, 1)
                    dve.wait_ge(r_out, it * 2 + 3)
                    for h in range(2):
                        dve.tensor_scalar(R.scores[:, bass.ds(tile(h), 1), :], lg[:, h, :].unsqueeze(1), 0.5, 0.5, ALU.mult, ALU.add).then_inc(*c.up())

                turns(dve, body, c, 2 * (1 + 1 + RSTD_N + 1 + 1))


def even_mix(g, A, L, h_dram=None):
    M = Shared()
    M.sections = [(1, 0, 1), (NTL // 2, NTC, 0)]
    M.w_out = A["e_w_out"][0]
    M.x_rows = lambda t: g.x_dram[bass.ds(t * P, P), :]
    M.tiles, M.heads, M.rows = NT, BH, L.hb[:, :, :]
    M.gain = g.bc["e_g_h"].rearrange("p (n d) -> p n d", d=BD).unsqueeze(1).to_broadcast([P, NT, BH, BD])
    M.gate = L.qT[:, :, :].rearrange("p a t -> p (a t)").rearrange("p (n d) -> p n d", d=BW)
    M.gate_rows = g.vo_dram[:, BW:2 * BW].rearrange("(t p) n -> p t n", p=P)
    M.room = L.zT[:, 4:8, :].rearrange("p a t -> p (a t)")
    M.scratch = M.room.rearrange("p (n d) -> p n d", d=BW)
    M.halves = (lambda t: L.cat[:, bass.ds(t, 1), :], lambda t: L.hb[:, bass.ds(t, 1), :])
    return M


def odd_project(nc, g, A, L):
    QK = 2 * CW
    NH = QK // CD
    RUNS = ((0, CW), (CW, QK), (QK, QK + CW), (QK + CW, IN_ODD))

    def s(name):
        return nc.alloc_semaphore("op_" + name)

    with nc.cleanup_on_exit():
        w = nc.alloc_sbuf_tensor("op_w", [P, KD, IN_ODD], F32)
        x = nc.alloc_sbuf_tensor("op_x", [P, 2, D], F32)
        hT = nc.alloc_sbuf_tensor("op_hT", [P, 2, KD, P], F32)
        qk = nc.alloc_sbuf_tensor("op_qk", [P, QK], F32)
        S = Shared()
        S.sq, S.nrm, gains = L.spare[:, 0:QK], L.spare[:, QK:2 * QK], L.spare[:, 2 * QK:3 * QK]
        gqk = gains.rearrange("p (n d) -> p n d", d=CD)
        qkr = S.sq
        S.ra = nc.alloc_sbuf_tensor("op_ra", [P, NH, CD // 2], F32)
        S.rb = nc.alloc_sbuf_tensor("op_rb", [P, NH, CD // 2], F32)
        S.ss = nc.alloc_sbuf_tensor("op_ss", [P, 16], F32)
        S.r = nc.alloc_sbuf_tensor("op_r", [P, 16], F32)
        S.s1 = nc.alloc_sbuf_tensor("op_s1", [P, 16], F32)
        S.s2 = nc.alloc_sbuf_tensor("op_s2", [P, 16], F32)
        xs = nc.alloc_sbuf_tensor("op_xs", [P, 2, 8], F32)
        ps_ab = nc.alloc_psum_tensor("op_ps_ab", [P, 2, 2, 512], F32)
        ps_r = nc.alloc_psum_tensor("op_ps_r", [P, 4, 512], F32)
        w_in, x_sq, xh_ready, g_in = s("w_in"), s("x_sq"), s("xh_ready"), s("g_in")
        x_in = [s("x_in0"), s("x_in1")]
        t_done, h_act, h_dve = s("t_done"), s("h_act"), s("h_dve")
        r_done, r_act, r_dve = s("r_done"), s("r_act"), s("r_dve")
        qk_ready, qt_done, qt_act, qt_dve = s("qk_ready"), s("qt_done"), s("qt_act"), s("qt_dve")
        c = Count(nc, "op_dve_step")
        with nc.Block() as block:

            @block.sync
            def _(sp):
                for k in range(KD):
                    sp.dma_start(w[:, k, :], A["o_w_in"][0, k * P:(k + 1) * P, :]).then_inc(w_in, 16)
                for name, (at, width) in GO.items():
                    src = A[name].rearrange("a b d -> a (b d)") if name == "o_lam" else A[name]
                    sp.dma_start(L.go[:, at:at + width], src.partition_broadcast(P)).then_inc(g_in, 16)
                for h in range(2):
                    sp.dma_start(x[:, h, :], g.x_dram[h * P:(h + 1) * P, :]).then_inc(x_in[h], 16)
                with sp.Fori(0, PAIRS - 1) as j:
                    for h in range(2):
                        sp.wait_ge(t_done, j * 4 + 2 * h + 2)
                        sp.dma_start(x[:, h, :], g.x_dram[bass.ds(j * 256 + (2 + h) * P, P), :]).then_inc(x_in[h], 16)

            @block.tensor
            def _(pe):
                pe.sem_inc(qt_done, 1)

                def transposes(i, h):
                    pe.wait_ge(xh_ready, i * 2 + h + 1)
                    if not isinstance(i, int) or i > 0:
                        pe.wait_ge(qt_act, i * 2 + h - 1)
                        pe.wait_ge(qt_dve, i * 2 + h - 1)
                    for half in range(2):
                        for k in range(4 * half, 4 * half + 4):
                            mm = pe.transpose(ps_ab[:, h, half, (k % 4) * P:(k % 4) * P + P], x[:, h, k * P:(k + 1) * P], g.ident)
                        mm.then_inc(t_done, 1)

                def rows(i, h, groups):
                    pe.wait_ge(h_act, i * 2 + h + 1)
                    pe.wait_ge(h_dve, i * 2 + h + 1)
                    for n in groups:
                        a, b = RUNS[n]
                        pe.wait_ge((r_act, r_dve)[n % 2], i * 4 + 2 * h + 1 + n // 2)
                        for k in range(KD):
                            mm = pe.matmul(ps_r[:, n, 0:b - a], hT[:, h, k, :], w[:, k, a:b], start=k == 0, stop=k == KD - 1)
                        mm.then_inc(r_done, 1)

                def turn_qk(i, h):
                    pe.wait_ge(qk_ready, i * 2 + h + 2)
                    if not place_of(i, h)[1]:
                        pe.wait_ge(x_sq, i * 2 + h + 3)
                    for half in range(2):
                        for j in range(4):
                            mm = pe.transpose(ps_ab[:, h, half, j * P:(j + 1) * P], qkr[:, half * CW + j * P:half * CW + (j + 1) * P], g.ident)
                    mm.then_inc(qt_done, 1)

                pe.wait_ge(w_in, 16 * KD)

                def tile(i, h):
                    first, final, last, before, after = place_of(i, h)
                    rows(i, h, (0, 1))
                    if not first:
                        turn_qk(*before)
                    rows(i, h, (2,))
                    if not last:
                        transposes(*after)
                    rows(i, h, (3,))

                transposes(0, 0)
                walk_tiles(pe, tile)
                turn_qk(PAIRS - 1, 1)

            @block.scalar
            def _(act):
                act.sem_inc(r_act, 2)
                act.sem_inc(qk_ready, 1)

                def squares(i, h):
                    act.wait_ge(x_in[h], i * 16 + 16)
                    if not isinstance(i, int) or i > 0:
                        act.wait_ge(h_dve, i * 2 + h - 1)
                        act.wait_ge(h_act, i * 2 + h - 1)
                    act.activation(ps_ab[:, h, :, :].rearrange("p a n -> p (a n)"), x[:, h, :], ACT.Square,
                                   accum_out=xs[:, h, 0:1]).then_inc(x_sq, 1)

                def modulate(i, h):
                    act.wait_ge(t_done, i * 4 + 2 * h + 1)
                    for k in range(4):
                        gain, shift = modulation_of(g, 1, i, h, k)
                        m = act.activation(hT[:, h, k, :], ps_ab[:, h, 0, k * P:(k + 1) * P], ACT.Identity, scale=gain, bias=shift)
                    m.then_inc(h_act, 1)

                def rows_out(i, h):
                    act.wait_ge(r_done, i * 8 + 4 * h + 1)
                    act.wait_ge(qk_ready, i * 2 + h + 1)
                    act.copy(qk[:, 0:CW], ps_r[:, 0, :]).then_inc(r_act, 1)

                def v_out(i, h):
                    act.wait_ge(r_done, i * 8 + 4 * h + 3)
                    act.copy(L.vc[:, bass.ds(i * 2 + h, 1), :], ps_r[:, 2:3, :]).then_inc(r_act, 1)

                def q_out(i, h):
                    act.wait_ge(qt_done, i * 2 + h + 2)
                    act.copy(L.qcT[:, :, bass.ds(i * 256 + h * P, P)],
                             ps_ab[:, h, 0, :].rearrange("p (a n) -> p a n", n=P)).then_inc(qt_act, 1)

                def tile(i, h):
                    first, final, last, before, after = place_of(i, h)
                    rows_out(i, h)
                    if not first:
                        q_out(*before)
                    v_out(i, h)
                    if not last:
                        modulate(*after)
                    if not final:
                        squares(i + 1, h)

                squares(0, 0)
                squares(0, 1)
                modulate(0, 0)
                walk_tiles(act, tile)
                q_out(PAIRS - 1, 1)

            @block.vector
            def _(dve):
                dve.sem_inc(r_dve, 2)
                dve.wait_ge(g_in, 16 * len(GO))
                dve.tensor_copy(gqk[:, 0:NH // 2, :], L.gain["o_g_qc"].unsqueeze(1).to_broadcast([P, NH // 2, CD])).then_inc(*c.up())
                dve.tensor_copy(gqk[:, NH // 2:, :], L.gain["o_g_kc"].unsqueeze(1).to_broadcast([P, NH // 2, CD])).then_inc(*c.up())

                def normalise(i, h):
                    dve.wait_ge(x_sq, i * 2 + h + 1)
                    dve.tensor_scalar(xs[:, h, 1:2], xs[:, h, 0:1], 1.0 / D, EPS, ALU.mult, ALU.add).then_inc(*c.up())
                    rstd(dve, c, xs[:, h, 2:3], xs[:, h, 1:2], xs[:, h, 3:4], xs[:, h, 4:5])
                    dve.wait_ge(*c.now())
                    dve.tensor_scalar(x[:, h, :], x[:, h, :], xs[:, h, 2:3], None, ALU.mult).then_inc(xh_ready, 1)

                def modulate(i, h):
                    dve.wait_ge(t_done, i * 4 + 2 * h + 2)
                    for k in range(4, 8):
                        gain, shift = modulation_of(g, 1, i, h, k)
                        m = dve.tensor_scalar(hT[:, h, k, :], ps_ab[:, h, 1, (k - 4) * P:(k - 3) * P], gain, shift, ALU.mult, ALU.add)
                    m.then_inc(h_dve, 1)

                def rows_out(i, h):
                    dve.wait_ge(r_done, i * 8 + 4 * h + 2)
                    dve.tensor_copy(qk[:, CW:QK], ps_r[:, 1, :]).then_inc(r_dve, 1)

                def norm_rope(i, h):
                    dve.wait_ge(r_act, i * 4 + 2 * h + 3)
                    dve.wait_ge(r_dve, i * 4 + 2 * h + 3)
                    dve.wait_ge(qt_done, i * 2 + h + 1)
                    head_norm_rope(dve, c, g, S, NH, CD, gqk, True, qk[:, :], None)
                    n3 = S.nrm.rearrange("p (n d) -> p n d", d=CD)
                    o3 = qkr.rearrange("p (n d) -> p n d", d=CD)
                    cos = g.rope[:, bass.ds(i * 2 + h, 1), 0:32].to_broadcast([P, NH, 32])
                    sin = g.rope[:, bass.ds(i * 2 + h, 1), 32:64].to_broadcast([P, NH, 32])
                    rope_pairs(dve, c, S, n3, o3, cos, sin)
                    dve.wait_ge(*c.now())
                    dve.sem_inc(qk_ready, 1)

                def latent_out(i, h):
                    dve.wait_ge(r_done, i * 8 + 4 * h + 4)
                    dve.tensor_copy(L.zl[:, bass.ds(i * 2 + h, 1), :], ps_r[:, 3:4, 0:IN_ODD - 3 * CW]).then_inc(r_dve, 1)

                def k_out(i, h):
                    dve.wait_ge(qt_done, i * 2 + h + 2)
                    dve.tensor_copy(L.kcT[:, :, bass.ds(i * 256 + h * P, P)],
                                    ps_ab[:, h, 1, :].rearrange("p (a n) -> p a n", n=P)).then_inc(qt_dve, 1)

                def tile(i, h):
                    first, final, last, before, after = place_of(i, h)
                    rows_out(i, h)
                    if not first:
                        k_out(*before)
                    norm_rope(i, h)
                    if not last:
                        modulate(*after)
                    latent_out(i, h)
                    if not final:
                        normalise(i + 1, h)

                normalise(0, 0)
                normalise(0, 1)
                modulate(0, 0)
                walk_tiles(dve, tile, c, 2 * (1 + RSTD_N) + 2 * (HEAD_NORM_N + ROPE_N))
                k_out(PAIRS - 1, 1)


def odd_latent(nc, g, A, L):
    NH = 2 * DH
    QW = DH * DK

    def s(name):
        return nc.alloc_semaphore("ol_" + name)

    with nc.cleanup_on_exit():
        wuq = nc.alloc_sbuf_tensor("ol_wuq", [P, DQL // P, QW], F32)
        wukv = nc.alloc_sbuf_tensor("ol_wukv", [P, DH * (DN + DV)], F32)
        zs = nc.alloc_sbuf_tensor("ol_zs", [P, 2, DQL + DKL], F32)
        zT = nc.alloc_sbuf_tensor("ol_zT", [P, 2, 3, P], F32)
        qk = nc.alloc_sbuf_tensor("ol_qk", [P, 2, NH, DK], F32)
        qkr = nc.alloc_sbuf_tensor("ol_qkr", [P, 2, NH, P], F32)
        gqk = nc.alloc_sbuf_tensor("ol_gqk", [P, 2, NH, DK], F32)
        S = Shared()
        S.sq, S.nrm = L.spare[:, 0:2 * NH * DK], L.spare[:, 2 * NH * DK:4 * NH * DK]
        S.ra = nc.alloc_sbuf_tensor("ol_ra", [P, NH, DR // 2], F32)
        S.rb = nc.alloc_sbuf_tensor("ol_rb", [P, NH, DR // 2], F32)
        S.ss, S.r, S.s1, S.s2 = (nc.alloc_sbuf_tensor("ol_" + n, [P, 2 * NT], F32) for n in ("ss", "r", "s1", "s2"))
        e12 = nc.alloc_sbuf_tensor("ol_e12", [P, 2], F32)
        ps_t = nc.alloc_psum_tensor("ol_ps_t", [P, 512], F32)
        ps_u = nc.alloc_psum_tensor("ol_ps_u", [P, 3, 512], F32)
        ps_x = nc.alloc_psum_tensor("ol_ps_x", [P, 2, 2, 512], F32)
        c = Count(nc, "ol_dve_step")
        w_in, lam_sum, lam_exp = s("w_in"), s("lam_sum"), s("lam_exp")
        zs_ready, t_done, t_out, u_done, u_act, u_dve = s("zs_ready"), s("t_done"), s("t_out"), s("u_done"), s("u_act"), s("u_dve")
        qk_ready, x_done, x_act, x_dve = s("qk_ready"), s("x_done"), s("x_act"), s("x_dve")

        def walk(eng, turn, c=None, per=0):
            with eng.Fori(0, PAIRS - 1) as i:
                if c:
                    c.turn(i, per)
                turn(i, False)
            if c:
                c.turned(PAIRS - 1)
            turn(PAIRS - 1, True)

        with nc.Block() as block:

            @block.sync
            def _(sp):
                sp.dma_start(wuq[:, :, :], A["o_w_uq"][0].rearrange("(k p) n -> p k n", p=P)).then_inc(w_in, 16)
                sp.dma_start(wukv[:, :], A["o_w_ukv"][0]).then_inc(w_in, 16)

            @block.tensor
            def _(pe):
                pe.sem_inc(t_done, 2)
                pe.sem_inc(u_done, 2)
                pe.sem_inc(x_done, 1)
                pe.wait_ge(w_in, 32)

                def turn_rows(i):
                    for h in range(2):
                        pe.wait_ge(zs_ready, i * 2 + h + 1)
                        pe.wait_ge(t_out, i * 2 + h + 1)
                        for k in range(3):
                            mm = pe.transpose(ps_t[:, k * P:(k + 1) * P], zs[:, h, k * P:(k + 1) * P], g.ident)
                        mm.then_inc(t_done, 1)

                def turn(i, final):
                    for h in range(2):
                        pe.wait_ge(t_out, i * 2 + h + 2)
                        pe.wait_ge(u_act, i * 2 + h + 1)
                        pe.wait_ge(u_dve, i * 2 + h + 1)
                        for k in range(2):
                            pe.matmul(ps_u[:, 0, 0:QW], zT[:, h, k, :], wuq[:, k, :], start=k == 0, stop=k == 1)
                        for n in range(2):
                            mm = pe.matmul(ps_u[:, 1 + n, 0:2 * (DN + DV)], zT[:, h, 2, :], wukv[:, n * 2 * (DN + DV):(n + 1) * 2 * (DN + DV)],
                                           start=True, stop=True)
                        mm.then_inc(u_done, 1)
                    if not final:
                        turn_rows(i + 1)
                    for h in range(2):
                        pe.wait_ge(qk_ready, i + 2)
                        pe.wait_ge(x_act, i * 2 + h + 1)
                        pe.wait_ge(x_dve, i * 2 + h + 1)
                        for n in range(NH):
                            mm = pe.transpose(ps_x[:, h, n // 4, (n % 4) * P:(n % 4) * P + P], qkr[:, h, n, :], g.ident)
                        mm.then_inc(x_done, 1)

                turn_rows(0)
                walk(pe, turn)

            @block.scalar
            def _(act):
                act.sem_inc(x_act, 2)
                act.sem_inc(t_out, 1)
                act.sem_inc(u_act, 1)
                act.wait_ge(lam_sum, 1)
                act.activation(e12[:, :], e12[:, :], ACT.Exp).then_inc(lam_exp, 1)

                def rows_out(i):
                    for h in range(2):
                        act.wait_ge(t_done, i * 2 + h + 3)
                        act.wait_ge(u_done, i * 2 + h + 1)
                        act.copy(zT[:, h, :, :], ps_t[:, 0:3 * P].rearrange("p (k t) -> p k t", t=P)).then_inc(t_out, 1)

                def turn(i, final):
                    for h in range(2):
                        act.wait_ge(u_done, i * 2 + h + 3)
                        act.wait_ge(qk_ready, i + 1)
                        act.copy(qk[:, h, 0:DH, :], ps_u[:, 0, 0:QW].rearrange("p (n d) -> p n d", d=DK))
                        kv = ps_u[:, 1, 0:2 * (DN + DV)].rearrange("p (n d) -> p n d", d=DN + DV)
                        act.copy(qk[:, h, DH:DH + 2, 0:DN], kv[:, :, 0:DN])
                        act.copy(L.vd[:, bass.ds(i * 2 + h, 1), 0:2 * DV].rearrange("p o (n d) -> p (o n) d", d=DV), kv[:, :, DN:]).then_inc(u_act, 1)
                    if not final:
                        rows_out(i + 1)
                    for h in range(2):
                        act.wait_ge(x_done, i * 2 + h + 2)
                        act.copy(L.qdT[:, :, bass.ds(i * 256 + h * P, P)],
                                 ps_x[:, h, 0, :].rearrange("p (a n) -> p a n", n=P)).then_inc(x_act, 1)

                rows_out(0)
                walk(act, turn)

            @block.vector
            def _(dve):
                def own():
                    dve.wait_ge(*c.now())

                dve.sem_inc(x_dve, 2)
                dve.sem_inc(u_dve, 1)
                dve.sem_inc(qk_ready, 1)
                dve.memset(qkr[:, :, :, :], 0.0).then_inc(*c.up())
                for h in range(2):
                    dve.tensor_copy(gqk[:, h, 0:DH, :], L.gain["o_g_qd"].unsqueeze(1).to_broadcast([P, DH, DK])).then_inc(*c.up())
                    dve.tensor_copy(gqk[:, h, DH:, :], L.gain["o_g_kd"].unsqueeze(1).to_broadcast([P, DH, DK])).then_inc(*c.up())
                lam = L.gain["o_lam"].rearrange("p (a b d) -> p a b d", a=2, b=2)
                prod = S.sq[:, 0:2 * CD].rearrange("p (a d) -> p a d", a=2)
                dve.tensor_tensor(prod, lam[:, :, 0, :], lam[:, :, 1, :], ALU.mult).then_inc(*c.up())
                own()
                dve.tensor_reduce(e12[:, :], prod, AX.X, ALU.add).then_inc(lam_sum, 1)
                dve.tensor_scalar(L.gain["o_g_sub"], L.gain["o_g_sub"], 1.0 - LAM_INIT, None, ALU.mult).then_inc(*c.up())
                dve.wait_ge(lam_exp, 1)
                dve.tensor_tensor(L.neg_lam[:, :], e12[:, 1:2], e12[:, 0:1], ALU.subtract).then_inc(*c.up())
                own()
                dve.tensor_scalar(L.neg_lam[:, :], L.neg_lam[:, :], LAM_INIT, None, ALU.subtract).then_inc(*c.up())
                own()
                sq = L.spare[:, 0:NT * (DQL + DKL)].rearrange("p (t n) -> p t n", t=NT)
                dve.tensor_tensor(sq, L.zl[:, :, 0:DQL + DKL], L.zl[:, :, 0:DQL + DKL], ALU.mult).then_inc(*c.up())
                parts = ((0, DQL), (DQL, DKL))
                for n, (a, width) in enumerate(parts):
                    own()
                    dve.tensor_reduce(S.ss[:, n * NT:(n + 1) * NT], sq[:, :, a:a + width], AX.X, ALU.add).then_inc(*c.up())
                    own()
                    dve.tensor_scalar(S.ss[:, n * NT:(n + 1) * NT], S.ss[:, n * NT:(n + 1) * NT], 1.0 / width, EPS, ALU.mult, ALU.add).then_inc(*c.up())
                rstd(dve, c, S.r[:, :], S.ss[:, :], S.s1[:, :], S.s2[:, :])
                own()
                for n, (a, width) in enumerate(parts):
                    part = L.zl[:, :, a:a + width]
                    dve.tensor_tensor(part, part, S.r[:, n * NT:(n + 1) * NT].unsqueeze(2).to_broadcast([P, NT, width]), ALU.mult).then_inc(*c.up())
                flat = "p t n d -> p (t n d)"

                def rows_of(i):
                    for h in range(2):
                        dve.wait_ge(t_done, i * 2 + h + 1)
                        own()
                        dve.tensor_tensor(zs[:, h:h + 1, 0:DQL], L.zl[:, bass.ds(i * 2 + h, 1), 0:DQL], L.gain["o_g_cq"].unsqueeze(1), ALU.mult).then_inc(*c.up())
                        dve.tensor_tensor(zs[:, h:h + 1, DQL:], L.zl[:, bass.ds(i * 2 + h, 1), DQL:DQL + DKL], L.gain["o_g_ckv"].unsqueeze(1), ALU.mult).then_inc(*c.up())
                        own()
                        dve.sem_inc(zs_ready, 1)

                def turn(i, final):
                    for h in range(2):
                        dve.wait_ge(u_done, i * 2 + h + 3)
                        kv = ps_u[:, 2, 0:2 * (DN + DV)].rearrange("p (n d) -> p n d", d=DN + DV)
                        dve.tensor_copy(qk[:, h, DH + 2:NH, 0:DN], kv[:, :, 0:DN]).then_inc(*c.up())
                        dve.tensor_copy(L.vd[:, bass.ds(i * 2 + h, 1), 2 * DV:].rearrange("p o (n d) -> p (o n) d", d=DV), kv[:, :, DN:]).then_inc(*c.up())
                        dve.tensor_copy(qk[:, h, DH:NH, DN:DK], L.zl[:, bass.ds(i * 2 + h, 1), DQL + DKL:].to_broadcast([P, DH, DR])).then_inc(*c.up())
                        own()
                        dve.sem_inc(u_dve, 1)
                    if not final:
                        rows_of(i + 1)
                    dve.wait_ge(u_act, i * 2 + 3)
                    dve.wait_ge(x_done, i * 2 + 1)
                    head_norm_rope(dve, c, g, S, 2 * NH, DK, gqk[:, :, :, :].rearrange("p t n d -> p (t n) d"), True, qk[:, :, :, :].rearrange(flat), None)
                    n4 = S.nrm.rearrange("p (t n d) -> p t n d", t=2, d=DK)
                    own()
                    for h in range(2):
                        dve.tensor_copy(qkr[:, h, :, 0:DN], n4[:, h, :, 0:DN]).then_inc(*c.up())
                        cos = g.rope[:, bass.ds(i * 2 + h, 1), 64:80].to_broadcast([P, NH, 16])
                        sin = g.rope[:, bass.ds(i * 2 + h, 1), 80:96].to_broadcast([P, NH, 16])
                        rope_pairs(dve, c, S, n4[:, h, :, DN:DK], qkr[:, h, :, DN:DK], cos, sin)
                    own()
                    dve.sem_inc(qk_ready, 1)
                    for h in range(2):
                        dve.wait_ge(x_done, i * 2 + h + 2)
                        dve.tensor_copy(L.kdT[:, :, bass.ds(i * 256 + h * P, P)],
                                        ps_x[:, h, 1, :].rearrange("p (a n) -> p a n", n=P)).then_inc(x_dve, 1)

                rows_of(0)
                walk(dve, turn, c, 4 + 6 + HEAD_NORM_N + 2 + 2 * ROPE_N)


def odd_attend(nc, g, A, L):
    with nc.cleanup_on_exit():
        q = nc.alloc_sbuf_tensor("oa_q", [P, 2, 4, P], F32)

        def out(t2, at):
            return lambda it: L.cat[:, bass.ds(it * 2 + t2, 1), at:at + P]

        mla = [Job([(q[:, t2, hd, :], L.kdT[:, hd, :])], L.vd[:, :, hd * DV:(hd + 1) * DV], slice(0, DV), out(t2, CW + hd * DV), t2)
               for t2 in range(2) for hd in range(DH)]
        diff = [Job([(q[rows, t2, hd, :], L.kcT[rows, hd, :]) for rows in (slice(0, 64), slice(64, 128))],
                    L.vc[:, :, hd * CV:(hd + 1) * CV], slice(0, CV), out(t2, hd * CV), t2)
                for t2 in range(2) for hd in range(CH)]

        def stage(qT):
            return [(q[:, t2, :, :], lambda it, t2=t2: qT[:, :, bass.ds(it * 256 + (NTC + t2) * P, P)]) for t2 in range(2)]

        attend(nc, g, "oa_", [Section(NTL // 2, NT, DK ** -0.5, mla, stage(L.qdT), 0),
                              Section(NTL // 2, NT, CD ** -0.5, diff, stage(L.qcT), NTL)], L.neg_lam[:, :])


def odd_mix(g, A, L):
    M = Shared()
    M.sections = [(NTL // 2, 0, 0)]
    M.w_out = A["o_w_out"][0]
    M.x_rows = lambda t: g.x_dram[bass.ds(t * P + CTX, P), :]
    M.tiles, M.heads, M.rows = NTL, CH, L.cat[:, :, 0:CW]
    M.gain = L.gain["o_g_sub"].unsqueeze(1).unsqueeze(1).to_broadcast([P, NTL, CH, CV])
    M.gate = None
    M.room = L.room[:, :]
    M.scratch = L.room[:, 0:NTL * CW].rearrange("p (n d) -> p n d", d=CW)
    M.halves = (lambda t: L.cat[:, bass.ds(t, 1), 0:CW], lambda t: L.cat[:, bass.ds(t, 1), CW:])
    return M


def route(nc, g, A, layer, R, nt):
    tag = f"rt{layer}_"
    n, m = nt * NE, nt * NG

    def s(name):
        return nc.alloc_semaphore(tag + name)

    with nc.cleanup_on_exit():
        def sb(name, cols, dt=F32):
            return nc.alloc_sbuf_tensor(tag + name, [P, cols], dt)

        sel, one1, one2, key, tmp = (sb(x, n) for x in ("sel", "one1", "one2", "key", "tmp"))
        m1, m2, top, best = (sb(x, m) for x in ("m1", "m2", "top", "best"))
        down, number = sb("down", PER), sb("number", NE)
        gs = sb("gs", 4 * nt)
        blocks, ends, ones_e = sb("blocks", NE), sb("ends", NE), sb("ones_e", NE)
        blk_i = sb("blk_i", NE, I32)
        place, place_i, lo, hi = sb("place", 2 * nt), sb("place_i", 2 * nt, I32), sb("lo", 2 * nt, I32), sb("hi", 2 * nt, I32)
        lo_f, hi_f = sb("lo_f", 2 * nt), sb("hi_f", 2 * nt)
        slot_i = sb("slot_i", 2 * nt, I32)
        tok = sb("tok", nt, I32)
        zero = sb("zero", MAXB, I32)
        ps_a = nc.alloc_psum_tensor(tag + "ps_a", [P, 512], F32)
        ps_b = nc.alloc_psum_tensor(tag + "ps_b", [P, 512], F32)
        c = Count(nc, tag + "dve_step")
        consts, tok_ready, assigned, counted, placed, cleared, scattered, listed = (
            s("consts"), s("tok_ready"), s("assigned"), s("counted"), s("placed"), s("cleared"), s("scattered"), s("listed"))

        def ge(ap):
            return ap[:, 0:n].rearrange("p (a e) -> p a e", e=PER)

        def te(ap):
            return ap[:, 0:n].rearrange("p (t e) -> p t e", e=NE)

        with nc.Block() as block:

            @block.gpsimd
            def _(pool):
                pool.iota(down[:, :], pattern=[[-1, PER]], base=PER, channel_multiplier=0,
                          allow_small_or_imprecise_dtypes=True).then_inc(consts, 1)
                pool.iota(number[:, :], pattern=[[1, NE]], base=0, channel_multiplier=0,
                          allow_small_or_imprecise_dtypes=True).then_inc(consts, 1)
                pool.memset(zero[:, :], 0).then_inc(consts, 1)
                pool.iota(tok[:, :], pattern=[[P, nt]], base=0, channel_multiplier=1).then_inc(tok_ready, 1)
                pool.wait_ge(tok_ready, 1)
                pool.wait_ge(cleared, 16)
                pool.wait_ge(placed, 1)
                for k in range(2 * nt):
                    pool.indirect_dma_start(out=R.list_dram, out_offset=bass.IndirectOffsetOnAxis(slot_i[:, k:k + 1].bitcast(U32), 0),
                                            in_=tok[:, k // 2:k // 2 + 1], in_offset=None).then_inc(scattered, 16)

            @block.sync
            def _(sp):
                sp.wait_ge(consts, 3)
                sp.dma_start(R.list_dram.rearrange("(p b) o -> p (b o)", p=P), zero[:, :]).then_inc(cleared, 16)
                load_expert(sp, A, layer, R, 0, 0)
                sp.wait_ge(scattered, 16 * 2 * nt)
                sp.dma_start(R.list[:, :], R.list_dram.rearrange("(p b) o -> p (b o)", p=P)).then_inc(listed, 16)
                load_expert(sp, A, layer, R, 1, 1)
                sp.wait_ge(listed, 16)

            @block.tensor
            def _(pe):
                pe.wait_ge(assigned, 1)
                pe.matmul(ps_a[:, 0:n], g.consts[:, 2 * P:3 * P], tmp[:, 0:n], start=True, stop=True)
                pe.matmul(ps_b[:, 0:n], g.ones, tmp[:, 0:n], start=True, stop=True).then_inc(counted, 1)

            @block.vector
            def _(dve):
                def own():
                    dve.wait_ge(*c.now())

                dve.memset(ones_e[:, :], 1.0).then_inc(*c.up())
                dve.tensor_tensor(te(sel), R.scores[:, 0:nt, :], g.bc["b_router"].unsqueeze(1).to_broadcast([P, nt, NE]), ALU.add).then_inc(*c.up())
                dve.wait_ge(consts, 3)

                def first_of(src3, top2, one3, count, groups):
                    wide = [P, groups, count]
                    own()
                    dve.tensor_reduce(top2, src3, AX.X, ALU.max).then_inc(*c.up())
                    own()
                    dve.tensor_tensor(one3, src3, top2.unsqueeze(2).to_broadcast(wide), ALU.is_equal).then_inc(*c.up())
                    own()
                    key3 = key[:, 0:groups * count].rearrange("p (a e) -> p a e", e=count)
                    dve.tensor_tensor(key3, one3, down[:, PER - count:PER].unsqueeze(1).to_broadcast(wide), ALU.mult).then_inc(*c.up())
                    own()
                    dve.tensor_reduce(best[:, 0:groups], key3, AX.X, ALU.max).then_inc(*c.up())
                    own()
                    dve.tensor_tensor(one3, key3, best[:, 0:groups].unsqueeze(2).to_broadcast(wide), ALU.is_equal).then_inc(*c.up())

                first_of(ge(sel), m1[:, 0:m], ge(one1), PER, m)
                own()
                dve.scalar_tensor_tensor(out=tmp[:, 0:n], in0=one1[:, 0:n], scalar=-BIG, in1=sel[:, 0:n], op0=ALU.mult, op1=ALU.add).then_inc(*c.up())
                first_of(ge(tmp), m2[:, 0:m], ge(one2), PER, m)
                own()
                dve.tensor_tensor(m1[:, 0:m], m1[:, 0:m], m2[:, 0:m], ALU.add).then_inc(*c.up())
                first_of(m1[:, 0:m].rearrange("p (t g) -> p t g", g=NG), gs[:, 0:nt], m2[:, 0:m].rearrange("p (t g) -> p t g", g=NG), NG, nt)
                for one in (one1, one2):
                    own()
                    dve.tensor_tensor(ge(one), ge(one), m2[:, 0:m].unsqueeze(2).to_broadcast([P, m, PER]), ALU.mult).then_inc(*c.up())
                own()
                dve.tensor_tensor(tmp[:, 0:n], one1[:, 0:n], one2[:, 0:n], ALU.add).then_inc(assigned, 1)
                for k, one in enumerate((one1, one2)):
                    own()
                    dve.tensor_tensor(te(key), te(one), R.scores[:, 0:nt, :], ALU.mult).then_inc(*c.up())
                    own()
                    dve.tensor_reduce(gs[:, k * nt:(k + 1) * nt], te(key), AX.X, ALU.add).then_inc(*c.up())
                own()
                dve.tensor_tensor(gs[:, 2 * nt:3 * nt], gs[:, 0:nt], gs[:, nt:2 * nt], ALU.add).then_inc(*c.up())
                own()
                dve.reciprocal(gs[:, 3 * nt:4 * nt], gs[:, 2 * nt:3 * nt]).then_inc(*c.up())
                own()
                for k in range(2):
                    dve.tensor_tensor(R.gate[:, 0:nt, k], gs[:, k * nt:(k + 1) * nt], gs[:, 3 * nt:4 * nt], ALU.mult).then_inc(*c.up())
                dve.wait_ge(counted, 1)
                dve.tensor_tensor(key[:, 0:n], ps_a[:, 0:n], tmp[:, 0:n], ALU.subtract).then_inc(*c.up())
                dve.memset(sel[:, 0:NE], 0.0).then_inc(*c.up())
                for t in range(1, nt):
                    own()
                    dve.tensor_tensor(sel[:, t * NE:(t + 1) * NE], sel[:, (t - 1) * NE:t * NE], ps_b[:, (t - 1) * NE:t * NE], ALU.add).then_inc(*c.up())
                own()
                dve.tensor_tensor(blocks[:, :], sel[:, n - NE:n], ps_b[:, n - NE:n], ALU.add).then_inc(*c.up())
                own()
                dve.tensor_scalar(blk_i[:, :], blocks[:, :], float(P - 1), None, ALU.add).then_inc(*c.up())
                own()
                dve.tensor_scalar(blk_i[:, :], blk_i[:, :], 7, None, ALU.logical_shift_right).then_inc(*c.up())
                own()
                dve.tensor_scalar(blocks[:, :], blk_i[:, :], 1.0, None, ALU.max).then_inc(*c.up())
                own()
                dve.tensor_tensor_scan(ends[:, :], ones_e[:, :], blocks[:, :], 0.0, ALU.mult, ALU.add).then_inc(*c.up())
                own()
                dve.tensor_tensor(ends[:, :], ends[:, :], blocks[:, :], ALU.subtract).then_inc(*c.up())
                own()
                dve.tensor_tensor(number[:, :], ends[:, :], number[:, :], ALU.subtract).then_inc(*c.up())
                own()
                dve.scalar_tensor_tensor(out=number[:, :], in0=number[:, :], scalar=16.0, in1=blocks[:, :], op0=ALU.mult, op1=ALU.add).then_inc(*c.up())
                own()
                dve.tensor_scalar(number[:, :], number[:, :], -1.0, None, ALU.add).then_inc(*c.up())
                own()
                pairs = number[:, :].rearrange("p (n h) -> p n h", h=2)
                dve.scalar_tensor_tensor(out=R.table[:, :].unsqueeze(2), in0=pairs[:, :, 1:2], scalar=512.0, in1=pairs[:, :, 0:1],
                                         op0=ALU.mult, op1=ALU.add).then_inc(*c.up())
                dve.tensor_tensor(key[:, 0:n], key[:, 0:n], sel[:, 0:n], ALU.add).then_inc(*c.up())
                own()
                dve.scalar_tensor_tensor(out=te(key), in0=ends[:, :].unsqueeze(1).to_broadcast([P, nt, NE]), scalar=float(P), in1=te(key),
                                         op0=ALU.mult, op1=ALU.add).then_inc(*c.up())
                pl = place[:, :].rearrange("p (t k) -> p t k", k=2)
                for k, one in enumerate((one1, one2)):
                    own()
                    dve.tensor_tensor(te(one), te(one), te(key), ALU.mult).then_inc(*c.up())
                    own()
                    dve.tensor_reduce(pl[:, :, k], te(one), AX.X, ALU.add).then_inc(*c.up())
                own()
                dve.tensor_copy(R.dest[:, 0:2 * nt], place[:, :]).then_inc(*c.up())
                own()
                dve.tensor_scalar(lo[:, :], R.dest[:, 0:2 * nt], P - 1, None, ALU.bitwise_and).then_inc(*c.up())
                dve.tensor_scalar(hi[:, :], R.dest[:, 0:2 * nt], 7, None, ALU.logical_shift_right).then_inc(*c.up())
                own()
                dve.tensor_copy(lo_f[:, :], lo[:, :]).then_inc(*c.up())
                dve.tensor_copy(hi_f[:, :], hi[:, :]).then_inc(*c.up())
                own()
                dve.scalar_tensor_tensor(out=slot_i[:, :], in0=lo_f[:, :], scalar=float(MAXB), in1=hi_f[:, :], op0=ALU.mult, op1=ALU.add).then_inc(*c.up())
                own()
                dve.sem_inc(placed, 1)


def load_expert(sp, A, layer, R, e, h):
    for dst, name in ((R.w1, "w1"), (R.w3, "w3")):
        sp.dma_start(dst[:, h, :, :], A[name][layer, bass.ds(e, 1), :, :].rearrange("o (k p) n -> p (o k) n", p=P)).then_inc(R.w13_in[h], 16)
    sp.dma_start(R.w2[:, h, :, :], A["w2"][layer, bass.ds(e, 1), :, :].rearrange("o (k p) n -> p (o k) n", p=P)).then_inc(R.w2_in[h], 16)


def split_entry(nc, entry, h):
    one = entry // 512 if h else entry % 512
    return nc.s_assert_within(one // 16, 0, MAXB - NE, skip_runtime_bounds_check_because="MAXB blocks at most, one each for NE experts"), one % 16


def experts(nc, g, A, layer, R):
    tag = f"ex{layer}_"
    KE = DE // P

    def s(name):
        return nc.alloc_semaphore(tag + name)

    with nc.cleanup_on_exit():
        w1, w3, w2, w13_in, w2_in = R.w1, R.w3, R.w2, R.w13_in, R.w2_in
        idx = nc.alloc_sbuf_tensor(tag + "idx", [P, 3], I32)
        xg = nc.alloc_sbuf_tensor(tag + "xg", [P, 3, D], F32)
        xT = nc.alloc_sbuf_tensor(tag + "xT", [P, 3, KD, P], F32)
        th = nc.alloc_sbuf_tensor(tag + "th", [P, 2, P], F32)
        hT = nc.alloc_sbuf_tensor(tag + "hT", [P, 3, KE, P], F32)
        y = nc.alloc_sbuf_tensor(tag + "y", [P, 3, D], F32)
        ps_x = nc.alloc_psum_tensor(tag + "ps_x", [P, 2, 512], F32)
        ps_h = nc.alloc_psum_tensor(tag + "ps_h", [P, 4, 512], F32)
        ps_y = nc.alloc_psum_tensor(tag + "ps_y", [P, 2, 512], F32)
        w_used, written = s("w_used"), s("written")
        idx_done, idx_seen, gathered = s("idx_done"), s("idx_seen"), [s("gathered0"), s("gathered1"), s("gathered2")]
        t_done, x_act, x_dve, h_done, th_done, th_used, h_ready = (s("t_done"), s("x_act"), s("x_dve"), s("h_done"),
                                                                  s("th_done"), s("th_used"), s("h_ready"))
        y_done, y_act, y_dve, y_st = s("y_done"), s("y_act"), s("y_dve"), [s("y_st0"), s("y_st1"), s("y_st2")]

        def walk(eng, block_of, expert_end=None):
            with eng.Fori(0, NE // 2) as i:
                entry = eng.value_load(R.table[0:1, bass.ds(i, 1)], min_val=0, max_val=512 * 512 - 1)
                for h in range(2):
                    e = i * 2 + h
                    before, more = split_entry(nc, entry, h)
                    first = before + e
                    block_of(i, e, h, h, first, 2, i)
                    with eng.If(more > 0):
                        with eng.Fori(0, more) as b:
                            gb = nc.s_assert_within(first + b + 1, 1, MAXB - 1, skip_runtime_bounds_check_because="the experts have MAXB blocks at most")
                            block_of(i, e, h, 2, gb, 1, before + b)
                    if expert_end:
                        expert_end(i, e, h)

        with nc.Block() as block:

            @block.sync
            def _(sp):
                with sp.Fori(1, NE // 2) as i:
                    for h in range(2):
                        sp.wait_ge(w_used, i * 2 + h + 1)
                        load_expert(sp, A, layer, R, i * 2 + h, h)

            @block.gpsimd
            def _(pool):
                def block_of(i, e, h, b3, gb, lag, use):
                    pool.wait_ge(t_done, gb * 2 + (2 if lag == 2 else 4))
                    pool.tensor_copy(idx[:, b3:b3 + 1], R.list[:, bass.ds(gb, 1)]).then_inc(idx_done, 1)
                    pool.wait_ge(idx_done, gb + 1)
                    pool.sem_inc(idx_seen, 1)
                    pool.indirect_dma_start(out=xg[:, b3, :], out_offset=None, in_=R.f_dram,
                                            in_offset=bass.IndirectOffsetOnAxis(idx[:, b3:b3 + 1].bitcast(U32), 0)).then_inc(gathered[b3], 16)

                walk(pool, block_of)

            @block.tensor
            def _(pe):
                pe.sem_inc(t_done, 4)
                pe.sem_inc(w_used, 2)

                def block_of(i, e, h, b3, gb, lag, use):
                    pe.wait_ge(gathered[b3], use * 16 + 16)
                    pe.wait_ge(x_act, gb + 1)
                    pe.wait_ge(x_dve, gb + 1)
                    for half in range(2):
                        for k in range(4 * half, 4 * half + 4):
                            mm = pe.transpose(ps_x[:, half, (k % 4) * P:(k % 4) * P + P], xg[:, b3, k * P:(k + 1) * P], g.ident)
                        mm.then_inc(t_done, 1)
                    if b3 < 2:
                        pe.wait_ge(w13_in[h], i * 32 + 32)
                    pe.wait_ge(x_act, gb + 2)
                    for f in range(KE):
                        pe.wait_ge(h_ready, gb * 4 + f + 1)
                        for n, w in enumerate((w1, w3)):
                            for k in range(KD):
                                if f == 0 and n == 0 and k == 4:
                                    pe.wait_ge(x_dve, gb + 2)
                                mm = pe.matmul(ps_h[:, f, n * P:(n + 1) * P], w[:, h, k, f * P:(f + 1) * P], xT[:, b3, k, :],
                                               start=k == 0, stop=k == KD - 1)
                        mm.then_inc(h_done, 1)
                    if b3 < 2:
                        pe.wait_ge(w2_in[h], i * 16 + 16)
                    pe.wait_ge(y_act, gb + 1)
                    pe.wait_ge(y_dve, gb + 1)
                    for half in range(2):
                        for k in range(KE):
                            if half == 0:
                                pe.wait_ge(h_ready, gb * 4 + 5 + k)
                            mm = pe.matmul(ps_y[:, half, :], hT[:, b3, k, :], w2[:, h, k, half * 512:(half + 1) * 512],
                                           start=k == 0, stop=k == KE - 1)
                        mm.then_inc(y_done, 1)

                def expert_end(i, e, h):
                    pe.matmul(ps_h[:, 0, 0:P], g.ident, g.ident, start=True, stop=True).then_inc(w_used, 1)

                walk(pe, block_of, expert_end)

            @block.scalar
            def _(act):
                act.sem_inc(x_act, 1)
                act.sem_inc(y_act, 1)

                def block_of(i, e, h, b3, gb, lag, use):
                    act.wait_ge(t_done, gb * 2 + 5)
                    act.wait_ge(y_done, gb * 2 + (2 if lag == 2 else 4))
                    act.copy(xT[:, b3, 0:4, :], ps_x[:, 0, :].rearrange("p (k t) -> p k t", t=P)).then_inc(x_act, 1)
                    for f in range(KE):
                        act.wait_ge(h_done, gb * 4 + f + 1)
                        act.wait_ge(th_used, gb * 4 + f + 1)
                        act.activation(th[:, f % 2, :], ps_h[:, f, 0:P], ACT.Tanh, scale=0.5).then_inc(th_done, 1)
                    act.wait_ge(y_done, gb * 2 + 5)
                    act.wait_ge(y_st[b3], use * 16 + 16)
                    act.copy(y[:, b3, 0:512], ps_y[:, 0, :]).then_inc(y_act, 1)
                    act.wait_ge(y_act, gb + 2)
                    act.wait_ge(y_dve, gb + 2)
                    act.dma_start(R.y_dram[bass.ds(gb * P, P), :], y[:, b3, :]).then_inc(y_st[b3], 16)

                for b in range(3):
                    act.sem_inc(y_st[b], 16)
                walk(act, block_of)
                entry = act.value_load(R.table[0:1, NE // 2 - 1:NE // 2], min_val=0, max_val=512 * 512 - 1)
                before, more = split_entry(nc, entry, 1)
                for b in range(2):
                    act.wait_ge(y_st[b], 16 + 16 * (NE // 2))
                act.wait_ge(y_st[2], (before + more) * 16 + 16)
                act.sem_inc(written, 1)

            @block.vector
            def _(dve):
                dve.sem_inc(x_dve, 1)
                dve.sem_inc(y_dve, 1)
                dve.sem_inc(th_used, 2)
                dve.sem_inc(h_ready, 4)
                dve.sem_inc(y_done, 4)

                def block_of(i, e, h, b3, gb, lag, use):
                    dve.wait_ge(t_done, gb * 2 + 6)
                    dve.wait_ge(y_done, gb * 2 + (2 if lag == 2 else 4))
                    dve.tensor_copy(xT[:, b3, 4:8, :], ps_x[:, 1, :].rearrange("p (k t) -> p k t", t=P)).then_inc(x_dve, 1)
                    for f in range(KE):
                        dve.wait_ge(th_done, gb * 4 + f + 1)
                        dve.scalar_tensor_tensor(out=hT[:, b3, f, :], in0=th[:, f % 2, :], scalar=1.0, in1=ps_h[:, f, 0:P],
                                                 op0=ALU.add, op1=ALU.mult).then_inc(th_used, 1)
                        dve.wait_ge(th_used, gb * 4 + f + 3)
                        dve.scalar_tensor_tensor(out=hT[:, b3, f, :], in0=hT[:, b3, f, :], scalar=0.5, in1=ps_h[:, f, P:2 * P],
                                                 op0=ALU.mult, op1=ALU.mult).then_inc(h_ready, 1)
                    dve.wait_ge(y_done, gb * 2 + 6)
                    dve.wait_ge(y_st[b3], use * 16 + 16)
                    dve.tensor_copy(y[:, b3, 512:1024], ps_y[:, 1, :]).then_inc(y_dve, 1)

                walk(dve, block_of)


def combine(nc, g, A, layer, M, R):
    tag = f"cb{layer}_"

    def s(name):
        return nc.alloc_semaphore(tag + name)

    with nc.cleanup_on_exit():
        kinds = sorted({sec[2] for sec in M.sections})
        rows = nc.alloc_sbuf_tensor(tag + "rows", [P, len(kinds), D], F32)
        x = nc.alloc_sbuf_tensor(tag + "x", [P, 4, D], F32)
        y = nc.alloc_sbuf_tensor(tag + "y", [P, 4, 2, D], F32)
        ps = nc.alloc_psum_tensor(tag + "ps", [P, 2, D], F32)
        row_mm, row_out, x_new = s("row_mm"), s("row_out"), s("x_new")
        x_in, x_st, y_in = ([s(f"{n}{b}") for b in range(4)] for n in ("x_in", "x_st", "y_in"))
        c = Count(nc, tag + "dve_step")
        pairs = []
        for count, tile0, kind in M.sections:
            pairs += [(tile0 + 2 * j, kind) for j in range(count)]

        with nc.Block() as block:

            @block.sync
            def _(sp):
                for n, (tile, kind) in enumerate(pairs):
                    for h in range(2):
                        b, use = 2 * (n % 2) + h, n // 2
                        if use:
                            sp.wait_ge(x_st[b], 16 * use)
                        sp.dma_start(x[:, b, :], M.x_rows(tile + h)).then_inc(x_in[b], 16)

            @block.gpsimd
            def _(pool):
                for n, (tile, kind) in enumerate(pairs):
                    for h in range(2):
                        b = 2 * (n % 2) + h
                        if n > 1:
                            pool.wait_ge(x_new, 2 * (n - 2) + h + 1)
                        for k in range(2):
                            pool.indirect_dma_start(out=y[:, b, k, :], out_offset=None, in_=R.y_dram,
                                                    in_offset=bass.IndirectOffsetOnAxis(R.dest[:, 2 * (tile + h) + k:2 * (tile + h) + k + 1].bitcast(U32), 0)).then_inc(y_in[b], 16)

            @block.tensor
            def _(pe):
                for n, kind in enumerate(kinds):
                    broadcast_rows(pe, g, ps[:, n, :], g.mod[:, layer * 48 + V_G2 * KD:layer * 48 + V_G2 * KD + KD, kind], row_mm)

            @block.scalar
            def _(act):
                for n, (tile, kind) in enumerate(pairs):
                    for h in range(2):
                        b = 2 * (n % 2) + h
                        act.wait_ge(x_new, 2 * n + h + 1)
                        act.dma_start(R.final(tile + h), x[:, b, :]).then_inc(x_st[b], 16)
                for b in range(4):
                    act.wait_ge(x_st[b], 16 * len(pairs[b // 2::2]))

            @block.vector
            def _(dve):
                def own():
                    dve.wait_ge(*c.now())

                for n in range(len(kinds)):
                    dve.wait_ge(row_mm, n + 1)
                    dve.tensor_copy(rows[:, n, :], ps[:, n, :]).then_inc(row_out, 1)
                dve.wait_ge(row_out, len(kinds))
                for n, (tile, kind) in enumerate(pairs):
                    for h in range(2):
                        b, use = 2 * (n % 2) + h, n // 2
                        y0, y1 = y[:, b, 0, :], y[:, b, 1, :]
                        dve.wait_ge(y_in[b], 32 * (use + 1))
                        dve.tensor_scalar(y0, y0, R.gate[:, tile + h, 0:1], None, ALU.mult).then_inc(*c.up())
                        own()
                        dve.scalar_tensor_tensor(out=y0, in0=y1, scalar=R.gate[:, tile + h, 1:2], in1=y0, op0=ALU.mult, op1=ALU.add).then_inc(*c.up())
                        own()
                        dve.tensor_tensor(y0, y0, rows[:, kinds.index(kind), :], ALU.mult).then_inc(*c.up())
                        own()
                        dve.wait_ge(x_in[b], 16 * (use + 1))
                        dve.tensor_tensor(x[:, b, :], x[:, b, :], y0, ALU.add).then_inc(x_new, 1)


def ffn(nc, g, A, layer, M, R, nt, upto):
    with nc.cleanup_on_exit():
        R.list = nc.alloc_sbuf_tensor(f"list{layer}", [P, MAXB], I32)
        R.table = nc.alloc_sbuf_tensor(f"table{layer}", [P, NE // 2], I32)
        R.dest = nc.alloc_sbuf_tensor(f"dest{layer}", [P, 2 * NT], I32)
        R.gate = nc.alloc_sbuf_tensor(f"gate{layer}", [P, NT, 2], F32)
        R.w1 = nc.alloc_sbuf_tensor(f"w1_{layer}", [P, 2, KD, DE], F32)
        R.w3 = nc.alloc_sbuf_tensor(f"w3_{layer}", [P, 2, KD, DE], F32)
        R.w2 = nc.alloc_sbuf_tensor(f"w2_{layer}", [P, 2, DE // P, D], F32)
        R.w13_in, R.w2_in = ([nc.alloc_semaphore(f"{n}_in{h}_{layer}") for h in range(2)] for n in ("w13", "w2"))
        route(nc, g, A, layer, R, nt)
        if upto == 5:
            return
        experts(nc, g, A, layer, R)
        if upto == 6:
            return
        combine(nc, g, A, layer, M, R)


def build(nc, A, out, upto=99, only=None):
    g = Shared()
    g.x_dram = nc.dram_tensor("x_stream", (T, D), F32, kind="Internal").ap()
    g.consts = nc.alloc_sbuf_tensor("consts_sb", [P, NCONST], F32)
    g.ident = g.consts[:, 0:P]
    g.ones = g.consts[:, P:2 * P]
    g.cols = nc.alloc_sbuf_tensor("cols", [P, COLS_B], F32)
    g.mod = nc.alloc_sbuf_tensor("mod", [P, 96, 2], F32)
    g.gain = nc.alloc_sbuf_tensor("gain", [P, 2, 2, KD, 2], F32)
    g.rope = nc.alloc_sbuf_tensor("rope_sb", [P, NT, 96], F32)
    g.gbc = nc.alloc_sbuf_tensor("gbc", [P, GB_N], F32)
    g.broadcasts = [(n, g.gbc[:, GB[n][0]:GB[n][0] + GB[n][1]]) for n in GB]
    g.bc = {n: g.gbc[:, GB[n][0]:GB[n][0] + GB[n][1]] for n in GB}
    g.vo_dram = nc.dram_tensor("vo_dram", (T, 2 * BW), F32, kind="Internal").ap()
    R = Shared()
    R.f_dram = nc.dram_tensor("f_dram", (T, D), F32, kind="Internal").ap()
    R.list_dram = nc.dram_tensor("list_dram", (P * MAXB, 1), I32, kind="Internal").ap()
    g.y_dram = R.y_dram = nc.dram_tensor("y_dram", (P * MAXB, D), F32, kind="Internal").ap()
    R.final = lambda t: g.x_dram[t * P:(t + 1) * P, :]
    R.scores = nc.alloc_sbuf_tensor("scores", [P, NT, NE], F32)
    with nc.cleanup_on_exit():
        L = Shared()
        L.qT = nc.alloc_sbuf_tensor("qT", [P, 4, T], F32)
        L.kT = nc.alloc_sbuf_tensor("kT", [P, T], F32)
        L.v = nc.alloc_sbuf_tensor("v", [P, NT, AKW], F32)
        L.gates = nc.alloc_sbuf_tensor("gates", [P, NT, 4 * BH], F32)
        L.zT = nc.alloc_sbuf_tensor("zT", [P, 8, T], F32)
        with nc.cleanup_on_exit():
            L.w = nc.alloc_sbuf_tensor("w", [P, KD, IN_EVEN], F32)
            L.w_in = nc.alloc_semaphore("e_w_in_loaded")
            modulation(nc, g, A, L)
            even_project(nc, g, A, L)
        if upto == 1:
            return
        L.hb = nc.alloc_sbuf_tensor("hb", [P, NT, BW], F32)
        if only is None or 2 in only:
            even_mlstm(nc, g, A, L)
        if upto == 2:
            return
        L.cat = L.zT[:, 0:4, :].rearrange("p a t -> p (a t)").rearrange("p (n d) -> p n d", d=AW)
        even_attend(nc, g, A, L)
        if upto == 3:
            return
        M = even_mix(g, A, L)
        mix_out(nc, g, A, 0, M, R)
        if upto == 4:
            return
    ffn(nc, g, A, 0, M, R, NT, upto)
    if upto in (5, 6, 7):
        return
    with nc.cleanup_on_exit():
        L = Shared()
        L.go = nc.alloc_sbuf_tensor("go", [P, GO_N], F32)
        L.gain = {n: L.go[:, GO[n][0]:GO[n][0] + GO[n][1]] for n in GO}
        L.neg_lam = nc.alloc_sbuf_tensor("neg_lam", [P, 1], F32)
        cat = nc.alloc_sbuf_tensor("cat1", [P, NTL * D], F32)
        L.cat = cat[:, :].rearrange("p (t d) -> p t d", d=D)
        ZL = IN_ODD - 3 * CW
        L.zl = cat[:, 0:NT * ZL].rearrange("p (t n) -> p t n", n=ZL)
        L.spare = cat[:, NT * ZL:NTL * D]
        with nc.cleanup_on_exit():
            L.qcT = nc.alloc_sbuf_tensor("qcT", [P, CH, T], F32)
            L.kcT = nc.alloc_sbuf_tensor("kcT", [P, CH, T], F32)
            L.vc = nc.alloc_sbuf_tensor("vc", [P, NT, CW], F32)
            odd_project(nc, g, A, L)
            if upto == 11:
                return
            L.qdT = nc.alloc_sbuf_tensor("qdT", [P, DH, T], F32)
            L.kdT = nc.alloc_sbuf_tensor("kdT", [P, DH, T], F32)
            L.vd = nc.alloc_sbuf_tensor("vd", [P, NT, DH * DV], F32)
            odd_latent(nc, g, A, L)
            if upto == 12:
                return
            odd_attend(nc, g, A, L)
            if upto == 13:
                return
        L.room = nc.alloc_sbuf_tensor("room", [P, 5 * D], F32)
        M = odd_mix(g, A, L)
        mix_out(nc, g, A, 1, M, R)
        if upto == 14:
            return
    R.final = lambda t: out[0, t * P:(t + 1) * P, :]
    ffn(nc, g, A, 1, M, R, NTL, upto)


def places(vectors):
    at, out = 0, {}
    for name, width in vectors:
        out[name] = (at, width)
        at += width
    return out, at


GB, GB_N = places((("e_g_q", AD), ("e_g_k", AD), ("e_g_h", BW), ("e_b_gates", 4 * BH), ("b_router", NE)))
GO, GO_N = places((("o_g_qc", CD), ("o_g_kc", CD), ("o_g_sub", CV), ("o_g_cq", DQL), ("o_g_ckv", DKL), ("o_g_qd", DK),
                   ("o_g_kd", DK), ("o_lam", 4 * CD)))

NCONST = 6 * P


def constants():
    s, j = np.indices((P, P))
    upper = (s <= j).astype(np.float32)
    lower = (s >= j).astype(np.float32)
    consts = np.concatenate([np.eye(P, dtype=np.float32), np.ones((P, P), np.float32), upper, lower,
                             (upper - 1) * np.float32(BIG), (lower - 1) * np.float32(BIG)], axis=1)
    rope = []
    for rot in (AD, DR):
        n = rot // 4
        inv = np.float32(10000.0) ** (-np.arange(n, dtype=np.float32) / np.float32(n))
        pos = np.arange(SEQ)
        ang = np.concatenate([(pos // GRID_W)[:, None] * inv, (pos % GRID_W)[:, None] * inv], axis=1).astype(np.float32)
        cos = np.concatenate([np.ones((CTX, 2 * n), np.float32), np.cos(ang)])
        sin = np.concatenate([np.zeros((CTX, 2 * n), np.float32), np.sin(ang)])
        rope += [cos, sin]
    return consts, np.concatenate(rope, axis=1).astype(np.float32)


_INS = ["x", "c", "ctx", "c_ctx", "w_ada", "b_ada", "g_mix", "g_ffn", "e_w_in", "e_w_out", "e_g_q", "e_g_k", "e_conv_w",
        "e_conv_b", "e_b_gates", "e_g_h", "o_w_in", "o_w_out", "o_g_qc", "o_g_kc", "o_lam", "o_g_sub", "o_g_cq", "o_w_uq",
        "o_g_ckv", "o_w_ukv", "o_g_qd", "o_g_kd", "w_router", "b_router", "w1", "w3", "w2"]


def kernel(**inputs):
    import concourse.bacc as _bacc
    from concourse.bass_utils import run_bass_kernel_spmd as _run

    nc = _bacc.Bacc("TRN2", target_bir_lowering=False, num_devices=1)
    consts, rope = constants()
    arrays, args = {}, {}
    for name in _INS + ["consts", "rope"]:
        a = {"consts": consts, "rope": rope}.get(name)
        a = np.ascontiguousarray(inputs[name]) if a is None else a
        arrays[f"in_{name}"] = a
        args[name] = nc.dram_tensor(f"in_{name}", a.shape, mybir.dt.from_np(a.dtype), kind="ExternalInput").ap()
    out = nc.dram_tensor("out_0", (1, SEQ, D), F32, kind="ExternalOutput").ap()
    build(nc, args, out)
    r = _run(nc, [arrays], core_ids=[0])
    return r.results[0]["out_0"]
```
